# Optimizing a Trainium2 kernel written in Bass

```python
import jax
import jax.numpy as jnp
from jax import lax
import numpy as np
import jax, jax.numpy as jnp

D_MODEL = 1024
BATCH = 1
SEQ = 256
DEPTH = 2

CTX_LEN = 256
GRID_W = 64
HEAD_DIM = 64
ROPE_THETA = 10000.0
QBLK = 128
EPS = 1e-6

A_HEADS = (D_MODEL // 2) // HEAD_DIM
A_KV_HEADS = A_HEADS // 4
A_WIDTH = A_HEADS * HEAD_DIM
B_WIDTH = D_MODEL - A_WIDTH
CONV_WIDTH = 31
AB_IN = A_WIDTH + 2 * A_KV_HEADS * HEAD_DIM + 2 * B_WIDTH

C_HEADS = (D_MODEL // 2) // HEAD_DIM
C_KV_HEADS = C_HEADS // 4
C_WIDTH = C_HEADS * HEAD_DIM
WINDOW = 128
D_WIDTH = D_MODEL - C_WIDTH
POOL_SIZES = (2, 4, 8, 16)
POOL_GROUP_WIDTH = D_WIDTH // len(POOL_SIZES)
CD_IN = C_WIDTH + 2 * C_KV_HEADS * HEAD_DIM + D_WIDTH

N_EXPERT_GROUPS = 4
EXPERTS_PER_GROUP = 8
N_EXPERTS = N_EXPERT_GROUPS * EXPERTS_PER_GROUP
TOP_K_INNER = 2
D_EXPERT = D_MODEL // 2
MOE_BLOCK = 128


def _rmsnorm(x, g):
    xf = x.astype(jnp.float32)
    y = xf * lax.rsqrt(jnp.mean(xf * xf, axis=-1, keepdims=True) + EPS)
    return (y * g.astype(jnp.float32)).astype(x.dtype)

def _modulate(h, shift, scale):
    return h * (1 + scale) + shift

def _rope_tables(n_lat):
    rows = n_lat // GRID_W
    row = jnp.repeat(jnp.arange(rows, dtype=jnp.float32), GRID_W)
    col = jnp.tile(jnp.arange(GRID_W, dtype=jnp.float32), rows)
    n_freq = HEAD_DIM // 4
    inv = ROPE_THETA ** (-jnp.arange(n_freq, dtype=jnp.float32) / n_freq)
    ang = jnp.concatenate([row[:, None] * inv, col[:, None] * inv], axis=-1)
    return jnp.cos(ang), jnp.sin(ang)

def _rope(x, cos, sin):
    half = HEAD_DIM // 2
    x1, x2 = x[..., :half], x[..., half:]
    c = cos.astype(x.dtype)
    s = sin.astype(x.dtype)
    return jnp.concatenate([x1 * c - x2 * s, x2 * c + x1 * s], axis=-1)

def _heads(t, n):
    b, s, _ = t.shape
    return t.reshape(b, s, n, HEAD_DIM).transpose(0, 2, 1, 3)

def _group(q, n_kv):
    b, h, s, d = q.shape
    return q.reshape(b, n_kv, h // n_kv, s, d)

def _merge(o):
    b, k, g, s, d = o.shape
    return o.transpose(0, 3, 1, 2, 4).reshape(b, s, k * g * d)

def _attend(q, k, v, mask, sink):
    s = jnp.einsum('bkgqd,bksd->bkgqs', q, k).astype(jnp.float32) * (HEAD_DIM ** -0.5)
    if mask is not None:
        s = jnp.where(mask, s, -jnp.inf)
    if sink is None:
        p = jax.nn.softmax(s, axis=-1)
    else:
        sk = jnp.broadcast_to(sink.astype(jnp.float32)[None, :, :, None, None], s.shape[:-1] + (1,))
        p = jax.nn.softmax(jnp.concatenate([s, sk], axis=-1), axis=-1)[..., :-1]
    return jnp.einsum('bkgqs,bksd->bkgqd', p.astype(v.dtype), v)

def _dense_attn_blocks(q, k, v):
    b, hk, g, s, d = q.shape
    nb = s // QBLK
    qb = jnp.moveaxis(q.reshape(b, hk, g, nb, QBLK, d), 3, 0)
    ob = lax.map(lambda qi: _attend(qi, k, v, None, None), qb)
    return jnp.moveaxis(ob, 0, 3).reshape(b, hk, g, s, d)

def _window_attn_blocks(q, k_lat, v_lat, k_ctx, v_ctx, sink):
    b, hk, g, s, d = q.shape
    nb = s // QBLK
    span = QBLK + 2 * WINDOW
    n_ctx = k_ctx.shape[2]
    pad = ((0, 0), (0, 0), (WINDOW, WINDOW), (0, 0))
    kp = jnp.pad(k_lat, pad)
    vp = jnp.pad(v_lat, pad)
    qb = jnp.moveaxis(q.reshape(b, hk, g, nb, QBLK, d), 3, 0)
    r = jnp.arange(QBLK)
    j = jnp.arange(span)
    ctx_mask = jnp.ones((QBLK, n_ctx), dtype=bool)

    def block(args):
        qi, i = args
        start = i * QBLK
        kw = lax.dynamic_slice_in_dim(kp, start, span, axis=2)
        vw = lax.dynamic_slice_in_dim(vp, start, span, axis=2)
        qpos = start + r
        kpos = start - WINDOW + j
        band = (jnp.abs(qpos[:, None] - kpos[None, :]) <= WINDOW) & ((kpos >= 0) & (kpos < s))[None, :]
        mask = jnp.concatenate([ctx_mask, band], axis=1)
        return _attend(qi, jnp.concatenate([k_ctx, kw], axis=2), jnp.concatenate([v_ctx, vw], axis=2), mask, sink)

    ob = lax.map(block, (qb, jnp.arange(nb)))
    return jnp.moveaxis(ob, 0, 3).reshape(b, hk, g, s, d)

def _conv_module(u, conv_w, conv_b, ln_g, ln_b):
    a, gate = jnp.split(u, 2, axis=-1)
    glu = a * jax.nn.sigmoid(gate)
    y = lax.conv_general_dilated(glu, conv_w[:, None, :], window_strides=(1,),
                                 padding=[(CONV_WIDTH // 2, CONV_WIDTH // 2)],
                                 dimension_numbers=('NWC', 'WIO', 'NWC'),
                                 feature_group_count=B_WIDTH) + conv_b
    yf = y.astype(jnp.float32)
    mu = jnp.mean(yf, axis=-1, keepdims=True)
    var = jnp.mean((yf - mu) ** 2, axis=-1, keepdims=True)
    yn = ((yf - mu) * lax.rsqrt(var + EPS) * ln_g.astype(jnp.float32) + ln_b.astype(jnp.float32)).astype(u.dtype)
    return jax.nn.silu(yn)

def _pool_mixer(u, pool_w, pool_scale):
    b, s, _ = u.shape
    uf = u.astype(jnp.float32)
    cs = jnp.pad(jnp.cumsum(uf, axis=1), ((0, 0), (1, 0), (0, 0)))
    t = jnp.arange(s)
    outs = []
    for gi, w in enumerate(POOL_SIZES):
        lo_c, hi_c = gi * POOL_GROUP_WIDTH, (gi + 1) * POOL_GROUP_WIDTH
        lo = jnp.clip(t - w // 2, 0, s)
        hi = jnp.clip(t - w // 2 + w, 0, s)
        csg = cs[..., lo_c:hi_c]
        mean = (jnp.take(csg, hi, axis=1) - jnp.take(csg, lo, axis=1)) / (hi - lo).astype(jnp.float32)[None, :, None]
        outs.append(mean - uf[..., lo_c:hi_c])
    p = jnp.stack(outs, axis=2).astype(u.dtype)
    y = jnp.einsum('bsgc,gcd->bsgd', p, pool_w).reshape(b, s, D_WIDTH)
    return y * pool_scale

def _mixer_ab(hx, hc, w_in, w_out, q_g, k_g, conv_w, conv_b, ln_g, ln_b, cos, sin, ctx_out):
    kvw = A_KV_HEADS * HEAD_DIM
    o_k, o_v, o_u = A_WIDTH, A_WIDTH + kvw, A_WIDTH + 2 * kvw
    px = hx @ w_in
    qx = _rope(_rmsnorm(_heads(px[..., :o_k], A_HEADS), q_g), cos, sin)
    kx = _rope(_rmsnorm(_heads(px[..., o_k:o_v], A_KV_HEADS), k_g), cos, sin)
    vx = _heads(px[..., o_v:o_u], A_KV_HEADS)
    if ctx_out:
        pc = hc @ w_in
        kvc = pc[..., o_k:o_u]
    else:
        kvc = hc @ w_in[:, o_k:o_u]
    kc = _rmsnorm(_heads(kvc[..., :kvw], A_KV_HEADS), k_g)
    vc = _heads(kvc[..., kvw:], A_KV_HEADS)
    ox = _dense_attn_blocks(_group(qx, A_KV_HEADS), jnp.concatenate([kc, kx], axis=2), jnp.concatenate([vc, vx], axis=2))
    bx = _conv_module(px[..., o_u:], conv_w, conv_b, ln_g, ln_b)
    yx = jnp.concatenate([_merge(ox), bx], axis=-1) @ w_out
    if not ctx_out:
        return yx, None
    qc = _rmsnorm(_heads(pc[..., :o_k], A_HEADS), q_g)
    oc = _attend(_group(qc, A_KV_HEADS), kc, vc, None, None)
    bc = _conv_module(pc[..., o_u:], conv_w, conv_b, ln_g, ln_b)
    yc = jnp.concatenate([_merge(oc), bc], axis=-1) @ w_out
    return yx, yc

def _mixer_cd(hx, hc, w_in, w_out, q_g, k_g, sink, pool_w, pool_scale, cos, sin, ctx_out):
    kvw = C_KV_HEADS * HEAD_DIM
    o_k, o_v, o_u = C_WIDTH, C_WIDTH + kvw, C_WIDTH + 2 * kvw
    sink_g = sink.reshape(C_KV_HEADS, C_HEADS // C_KV_HEADS)
    px = hx @ w_in
    qx = _rope(_rmsnorm(_heads(px[..., :o_k], C_HEADS), q_g), cos, sin)
    kx = _rope(_rmsnorm(_heads(px[..., o_k:o_v], C_KV_HEADS), k_g), cos, sin)
    vx = _heads(px[..., o_v:o_u], C_KV_HEADS)
    if ctx_out:
        pc = hc @ w_in
        kvc = pc[..., o_k:o_u]
    else:
        kvc = hc @ w_in[:, o_k:o_u]
    kc = _rmsnorm(_heads(kvc[..., :kvw], C_KV_HEADS), k_g)
    vc = _heads(kvc[..., kvw:], C_KV_HEADS)
    ox = _window_attn_blocks(_group(qx, C_KV_HEADS), kx, vx, kc, vc, sink_g)
    dx = _pool_mixer(px[..., o_u:], pool_w, pool_scale)
    yx = jnp.concatenate([_merge(ox), dx], axis=-1) @ w_out
    if not ctx_out:
        return yx, None
    qc = _rmsnorm(_heads(pc[..., :o_k], C_HEADS), q_g)
    oc = _attend(_group(qc, C_KV_HEADS), kc, vc, None, sink_g)
    dc = _pool_mixer(pc[..., o_u:], pool_w, pool_scale)
    yc = jnp.concatenate([_merge(oc), dc], axis=-1) @ w_out
    return yx, yc

def _moe(h, grp_w, grp_b, exp_w, exp_b, w_gate, w_up, w_down):
    n_tok, d = h.shape
    tok_idx = jnp.arange(n_tok)
    g_logits = (h @ grp_w).astype(jnp.float32) + grp_b.astype(jnp.float32)
    g_sel = jnp.argmax(g_logits, axis=-1)
    g_w = jax.nn.softmax(g_logits, axis=-1)[tok_idx, g_sel]
    e_logits = ((h @ exp_w).astype(jnp.float32) + exp_b.astype(jnp.float32)).reshape(n_tok, N_EXPERT_GROUPS, EXPERTS_PER_GROUP)[tok_idx, g_sel]
    e_p, e_i = lax.top_k(jax.nn.softmax(e_logits, axis=-1), TOP_K_INNER)
    wts = (g_w[:, None] * e_p / jnp.sum(e_p, axis=-1, keepdims=True)).reshape(-1)
    eid = (g_sel[:, None] * EXPERTS_PER_GROUP + e_i).reshape(-1).astype(jnp.int32)
    n_asg = n_tok * TOP_K_INNER
    flat_tok = jnp.repeat(tok_idx, TOP_K_INNER).astype(jnp.int32)
    order = jnp.argsort(eid)
    se, stok, sw = eid[order], flat_tok[order], wts[order]
    counts = jnp.bincount(eid, length=N_EXPERTS).astype(jnp.int32)
    padded = (counts + MOE_BLOCK - 1) // MOE_BLOCK * MOE_BLOCK
    start = jnp.cumsum(counts) - counts
    pend = jnp.cumsum(padded)
    dest = (pend - padded)[se] + jnp.arange(n_asg, dtype=jnp.int32) - start[se]
    n_blk = -(-(n_asg + N_EXPERTS * (MOE_BLOCK - 1)) // MOE_BLOCK)
    cap = n_blk * MOE_BLOCK
    buf_tok = jnp.full((cap,), n_tok, jnp.int32).at[dest].set(stok)
    buf_w = jnp.zeros((cap,), h.dtype).at[dest].set(sw.astype(h.dtype))
    blk_e = jnp.minimum(jnp.searchsorted(pend, jnp.arange(n_blk, dtype=jnp.int32) * MOE_BLOCK, side='right'), N_EXPERTS - 1)
    h_pad = jnp.concatenate([h, jnp.zeros((1, d), h.dtype)], axis=0)

    def run(args):
        tok, wt, e = args
        xb = h_pad[tok]
        hid = jax.nn.silu(xb @ w_gate[e]) * (xb @ w_up[e])
        return (hid @ w_down[e]) * wt[:, None]

    ys = lax.map(run, (buf_tok.reshape(n_blk, MOE_BLOCK), buf_w.reshape(n_blk, MOE_BLOCK), blk_e))
    out = jnp.zeros((n_tok + 1, d), h.dtype).at[buf_tok].add(ys.reshape(cap, d))
    return out[:n_tok]

def first_inputs(seed: int = 0) -> dict:
    key = jax.random.key(seed)
    keys = jax.random.split(key, 48)
    counter = iter(range(48))

    def nrm(shape, scale):
        return jax.random.normal(keys[next(counter)], shape, jnp.float32) * scale

    n_even = (DEPTH + 1) // 2
    n_odd = DEPTH // 2
    dm = D_MODEL
    return {
        'x': nrm((BATCH, SEQ, dm), 1.0),
        'c': nrm((BATCH, dm), 1.0),
        'ctx': nrm((BATCH, CTX_LEN, dm), 1.0),
        'c_ctx': nrm((dm,), 1.0),
        'mod_w': nrm((DEPTH, dm, 6 * dm), 0.5 * dm ** -0.5),
        'mod_b': nrm((DEPTH, 6 * dm), 0.02),
        'ln1_g': 1.0 + nrm((DEPTH, dm), 0.02),
        'ln2_g': 1.0 + nrm((DEPTH, dm), 0.02),
        'w_in_ab': nrm((n_even, dm, AB_IN), dm ** -0.5),
        'w_out_ab': nrm((n_even, A_WIDTH + B_WIDTH, dm), dm ** -0.5),
        'q_norm_a': 1.0 + nrm((n_even, HEAD_DIM), 0.02),
        'k_norm_a': 1.0 + nrm((n_even, HEAD_DIM), 0.02),
        'conv_w': nrm((n_even, CONV_WIDTH, B_WIDTH), CONV_WIDTH ** -0.5),
        'conv_b': nrm((n_even, B_WIDTH), 0.02),
        'conv_ln_g': 1.0 + nrm((n_even, B_WIDTH), 0.02),
        'conv_ln_b': nrm((n_even, B_WIDTH), 0.02),
        'w_in_cd': nrm((n_odd, dm, CD_IN), dm ** -0.5),
        'w_out_cd': nrm((n_odd, C_WIDTH + D_WIDTH, dm), dm ** -0.5),
        'q_norm_c': 1.0 + nrm((n_odd, HEAD_DIM), 0.02),
        'k_norm_c': 1.0 + nrm((n_odd, HEAD_DIM), 0.02),
        'sink_c': nrm((n_odd, C_HEADS), 0.5),
        'pool_w': nrm((n_odd, len(POOL_SIZES), POOL_GROUP_WIDTH, POOL_GROUP_WIDTH), POOL_GROUP_WIDTH ** -0.5),
        'pool_scale': 1.0 + nrm((n_odd, D_WIDTH), 0.02),
        'rt_grp_w': nrm((DEPTH, dm, N_EXPERT_GROUPS), dm ** -0.5),
        'rt_grp_b': nrm((DEPTH, N_EXPERT_GROUPS), 0.01),
        'rt_exp_w': nrm((DEPTH, dm, N_EXPERTS), dm ** -0.5),
        'rt_exp_b': nrm((DEPTH, N_EXPERTS), 0.01),
        'ex_gate': nrm((DEPTH, N_EXPERTS, dm, D_EXPERT), dm ** -0.5),
        'ex_up': nrm((DEPTH, N_EXPERTS, dm, D_EXPERT), dm ** -0.5),
        'ex_down': nrm((DEPTH, N_EXPERTS, D_EXPERT, dm), D_EXPERT ** -0.5),
    }

def first_block(x, c, ctx, c_ctx, mod_w, mod_b, ln1_g, ln2_g,
              w_in_ab, w_out_ab, q_norm_a, k_norm_a, conv_w, conv_b, conv_ln_g, conv_ln_b,
              w_in_cd, w_out_cd, q_norm_c, k_norm_c, sink_c, pool_w, pool_scale,
              rt_grp_w, rt_grp_b, rt_exp_w, rt_exp_b, ex_gate, ex_up, ex_down):
    b, s, dm = x.shape
    cos, sin = _rope_tables(s)
    for i in range(DEPTH):
        last = i == DEPTH - 1
        li = i // 2
        mod = jax.nn.silu(c) @ mod_w[i] + mod_b[i]
        modc = jax.nn.silu(c_ctx) @ mod_w[i] + mod_b[i]
        sh1, sc1, g1, sh2, sc2, g2 = jnp.split(mod[:, None, :], 6, axis=-1)
        sh1c, sc1c, g1c, sh2c, sc2c, g2c = jnp.split(modc[None, None, :], 6, axis=-1)
        hx = _modulate(_rmsnorm(x, ln1_g[i]), sh1, sc1)
        hc = _modulate(_rmsnorm(ctx, ln1_g[i]), sh1c, sc1c)
        if i % 2 == 0:
            yx, yc = _mixer_ab(hx, hc, w_in_ab[li], w_out_ab[li], q_norm_a[li], k_norm_a[li],
                               conv_w[li], conv_b[li], conv_ln_g[li], conv_ln_b[li], cos, sin, not last)
        else:
            yx, yc = _mixer_cd(hx, hc, w_in_cd[li], w_out_cd[li], q_norm_c[li], k_norm_c[li],
                               sink_c[li], pool_w[li], pool_scale[li], cos, sin, not last)
        x = x + g1 * yx
        hx = _modulate(_rmsnorm(x, ln2_g[i]), sh2, sc2)
        if last:
            ox = _moe(hx.reshape(b * s, dm), rt_grp_w[i], rt_grp_b[i], rt_exp_w[i], rt_exp_b[i],
                      ex_gate[i], ex_up[i], ex_down[i]).reshape(b, s, dm)
            x = x + g2 * ox
        else:
            ctx = ctx + g1c * yc
            hc = _modulate(_rmsnorm(ctx, ln2_g[i]), sh2c, sc2c)
            n_ctx = ctx.shape[1]
            tokens = jnp.concatenate([hc, hx], axis=1).reshape(-1, dm)
            out = _moe(tokens, rt_grp_w[i], rt_grp_b[i], rt_exp_w[i], rt_exp_b[i],
                       ex_gate[i], ex_up[i], ex_down[i]).reshape(b, n_ctx + s, dm)
            ctx = ctx + g2c * out[:, :n_ctx]
            x = x + g2 * out[:, n_ctx:]
    return x


NSA_HEADS = 8
NSA_KV_GROUPS = 1
NSA_HPG = NSA_HEADS // NSA_KV_GROUPS
SB_HEADS = 4
SB_HEAD_DIM = 128
ROPE_THETA_2 = 500000.0
ROT_DIM = HEAD_DIM // 4
CMP_BLOCK = 32
CMP_STRIDE = 16
CMP_HIDDEN = 256
SEL_BLOCK = 64
SEL_TOP_N = 8
WINDOW_2 = 512
Q_BLOCK = 128
D_FF = 4 * D_MODEL
RMS_EPS = 1e-6
NSA_W = NSA_HEADS * HEAD_DIM
KV_W = NSA_KV_GROUPS * HEAD_DIM
SB_W = SB_HEADS * SB_HEAD_DIM
IN_W = NSA_W + 6 * KV_W + 3 * NSA_HEADS + 3 * SB_W + 2 * D_MODEL


def rms_norm(x, g):
    xf = x.astype(jnp.float32)
    y = xf * lax.rsqrt(jnp.mean(xf * xf, axis=-1, keepdims=True) + RMS_EPS)
    return (y * g.astype(jnp.float32)).astype(x.dtype)

def to_heads(t, n, dh):
    b, s = t.shape[:2]
    return t.reshape(b, s, n, dh).transpose(0, 2, 1, 3)

def partial_rope(x, positions):
    half = ROT_DIM // 2
    inv_freq = jnp.power(ROPE_THETA_2, jnp.arange(half, dtype=jnp.float32) * (-2.0 / ROT_DIM))
    ang = positions.astype(jnp.float32)[:, None, :, None] * inv_freq
    cos, sin = jnp.cos(ang), jnp.sin(ang)
    xf = x.astype(jnp.float32)
    x1, x2, rest = xf[..., :half], xf[..., half:ROT_DIM], xf[..., ROT_DIM:]
    out = jnp.concatenate([x1 * cos - x2 * sin, x2 * cos + x1 * sin, rest], axis=-1)
    return out.astype(x.dtype)

def compress_blocks(kv, pe, w1, w2):
    s = kv.shape[2]
    nc = (s - CMP_BLOCK) // CMP_STRIDE + 1
    idx = CMP_STRIDE * jnp.arange(nc)[:, None] + jnp.arange(CMP_BLOCK)[None, :]
    blocks = kv[:, :, idx] + pe
    flat = blocks.reshape(blocks.shape[:3] + (CMP_BLOCK * HEAD_DIM,))
    return jax.nn.gelu(flat @ w1) @ w2

def nsa_attention(q_rope, q_plain, k_cmp, v_cmp, k_slc, v_slc, k_win, v_win, gates):
    out_dtype = q_rope.dtype
    f32 = jnp.float32
    scale = HEAD_DIM ** -0.5
    q_rope, q_plain, gates = q_rope.astype(f32) * scale, q_plain.astype(f32) * scale, gates.astype(f32)
    k_cmp, v_cmp = k_cmp.astype(f32), v_cmp.astype(f32)
    b, g, h, s, dh = q_rope.shape
    nb = s // Q_BLOCK
    nc = k_cmp.shape[2]
    ns = s // SEL_BLOCK
    n_sel = min(SEL_TOP_N, ns)
    cmp_last = CMP_STRIDE * jnp.arange(nc) + CMP_BLOCK - 1
    c_start = CMP_STRIDE * jnp.arange(nc)[:, None]
    s_start = SEL_BLOCK * jnp.arange(ns)[None, :]
    overlap = ((c_start < s_start + SEL_BLOCK) & (c_start + CMP_BLOCK > s_start)).astype(f32)
    ks_blocks = k_slc.astype(f32).reshape(b, g, ns, SEL_BLOCK, dh)
    vs_blocks = v_slc.astype(f32).reshape(b, g, ns, SEL_BLOCK, dh)
    pad = ((0, 0), (0, 0), (WINDOW_2, 0), (0, 0))
    kw_pad = jnp.pad(k_win.astype(f32), pad)
    vw_pad = jnp.pad(v_win.astype(f32), pad)
    b_ix = jnp.arange(b)[:, None, None, None]
    g_ix = jnp.arange(g)[None, :, None, None]
    blk = jnp.arange(ns)

    def block(i):
        q0 = i * Q_BLOCK
        t = q0 + jnp.arange(Q_BLOCK)
        qr = lax.dynamic_slice_in_dim(q_rope, q0, Q_BLOCK, axis=3)
        qp = lax.dynamic_slice_in_dim(q_plain, q0, Q_BLOCK, axis=3)
        gt = lax.dynamic_slice_in_dim(gates, q0, Q_BLOCK, axis=3)
        vis_c = cmp_last[None, :] <= t[:, None]
        s_c = jnp.einsum('bghqd,bgcd->bghqc', qp, k_cmp)
        p_c = jax.nn.softmax(jnp.where(vis_c, s_c, -1e30), axis=-1) * vis_c.astype(f32)
        o_c = jnp.einsum('bghqc,bgcd->bghqd', p_c, v_cmp)
        imp = jnp.einsum('bghqc,cn->bgqn', p_c, overlap)
        cur = t // SEL_BLOCK
        valid = blk[None, :] <= cur[:, None]
        forced = (blk[None, :] == 0) | (blk[None, :] == cur[:, None]) | (blk[None, :] == cur[:, None] - 1)
        score = jnp.where(valid, jnp.where(forced, jnp.inf, imp), -1.0)
        _, sel = lax.top_k(score, n_sel)
        k_g = ks_blocks[b_ix, g_ix, sel].reshape(b, g, Q_BLOCK, n_sel * SEL_BLOCK, dh)
        v_g = vs_blocks[b_ix, g_ix, sel].reshape(b, g, Q_BLOCK, n_sel * SEL_BLOCK, dh)
        pos = sel[..., None] * SEL_BLOCK + jnp.arange(SEL_BLOCK)
        vis_s = (pos <= t[:, None, None]).reshape(b, g, Q_BLOCK, n_sel * SEL_BLOCK)
        s_s = jnp.einsum('bghqd,bgqkd->bghqk', qr, k_g)
        p_s = jax.nn.softmax(jnp.where(vis_s[:, :, None], s_s, -1e30), axis=-1)
        o_s = jnp.einsum('bghqk,bgqkd->bghqd', p_s, v_g)
        kw = lax.dynamic_slice_in_dim(kw_pad, q0, Q_BLOCK + WINDOW_2, axis=2)
        vw = lax.dynamic_slice_in_dim(vw_pad, q0, Q_BLOCK + WINDOW_2, axis=2)
        kpos = q0 - WINDOW_2 + jnp.arange(Q_BLOCK + WINDOW_2)
        vis_w = (kpos[None, :] <= t[:, None]) & (kpos[None, :] > t[:, None] - WINDOW_2) & (kpos[None, :] >= 0)
        s_w = jnp.einsum('bghqd,bgkd->bghqk', qr, kw)
        p_w = jax.nn.softmax(jnp.where(vis_w, s_w, -1e30), axis=-1)
        o_w = jnp.einsum('bghqk,bgkd->bghqd', p_w, vw)
        return gt[..., 0:1] * o_c + gt[..., 1:2] * o_s + gt[..., 2:3] * o_w

    out = lax.map(block, jnp.arange(nb))
    out = out.transpose(1, 0, 4, 2, 3, 5).reshape(b, s, g * h * dh)
    return out.astype(out_dtype)

def stick_breaking_attention(q, k, v):
    out_dtype = q.dtype
    f32 = jnp.float32
    b, hh, s, dh = q.shape
    qf = q.astype(f32) * (SB_HEAD_DIM ** -0.5)
    kf, vf = k.astype(f32), v.astype(f32)
    nb = s // Q_BLOCK
    r = jnp.arange(Q_BLOCK)
    tri = (r[:, None] >= r[None, :]).astype(f32)
    diag_mask = r[None, :] < r[:, None]
    outs = []
    for i in range(nb):
        q0 = i * Q_BLOCK
        qb = qf[:, :, q0:q0 + Q_BLOCK]
        z_d = jnp.einsum('bhqd,bhkd->bhqk', qb, kf[:, :, q0:q0 + Q_BLOCK])
        l_d = jnp.where(diag_mask, jax.nn.log_sigmoid(-z_d), 0.0)
        c_d = l_d @ tri
        a_d = jnp.where(diag_mask, jnp.exp(z_d + c_d), 0.0)
        o = jnp.einsum('bhqk,bhkd->bhqd', a_d, vf[:, :, q0:q0 + Q_BLOCK])
        if i > 0:
            z_o = jnp.einsum('bhqd,bhkd->bhqk', qb, kf[:, :, :q0]).reshape(b, hh, Q_BLOCK, i, Q_BLOCK)
            c_o = jax.nn.log_sigmoid(-z_o) @ tri
            ci = jnp.arange(i)
            upper = (ci[:, None] > ci[None, :]).astype(f32)
            off = c_o[..., 0] @ upper + c_d[..., 0:1]
            a_o = jnp.exp(z_o + c_o + off[..., None])
            o = o + jnp.einsum('bhqck,bhckd->bhqd', a_o, vf[:, :, :q0].reshape(b, hh, i, Q_BLOCK, dh))
        outs.append(o)
    out = jnp.concatenate(outs, axis=2)
    return out.transpose(0, 2, 1, 3).reshape(b, s, hh * dh).astype(out_dtype)

def split_columns(proj):
    sizes = [NSA_W, KV_W, KV_W, KV_W, KV_W, KV_W, KV_W, 3 * NSA_HEADS, SB_W, SB_W, SB_W, 2 * D_MODEL]
    parts, start = [], 0
    for n in sizes:
        parts.append(proj[..., start:start + n])
        start += n
    return parts

def hybrid_layer(x, positions, norm_g, w_in, cmp_pe, cmp_w1, cmp_w2, w_nsa_o, w_sb_o, w_out, w_ff1, w_ff2):
    b, s, _ = x.shape
    hn = rms_norm(x, norm_g[0])
    (nsa_q, k_c, v_c, k_s, v_s, k_w, v_w, nsa_g, sb_q, sb_k, sb_v, merge_g) = split_columns(hn @ w_in)
    grp = (b, NSA_KV_GROUPS, NSA_HPG, s, HEAD_DIM)
    q_plain = to_heads(nsa_q, NSA_HEADS, HEAD_DIM)
    q_rope = partial_rope(q_plain, positions).reshape(grp)
    q_plain = q_plain.reshape(grp)
    kc = compress_blocks(to_heads(k_c, NSA_KV_GROUPS, HEAD_DIM), cmp_pe[0], cmp_w1[0], cmp_w2[0])
    vc = compress_blocks(to_heads(v_c, NSA_KV_GROUPS, HEAD_DIM), cmp_pe[1], cmp_w1[1], cmp_w2[1])
    ks = partial_rope(to_heads(k_s, NSA_KV_GROUPS, HEAD_DIM), positions)
    kw = partial_rope(to_heads(k_w, NSA_KV_GROUPS, HEAD_DIM), positions)
    gates = jax.nn.sigmoid(nsa_g).reshape(b, s, NSA_HEADS, 3).transpose(0, 2, 1, 3).reshape(grp[:4] + (3,))
    y_nsa = nsa_attention(q_rope, q_plain, kc, vc, ks, to_heads(v_s, NSA_KV_GROUPS, HEAD_DIM),
                          kw, to_heads(v_w, NSA_KV_GROUPS, HEAD_DIM), gates) @ w_nsa_o
    y_sb = stick_breaking_attention(to_heads(sb_q, SB_HEADS, SB_HEAD_DIM), to_heads(sb_k, SB_HEADS, SB_HEAD_DIM),
                                    to_heads(sb_v, SB_HEADS, SB_HEAD_DIM)) @ w_sb_o
    gate = jax.nn.sigmoid(merge_g)
    mixed = (gate[..., :D_MODEL] * y_nsa + gate[..., D_MODEL:] * y_sb) @ w_out
    x = x + rms_norm(mixed, norm_g[1])
    hf = rms_norm(x, norm_g[2])
    ff = jnp.square(jax.nn.relu(hf @ w_ff1)) @ w_ff2
    return x + rms_norm(ff, norm_g[3])

def second_inputs(seed: int = 0) -> dict:
    key = jax.random.key(seed)
    ks = jax.random.split(key, 12)
    f32 = jnp.float32

    def nrm(k, shape, fan_in):
        return jax.random.normal(k, shape, f32) * (fan_in ** -0.5)

    x = jax.random.normal(ks[0], (BATCH, SEQ, D_MODEL), f32)
    positions = jnp.broadcast_to(jnp.arange(SEQ, dtype=jnp.int32)[None, :], (BATCH, SEQ))
    norm_g = 1.0 + 0.05 * jax.random.normal(ks[1], (DEPTH, 4, D_MODEL), f32)
    w_in = nrm(ks[2], (DEPTH, D_MODEL, IN_W), D_MODEL)
    cmp_pe = 0.5 * jax.random.normal(ks[3], (DEPTH, 2, CMP_BLOCK, HEAD_DIM), f32)
    cmp_w1 = nrm(ks[4], (DEPTH, 2, CMP_BLOCK * HEAD_DIM, CMP_HIDDEN), CMP_BLOCK * HEAD_DIM)
    cmp_w2 = nrm(ks[5], (DEPTH, 2, CMP_HIDDEN, HEAD_DIM), CMP_HIDDEN)
    w_nsa_o = nrm(ks[6], (DEPTH, NSA_W, D_MODEL), NSA_W)
    w_sb_o = nrm(ks[7], (DEPTH, SB_W, D_MODEL), SB_W)
    w_out = nrm(ks[8], (DEPTH, D_MODEL, D_MODEL), D_MODEL)
    w_ff1 = nrm(ks[9], (DEPTH, D_MODEL, D_FF), D_MODEL)
    w_ff2 = nrm(ks[10], (DEPTH, D_FF, D_MODEL), D_FF)
    return {'x': x, 'positions': positions, 'norm_g': norm_g, 'w_in': w_in, 'cmp_pe': cmp_pe,
            'cmp_w1': cmp_w1, 'cmp_w2': cmp_w2, 'w_nsa_o': w_nsa_o, 'w_sb_o': w_sb_o,
            'w_out': w_out, 'w_ff1': w_ff1, 'w_ff2': w_ff2}

def second_block(x, positions, norm_g, w_in, cmp_pe, cmp_w1, cmp_w2, w_nsa_o, w_sb_o, w_out, w_ff1, w_ff2):
    for layer in range(DEPTH):
        x = hybrid_layer(x, positions, norm_g[layer], w_in[layer], cmp_pe[layer], cmp_w1[layer],
                         cmp_w2[layer], w_nsa_o[layer], w_sb_o[layer], w_out[layer],
                         w_ff1[layer], w_ff2[layer])
    return x


def setup_inputs(seed=0):
    out = dict(first_inputs(seed))
    for name, value in second_inputs(seed + 1).items():
        if name != "x":
            out[name + "_2"] = value
    return out


def reference(
    x, c, ctx, c_ctx, mod_w, mod_b, ln1_g, ln2_g, w_in_ab, w_out_ab, q_norm_a, k_norm_a, conv_w,
    conv_b, conv_ln_g, conv_ln_b, w_in_cd, w_out_cd, q_norm_c, k_norm_c, sink_c, pool_w,
    pool_scale, rt_grp_w, rt_grp_b, rt_exp_w, rt_exp_b, ex_gate, ex_up, ex_down, positions_2,
    norm_g_2, w_in_2, cmp_pe_2, cmp_w1_2, cmp_w2_2, w_nsa_o_2, w_sb_o_2, w_out_2, w_ff1_2,
    w_ff2_2,
):
    x = first_block(
        x, c, ctx, c_ctx, mod_w, mod_b, ln1_g, ln2_g, w_in_ab, w_out_ab, q_norm_a, k_norm_a,
        conv_w, conv_b, conv_ln_g, conv_ln_b, w_in_cd, w_out_cd, q_norm_c, k_norm_c, sink_c,
        pool_w, pool_scale, rt_grp_w, rt_grp_b, rt_exp_w, rt_exp_b, ex_gate, ex_up, ex_down,
    )
    return second_block(
        x, positions_2, norm_g_2, w_in_2, cmp_pe_2, cmp_w1_2, cmp_w2_2, w_nsa_o_2, w_sb_o_2,
        w_out_2, w_ff1_2, w_ff2_2,
    )


_drawn_inputs = setup_inputs


def setup_inputs(seed=0):
    import zlib

    import numpy as np

    out = dict(_drawn_inputs(seed))
    spreads = {}
    factors = {'ln1_g': 5.877,
     'q_norm_a': 8.0,
     'k_norm_a': 8.0,
     'conv_b': 13.86,
     'conv_ln_g': 18.039,
     'conv_ln_b': 18.31,
     'q_norm_c': 28.703,
     'k_norm_c': 26.235,
     'sink_c': 8.0,
     'pool_scale': 20.15,
     'rt_grp_b': 33.964,
     'rt_exp_b': 25.531,
     'ln2_g': 4.93,
     'norm_g_2': 2.929,
     'cmp_pe_2': 4.852}
    for name, (base, spread) in spreads.items():
        noise = np.random.default_rng([zlib.crc32(name.encode()), seed]).standard_normal(out[name].shape)
        drawn = base * np.exp(spread * noise) if base else spread * noise
        out[name] = jnp.asarray(drawn.astype(out[name].dtype))
    for name, factor in factors.items():
        out[name] = (out[name] * factor).astype(out[name].dtype)
    return out
```

```python
from contextlib import ExitStack

import concourse.bass as bass
from concourse import mybir

F32 = mybir.dt.float32
I32 = mybir.dt.int32
U32 = mybir.dt.uint32
ALU = mybir.AluOpType
ACT = mybir.ActivationFunctionType
AX_X = mybir.AxisListType.X

P = 128
D = 1024
KC = D // P
NX = 256
TG = 2
QT = NX // P
EPS = 1e-6
NEG = -1e30

HEADS = 8
DH = 64
SC_A = DH ** -0.5
QC = HEADS * DH // P
QKC = QC + 1
TAPS = 31
HALO = TAPS // 2
BC = 4
POOLS = (2, 4, 8, 16)
PPAD = 8
NG, NE, DE = 4, 32, 512
EC = DE // P
RL = NG + NE
SLOTS = 64
PAIR = 2 * SLOTS
MAXB = 48

CB, CS = 32, 16
NCMP = (NX - CB) // CS + 1
CPAD = 32
SBH, SBD = 4, 128
SC_B = SBD ** -0.5
FF = 4 * D
IN_W = 512 + 6 * 64 + 24 + 3 * 512 + 2 * D
COL_SB = 512 + 6 * 64 + 24
COL_MG = COL_SB + 3 * 512
TWO_PI = 6.283185307179586
C1 = 6.28125
C2 = 0.0019350051879882812
C3 = TWO_PI - C1 - C2
LINKS2 = 90
MAGIC = 12582912.0

PARAMS = [("cond", 2 * KC), ("mod_b", 2 * 48), ("ln1_g", 2 * KC), ("ln2_g", 2 * KC), ("qn_a", 1), ("kn_a", 1),
          ("conv_w", BC * TAPS), ("conv_b", BC), ("cln_g", BC), ("cln_b", BC), ("qn_c", 1), ("kn_c", 1),
          ("sink", HEADS), ("pool_scale", BC), ("rt_w", 2 * KC * RL), ("rt_b", 2 * RL)]
CONSTS = [("ident", P), ("headones", P), ("rot_a", P), ("swap", P), ("rot_b", P), ("dup0", P), ("dup1", P),
          ("tri_strict", P), ("negtri", P), ("trineg", P), ("band1", P), ("m01", P), ("iota", P),
          ("cos", NX), ("sin", NX), ("maskc", QT * NCMP), ("visc", QT * NCMP), ("invf", 1), ("eps", 1)]
LPARAMS = [("norm_g", 4 * KC), ("pe", 2 * (CB // 2)), ("w2", 2 * 2 * 64)]


def offsets(layout):
    out, at = {}, 0
    for name, n in layout:
        out[name] = (at, n)
        at += n
    return out, at


RING = 6
SLAB = 4096


def hybrid_program(nc, xT_in, params_in, consts_in, invcnt_in, lparams_in, pos_in, mod_w, w_in_ab, w_out_ab, w_in_cd,
                   w_out_cd, pool_w, ex_gate, ex_up, ex_down, w_in_2, cmp_w1, w_nsa_o, w_sb_o, w_out_2, w_ff1, w_ff2,
                   outT, y_rows):
    po, n_par = offsets(PARAMS)
    co, n_con = offsets(CONSTS)
    lo, n_lp = offsets(LPARAMS)
    ctx = ExitStack()
    with ctx:
        def sb(name, shape, dt=F32):
            return ctx.enter_context(nc.sbuf_tensor(name, shape, dt))

        def sem(name):
            return ctx.enter_context(nc.semaphore(name))

        ring = sb("ring", [P, RING, SLAB])
        xT = sb("xT", [P, TG, KC, NX])
        hT = sb("hT", [P, TG, KC, NX])
        cat = sb("cat", [P, 8, 512])
        sqb = sb("sqb", [P, 4, 512])
        E = sb("E", [P, 9216])
        par = sb("par", [P, n_par])
        con = sb("con", [P, n_con])
        lpar = sb("lpar", [P, n_lp])
        ones = sb("ones", [P, P])
        negones = sb("negones", [P, P])
        mneg = sb("mneg", [P, P])
        stdv = sb("stdv", [P, 512])
        modv = sb("modv", [P, 48, 2])
        scale1 = sb("scale1", [P, KC, 2])
        scale2 = sb("scale2", [P, KC, 2])
        condv = sb("condv", [P, KC, 2])
        mx = sb("mx", [P, 2, 2])
        nb = sb("nb", [P, 2, 2])
        sm = sb("sm", [P, 2, 2])
        es = sb("es", [P, 2, 1])
        ps = ctx.enter_context(nc.psum_tensor("ps", [P, 8, 512], F32))

        def pc(name, a=0, n=None):
            at, w = po[name]
            return par[:, at + a:at + (w if n is None else a + n)]

        def cc(name):
            at, w = co[name]
            return con[:, at:at + w]

        def lp(name, a, n):
            at, w = lo[name]
            return lpar[:, at + a:at + a + n]

        ident = cc("ident")

        def e3(at, a, b):
            return E[:, at:at + a * b].rearrange("p (a b) -> p a b", a=a)

        qk = e3(0, QKC, 512)
        kswap = E[:, 2560:3072]
        vtok = e3(3072, 4, P)
        GP = NX + 2 * HALO
        gpad = E[:, 3584:3584 + BC * TG * GP].rearrange("p (c g t) -> p c g t", c=BC, g=TG)
        UP = NX + 2 * PPAD
        upad = e3(3584, BC, UP)
        pwin = e3(3584 + BC * UP, 2, UP)
        pt_pool = e3(3584 + (BC + 2) * UP, BC, NX)
        invcnt = cat[:, 4:8, NX:512]
        prob = e3(7168, 2, 512)
        probT = E[:, 8192:9216].rearrange("p (u b q) -> p u b q", u=2, b=4)
        NTM = 4
        htok = cat[:, :, :].rearrange("p c t -> p (c t)").rearrange("p (n d) -> p n d", n=NTM)
        sel = E[:, 0:2 * NTM * PAIR].rearrange("p (u n s) -> p u n s", u=2, n=NTM)
        xg = E[:, 1024:2048].rearrange("p (u k s) -> p u k s", u=2, k=KC)
        silu_g = e3(2048, 2, EC * SLOTS)
        hid = E[:, 2560:3072].rearrange("p (u m s) -> p u m s", u=2, m=EC)
        yb = E[0:SLOTS, 3072:3072 + 2 * D].rearrange("p (u d) -> p u d", u=2)
        blk_cmp = E[0:1, 1024:1024 + MAXB * NE].rearrange("p (b e) -> p b e", b=MAXB)
        zrows = E[:, 5120:5120 + D]
        yg = E[:, 0:8192].rearrange("p (n k d) -> p n k d", n=NTM, k=2)
        lg = E[:, 8192:8336].rearrange("p (n r) -> p n r", n=NTM)
        lgp = e3(8336, NTM, 8)
        gm8 = e3(8368, NTM, 8)
        em8 = e3(8400, NTM, 8)
        pen = e3(8432, NTM, NG)
        rsc = e3(8448, 12, NTM)
        cum = e3(8496, 4, NE)
        M1 = e3(8624, 3, NTM * NE)
        gi8 = sb("gi8", [P, NTM, 8], U32)
        ei8 = sb("ei8", [P, NTM, 8], U32)
        slotf = sb("slotf", [P, NTM, 2])
        sloti = sb("sloti", [P, NTM * 2], I32)
        wts = sb("wts", [P, NTM, 2])
        blkf = sb("blkf", [1, MAXB + 2])
        blki = sb("blki", [1, MAXB + 2], I32)
        qp = xT[:, 1, 0:4, :]
        qr = xT[:, 1, 4:8, :]
        sbq = hT[:, 1, 0:4, :]
        sbk = hT[:, 1, 4:8, :]
        kv = e3(0, 3, NX)
        kdup = e3(768, 2, NX)
        vsw = e3(1280, QT, P)
        win = E[:, 1536:1536 + 512].rearrange("p (v j c) -> p v j c", v=2, j=CB // 2)
        sbv = e3(2048, QT, 512)
        mg = e3(3072, 16, NX)
        ffh = E[:, 0:8192].rearrange("p (c t) -> p c t", c=32)
        onsa = cat[:, 0:2, :].rearrange("p a (b t) -> p (a b) t", b=2)
        osb = cat[:, 2:4, :].rearrange("p a (b t) -> p (a b) t", b=2)
        mixT = cat[:, 4:8, :].rearrange("p a (b t) -> p (a b) t", b=2)
        trig = sb("trig", [P, 2, NX])
        cos2, sin2 = trig[:, 0, :], trig[:, 1, :]
        gates = sb("gates", [P, QT, 24])
        hcmp = sb("hcmp", [P, 4, 16])
        gcmp = sb("gcmp", [P, 4, NCMP])
        kcmp = sb("kcmp", [P, NCMP])
        vblk = sb("vblk", [P, 4, 64])
        pcp = sb("pcp", [P, QT, HEADS, CPAD])
        scmp = sqb[:, 2, 0:QT * HEADS * NCMP].rearrange("p (q h c) -> p q h c", q=QT, h=HEADS)
        pcT = sqb[:, 1, :].rearrange("p (b q) -> p b q", b=4)
        zs = E[:, 7168:7168 + SBH * 384].rearrange("p (h c) -> p h c", h=SBH)
        spl = cat[:, 4:7, :].rearrange("p a b -> p (a b)").rearrange("p (h c) -> p h c", h=SBH)
        yres = cat[:, 0:4, :].rearrange("p a (b t) -> p (a b) t", b=2)
        cst = sb("cst", [P, 3, QT * HEADS])

        inputs_in = sem("inputs_in")
        slab_in = [sem(f"slab_in{r}") for r in range(RING)]
        setup_done = sem("setup_done")
        cond_ready = sem("cond_ready")
        mod_mm = sem("mod_mm")
        mod_ready = sem("mod_ready")
        sq_ready = sem("sq_ready")
        ssq_mm = sem("ssq_mm")
        std_ready = sem("std_ready")
        rstd_ready = sem("rstd_ready")
        xn_ready = sem("xn_ready")
        h_ready = sem("h_ready")
        proj_mm = sem("proj_mm")
        proj_ev = sem("proj_ev")
        qsq_ready = sem("qsq_ready")
        qss_mm = sem("qss_mm")
        qstd_ready = sem("qstd_ready")
        qn_ready = sem("qn_ready")
        rot_mm = sem("rot_mm")
        rope_ready = sem("rope_ready")
        swap_mm = sem("swap_mm")
        swap_ev = sem("swap_ev")
        sc_mm = sem("sc_mm")
        nb_ready = sem("nb_ready")
        ex_ready = sem("ex_ready")
        pn_ready = sem("pn_ready")
        tr_mm = sem("tr_mm")
        pt_ready = sem("pt_ready")
        pv_mm = sem("pv_mm")
        o_ready = sem("o_ready")
        sink_ready = sem("sink_ready")
        glu_ready = sem("glu_ready")
        conv_ready = sem("conv_ready")
        cmu_mm = sem("cmu_mm")
        cd_ready = sem("cd_ready")
        csq_ready = sem("csq_ready")
        cvar_mm = sem("cvar_mm")
        cstd_ready = sem("cstd_ready")
        cn_ready = sem("cn_ready")
        bx_ready = sem("bx_ready")
        pool_ready = sem("pool_ready")
        pool_mm = sem("pool_mm")
        px_ready = sem("px_ready")
        invcnt_ready = sem("invcnt_ready")
        out_mm = sem("out_mm")
        x_ready = sem("x_ready")
        dchain = sem("dve_chain")
        achain = sem("act_chain")
        rt_mm = sem("rt_mm")
        ht_mm = sem("ht_mm")
        ht_ev = sem("ht_ev")
        gmax_ready = sem("gmax_ready")
        gexp_ready = sem("gexp_ready")
        m_ready = sem("m_ready")
        pos_mm = sem("pos_mm")
        plan_ready = sem("plan_ready")
        moe = []
        for l in range(2):
            moe.append({n: sem(f"{n}_{l}") for n in (
                "sel_ready", "xg_mm", "xg_ready", "gu_mm", "sg_ready", "hid_ready", "y_mm", "y_ready", "y_stored",
                "moe_chain")})
            moe[l]["w_in"] = [sem(f"w_in{r}_{l}") for r in range(RING)]
        stored_all = sem("stored_all")
        yg_in = [[sem(f"yg_in{l}{n}") for n in range(NTM if l == 0 else QT)] for l in range(2)]
        zrows_ready = sem("zrows_ready")
        tail_stored = sem("tail_stored")
        sel_over = sem("sel_over")
        mix_ready = sem("mix_ready")
        yt_mm = sem("yt_mm")
        x2_ready = sem("x2_ready")
        trig_done = sem("trig_done")
        trig_ready = sem("trig_ready")
        lpar_in = sem("lpar_in")
        p2_mm = sem("p2_mm")
        p2_ev = sem("p2_ev")
        r2_mm = sem("r2_mm")
        r2_ready = sem("r2_ready")
        cmp_mm = sem("cmp_mm")
        cmp_ready = sem("cmp_ready")
        gel_ready = sem("gel_ready")
        cev_ready = sem("cev_ready")
        pct_mm = sem("pct_mm")
        pct_ready = sem("pct_ready")
        cs_mm = sem("cs_mm")
        pcn_ready = sem("pcn_ready")
        pce_ready = sem("pce_ready")
        sbz_mm = sem("sbz_mm")
        sb_act = sem("sb_act")
        sb_dve = sem("sb_dve")
        sbc_mm = sem("sbc_mm")
        sbo_mm = sem("sbo_mm")
        y2_mm = sem("y2_mm")
        mix2_ready = sem("mix2_ready")
        wo_mm = sem("wo_mm")
        wo_ev = sem("wo_ev")
        nsq_ready = sem("nsq_ready")
        nss_mm = sem("nss_mm")
        nstd_ready = sem("nstd_ready")
        xo_ready = sem("xo_ready")
        d2chain = sem("d2_chain")
        f1_mm = sem("f1_mm")
        f1_ev = sem("f1_ev")
        ffh_ready = sem("ffh_ready")
        out_stored = sem("out_stored")
        spnop = sem("spnop")

        block = ctx.enter_context(nc.Block())
        n_in = 4

        def rows(w, c0, n):
            return w[:, c0:c0 + n].rearrange("(k p) n -> p k n", p=P)

        mod_slabs = [[(rows(mod_w[l], s * 512, 512), (KC, 512), (mod_mm, 12 * l + s + 1)) for s in range(12)]
                     for l in range(2)]
        ab_slabs = [(rows(w_in_ab, 0, 512), (KC, 512), (proj_mm, 4)), (rows(w_in_ab, 512, 512), (KC, 512), (proj_mm, 8)),
                    (rows(w_in_ab, 1024, 512), (KC, 512), (proj_mm, 12)), (rows(w_in_ab, 1536, 256), (KC, 256), (proj_mm, 14)),
                    (rows(w_out_ab, 0, 512), (KC, 512), (out_mm, 4)), (rows(w_out_ab, 512, 512), (KC, 512), (out_mm, 8))]
        cd_slabs = [(rows(w_in_cd, 0, 512), (KC, 512), (proj_mm, 18)), (rows(w_in_cd, 512, 512), (KC, 512), (proj_mm, 22)),
                    (rows(w_in_cd, 1024, 256), (KC, 256), (proj_mm, 24)),
                    (pool_w.rearrange("g c d -> c g d"), (BC, P), (pool_mm, 1)),
                    (rows(w_out_cd, 0, 512), (KC, 512), (out_mm, 12)), (rows(w_out_cd, 512, 512), (KC, 512), (out_mm, 16))]
        stream_a = mod_slabs[0] + ab_slabs
        stream_b = mod_slabs[1] + cd_slabs
        NA, NB_ = len(stream_a), len(stream_b)
        assert NA % RING == 0 and NB_ % RING == 0
        N2 = 36
        USED2 = 31

        def slab(n, shape):
            k, w = shape
            return ring[:, n % RING, 0:k * w].rearrange("p (k w) -> p k w", k=k)

        def slab2_uses(s):
            return (USED2 - s + RING - 1) // RING

        def slab2_count(i, j):
            s = j % RING
            return i * (16 * slab2_uses(s)) + 16 * ((NA + NB_) // RING + j // RING + 1)

        J_IN, J_CMP, J_NSA, J_SB, J_OUT, J_F1, J_F2 = 0, 9, 11, 12, 13, 15, 23
        P2N, WON = 34, 16

        def layer_slabs(i):
            win_ = w_in_2[bass.ds(i, 1), :, :].rearrange("a (k p) n -> p (a k) n", p=P)
            wc = cmp_w1[bass.ds(i, 1), :, :, :].rearrange("a v (j p) n -> p (a v) j n", p=P)
            wn = w_nsa_o[bass.ds(i, 1), :, :].rearrange("a (k p) n -> p (a k) n", p=P)
            ws = w_sb_o[bass.ds(i, 1), :, :].rearrange("a (k p) n -> p (a k) n", p=P)
            wo = w_out_2[bass.ds(i, 1), :, :].rearrange("a (k p) n -> p (a k) n", p=P)
            f1 = w_ff1[bass.ds(i, 1), :, :].rearrange("a (k p) n -> p (a k) n", p=P)
            f2 = w_ff2[bass.ds(i, 1), :, :].rearrange("a (k p) n -> p (a k) n", p=P)
            out = [(win_[:, :, 0:512], (KC, 512), (p2_mm, P2N, 4)), (win_[:, :, 512:COL_SB], (KC, COL_SB - 512), (p2_mm, P2N, 8))]
            out += [(win_[:, :, COL_SB + 512 * j:COL_SB + 512 * j + 512], (KC, 512), (p2_mm, P2N, (12, 16, 18)[j])) for j in range(3)]
            out += [(win_[:, :, COL_MG + 512 * j:COL_MG + 512 * j + 512], (KC, 512), (p2_mm, P2N, 22 + 4 * j)) for j in range(4)]
            out += [(wc[:, v], (CB // 2, 256), (cmp_mm, 3, v + 1)) for v in range(2)]
            out += [(wn, (4, D), (y2_mm, KC, KC)), (ws, (4, D), (y2_mm, KC, KC))]
            out += [(wo[:, :, 512 * j:512 * j + 512], (KC, 512), (wo_mm, WON, WON + 4 * j + 4)) for j in range(2)]
            out += [(f1[:, :, 512 * j:512 * j + 512], (KC, 512), (f1_mm, 32, 4 * j + 4)) for j in range(8)]
            out += [(f2[:, :, P * j:P * j + P], (32, P), (wo_mm, WON, WON + KC + j + 1)) for j in range(8)]
            assert len(out) == USED2
            return out

        def expert_loads(l, e):
            g = ex_gate[l][bass.ds(e, 1), :, :].rearrange("a (k p) n -> p (a k) n", p=P)
            u = ex_up[l][bass.ds(e, 1), :, :].rearrange("a (k p) n -> p (a k) n", p=P)
            d = ex_down[l][bass.ds(e, 1), :, :].rearrange("a (k p) n -> p (a k) n", p=P)
            return (g, (KC, DE)), (u, (KC, DE)), (d, (EC, D))

        @block.sync
        def _(sp):
            sp.dma_start(con[:, :], consts_in).then_inc(inputs_in, 16)
            sp.dma_start(par[:, :], params_in).then_inc(inputs_in, 16)
            sp.dma_start(xT[:, :, :, :], xT_in).then_inc(inputs_in, 16)
            sp.dma_start(E[:, 0:NX].bitcast(I32), pos_in).then_inc(inputs_in, 16)

            def static_loads(stream, n0):
                for j, (src, shape, _used) in enumerate(stream):
                    n = n0 + j
                    if j >= RING:
                        s, v = stream[j - RING][2]
                        sp.wait_ge(s, v)
                    sp.dma_start(slab(n, shape), src).then_inc(slab_in[n % RING], 16)
                    if stream is stream_b and j == NB_ - 6:
                        sp.wait_ge(h_ready, 3 * KC)
                        sp.dma_start(invcnt, invcnt_in).then_inc(invcnt_ready, 16)

            def expert_stream(l, before):
                sems = moe[l]
                sp.wait_ge(plan_ready, l + 1)
                pairs = sp.value_load(blki[0:1, MAXB:MAXB + 1], min_val=1, max_val=MAXB // 2)
                for s, v in before:
                    sp.wait_ge(s, v)
                with sp.Fori(0, pairs) as i:
                    for u in range(2):
                        e = sp.value_load(blki[0:1, bass.ds(2 * i + u, 1)], min_val=0, max_val=NE - 1)
                        loads = expert_loads(l, e)
                        for w in range(3):
                            sp.wait_ge(sems["gu_mm"] if w < 2 else sems["y_mm"], 2 * i + u + 1)
                            sp.sem_inc(spnop, 1)
                            src, shape = loads[w]
                            sp.dma_start(slab(3 * u + w, shape), src).then_inc(sems["w_in"][3 * u + w], 16)
                sp.wait_ge(sems["gu_mm"], 2 * pairs + 2)
                sp.sem_inc(spnop, 1)
                sp.wait_ge(sems["y_mm"], 2 * pairs + 2)
                sp.sem_inc(spnop, 1)

            static_loads(stream_a, 0)
            expert_stream(0, [stream_a[NA - RING + r][2] for r in range(RING)])
            static_loads(stream_b, NA)
            expert_stream(1, [stream_b[NB_ - RING + r][2] for r in range(RING)])

            with sp.Fori(0, 2) as i:
                slabs = layer_slabs(i)
                for j, (src, shape, _used) in enumerate(slabs):
                    if j < RING:
                        last = USED2 - 1 - (USED2 - 1 - j) % RING
                        sp.wait_ge(wo_mm, i * WON + KC + last - J_F2 + 1)
                    else:
                        s, per, v = slabs[j - RING][2]
                        sp.wait_ge(s, i * per + v)
                    sp.sem_inc(spnop, 1)
                    sp.dma_start(slab(j, shape), src).then_inc(slab_in[j % RING], 16)
                    if j == RING - 1:
                        sp.wait_ge(x2_ready, 6)
                        sp.wait_ge(xo_ready, i * 2 * KC + 1)
                        sp.sem_inc(spnop, 1)
                        sp.dma_start(lpar[:, :], lparams_in[bass.ds(i, 1), :, :].rearrange("a p n -> p (a n)")).then_inc(lpar_in, 16)
            sp.wait_ge(xo_ready, 2 * 2 * KC + 1)
            sp.dma_start(outT, xT[:, 0, :, :]).then_inc(out_stored, 16)
            sp.wait_ge(out_stored, 16)

        def g2(row):
            return row.rearrange("p (g t) -> p g t", g=TG)

        def src_of(full, k):
            return xT[:, :, k, :] if full else xT[:, 0, k, :]

        def hsrc(full, k):
            return hT[:, :, k, :] if full else hT[:, 0, k, :]

        def sq_of(full, k):
            return g2(sqb[:, k % 4, :]) if full else sqb[:, k % 4, 0:NX]

        def attention_units(layer):
            if layer == 0:
                return [(3 * h + k, h, k) for h in range(HEADS) for k in range(3)]
            return [(3 * HEADS + 2 * h + k, h, k) for h in range(HEADS) for k in range(2)]

        @block.scalar
        def _(act):
            chain = [0]

            def link(ins):
                chain[0] += 1
                ins.then_inc(achain, 1)
                act.wait_ge(achain, chain[0])

            eps = cc("eps")

            def norm(call, full, scale, shift):
                if not (isinstance(call, int) and call == 0):
                    act.wait_ge(h_ready, call * KC)
                for k in range(KC):
                    if k >= 4:
                        act.wait_ge(ssq_mm, call * KC + k - 3)
                    act.activation(sq_of(full, k), src_of(full, k), ACT.Square).then_inc(sq_ready, 1)
                act.wait_ge(ssq_mm, call * KC + KC)
                w = 512 if full else NX
                act.activation(stdv[:, 0:w], ps[:, 7, 0:w], ACT.Sqrt, bias=eps, scale=1.0 / D).then_inc(std_ready, 1)
                for k in range(KC):
                    act.wait_ge(xn_ready, call * KC + k + 1)
                    for g in range(TG if full else 1):
                        kw = dict(scale=scale(k, g))
                        if shift is not None:
                            kw["bias"] = shift(k, g)
                        ins = act.activation(hT[:, g, k, :], hT[:, g, k, :], ACT.Identity, **kw)
                    ins.then_inc(h_ready, 1)

            def evac(n, dst, src, func=ACT.Copy, **kw):
                act.wait_ge(proj_mm, n + 1)
                act.activation(dst, src, func, **kw).then_inc(proj_ev, 1)

            def qsq(g, c, w):
                act.wait_ge(proj_ev, proj_n["qk"][g])
                if g >= 2:
                    act.wait_ge(qss_mm, g - 1)
                act.activation(sqb[:, g % 2, 0:w], qk[:, c, 0:w], ACT.Square).then_inc(qsq_ready, 1)

            def qstd(g, w):
                act.wait_ge(qss_mm, g + 1)
                if g >= 2:
                    act.wait_ge(rope_ready, g - 1)
                act.activation(sqb[:, 2 + g % 2, 0:w], ps[:, 5, 0:w], ACT.Sqrt, bias=eps, scale=1.0 / DH).then_inc(qstd_ready, 1)

            def attend_exp(n, u, parts, sc):
                act.wait_ge(nb_ready, n + 1)
                for (c0, c1), m in parts:
                    ins = act.activation(prob[:, u, c0:c1], ps[:, u, c0:c1], ACT.Exp, bias=nb[:, u, m:m + 1], scale=sc,
                                         accum_out=sm[:, u, m:m + 1])
                ins.then_inc(ex_ready, 1)

            def attend_pt(n, u, nblk):
                act.wait_ge(tr_mm, n + 1)
                act.activation(probT[:, u, 0:nblk, :], ps[:, 2 + u, 0:nblk * P].rearrange("p (b q) -> p b q", b=nblk),
                               ACT.Copy).then_inc(pt_ready, 1)

            proj_n = {"qk": {}}
            act.wait_ge(inputs_in, 16 * n_in)
            act.activation(condv[:, :, :], pc("cond").rearrange("p (k c) -> p k c", c=2), ACT.Silu).then_inc(cond_ready, 1)

            act.wait_ge(trig_ready, 1)
            act.activation(sin2, sin2, ACT.Sin)
            act.activation(cos2, cos2, ACT.Sin).then_inc(trig_done, 1)

            def block1(layer):
                base, g0 = (0, 0) if layer == 0 else (14, 5)
                full = layer == 0
                act.wait_ge(mod_ready, layer + 1)
                norm(2 * layer, True, lambda k, g: scale1[:, k, g:g + 1], lambda k, g: modv[:, k, g:g + 1])
                w = 512 if full else NX
                for c in range(QKC):
                    wc = 512 if c == QC else w
                    evac(base + c, qk[:, c, 0:wc], ps[:, c % 4, 0:wc])
                    proj_n["qk"][g0 + c] = base + c + 1
                evac(base + 5, vtok, ps[:, 1, :].rearrange("p (n d) -> p n d", n=4))
                for n in range(8):
                    if n < QKC:
                        qsq(g0 + n, n, 512 if n == QC else w)
                    if full:
                        m = base + 6 + n
                        src = g2(ps[:, (6 + n) % 4, :])
                        if n < BC:
                            act.wait_ge(setup_done, 1)
                            evac(m, gpad[:, n, :, HALO:HALO + NX], src)
                        else:
                            evac(m, g2(cat[:, n, :]), src, ACT.Sigmoid)
                    elif n < BC:
                        act.wait_ge(setup_done, 3)
                        evac(base + 6 + n, upad[:, n, PPAD:PPAD + NX], ps[:, (6 + n) % 4, 0:NX])
                    if n < QKC:
                        qstd(g0 + n, 512 if n == QC else w)
                act.wait_ge(swap_mm, layer + 1)
                act.activation(kswap, ps[:, 6, :], ACT.Copy).then_inc(swap_ev, 1)
                units = attention_units(layer)
                for s in range(len(units) + 1):
                    if s < len(units):
                        n, h, kind = units[s]
                        u = n % 2
                        if n >= 2:
                            act.wait_ge(tr_mm, n - 1)
                        if kind == 2:
                            attend_exp(n, u, [((0, 256), 0), ((256, 512), 1)], SC_A)
                        else:
                            attend_exp(n, u, [((0, 512), 0)], SC_A)
                            if layer == 1:
                                act.activation(es[:, u, :], pc("sink", h, 1), ACT.Exp, bias=nb[:, u, 0:1]).then_inc(sink_ready, 1)
                    if s >= 1:
                        n, h, kind = units[s - 1]
                        if n >= 2:
                            act.wait_ge(pv_mm, n - 1)
                        attend_pt(n, n % 2, 4)
                        if s >= 2:
                            head_out(units[s - 2], layer)
                head_out(units[-1], layer)
                if full:
                    act.wait_ge(cd_ready, 1)
                    for c in range(BC):
                        act.activation(sqb[:, c, :], cat[:, 4 + c, :], ACT.Square).then_inc(csq_ready, 1)
                    act.wait_ge(cvar_mm, 1)
                    act.activation(stdv[:, :], ps[:, 5, :], ACT.Sqrt, bias=eps, scale=1.0 / 512).then_inc(cstd_ready, 1)
                    for c in range(BC):
                        act.wait_ge(cn_ready, c + 1)
                        act.activation(cat[:, 4 + c, :], cat[:, 4 + c, :], ACT.Silu, scale=pc("cln_g", c, 1),
                                       bias=pc("cln_b", c, 1)).then_inc(bx_ready, 1)
                act.wait_ge(x_ready, KC * (layer + 1))
                norm(2 * layer + 1, full, lambda k, g: scale2[:, k, g:g + 1], lambda k, g: modv[:, 24 + k, g:g + 1])

            def head_out(unit, layer):
                n, h, kind = unit
                last = kind == 2 if layer == 0 else kind == 1
                if h % 2 == 1 and last:
                    act.wait_ge(pv_mm, n + 1)
                    w = 512 if layer == 0 else NX
                    act.activation(cat[:, h // 2, 0:w], ps[:, 4 + (h // 2) % 2, 0:w], ACT.Copy).then_inc(o_ready, 1)

            def experts(l):
                nt = NTM if l == 0 else QT
                sems = moe[l]
                for q in range(2 * nt):
                    act.wait_ge(ht_mm, (0, 2 * NTM)[l] + q + 1)
                    act.activation(htok[:, q // 2, (q % 2) * 512:(q % 2) * 512 + 512], ps[:, 4 + q % 3, :], ACT.Copy).then_inc(ht_ev, 1)
                act.wait_ge(gmax_ready, l + 1)
                for n in range(nt):
                    act.activation(pen[:, n, :], lgp[:, n, 0:NG], ACT.Exp, bias=rsc[:, 0, n:n + 1], accum_out=rsc[:, 1, n:n + 1])
                act.activation(rsc[:, 3, 0:nt], rsc[:, 2, 0:nt], ACT.Exp).then_inc(gexp_ready, 1)
                act.wait_ge(plan_ready, l + 1)
                pairs = act.value_load(blki[0:1, MAXB:MAXB + 1], min_val=1, max_val=MAXB // 2)
                act.sem_inc(sems["y_ready"], 2)
                act.sem_inc(sems["y_stored"], 32)
                with act.Fori(0, pairs) as i:
                    for u in range(2):
                        act.wait_ge(sems["xg_mm"], 2 * i + u + 1)
                        act.activation(xg[:, u, :, :], ps[:, u, :].rearrange("p (k s) -> p k s", k=KC), ACT.Copy).then_inc(sems["xg_ready"], 1)
                    for u in range(2):
                        act.wait_ge(sems["gu_mm"], 2 * i + u + 3)
                        act.activation(silu_g[:, u, :], ps[:, 2 + u, 0:EC * SLOTS], ACT.Silu).then_inc(sems["sg_ready"], 1)
                    for u in range(2):
                        act.wait_ge(sems["y_mm"], 2 * i + u + 3)
                        act.wait_ge(sems["y_stored"], 32 * i + 32)
                        act.activation(yb[:, u, :], ps[0:SLOTS, 4 + 2 * u:6 + 2 * u, :].rearrange("p a b -> p (a b)"), ACT.Copy).then_inc(sems["y_ready"], 1)
                        act.wait_ge(sems["y_ready"], 2 * i + u + 3)
                        act.dma_start(y_rows[bass.ds(i * PAIR + u * SLOTS, SLOTS), :], yb[:, u, :]).then_inc(sems["y_stored"], 16)
                act.wait_ge(sems["y_stored"], 32 * pairs + 32)
                act.sem_inc(stored_all, 1)

            block1(0)
            experts(0)
            block1(1)
            experts(1)

            def layer2(i):
                call = 4 + 2 * i
                act.wait_ge(lpar_in, 16 * i + 16)
                act.wait_ge(x2_ready, 6)
                act.wait_ge(xo_ready, 2 * KC * i + 1)
                norm(call, False, lambda k, g: lp("norm_g", k, 1), None)

                def ev2(n, dst, src, func=ACT.Copy, **kw):
                    act.wait_ge(p2_mm, P2N * i + n + 1)
                    return act.activation(dst, src, func, **kw)

                for n in range(4):
                    ev2(n, qp[:, n, :], ps[:, n % 4, 0:NX]).then_inc(p2_ev, 1)
                for n in range(4, 7):
                    ev2(n, kv[:, n - 4, :], ps[:, n % 4, 0:NX]).then_inc(p2_ev, 1)
                ev2(7, vsw, ps[:, 3, 0:NX].rearrange("p (n d) -> p n d", n=QT))
                ev2(7, gates[:, :, :], ps[:, 3, NX:NX + 48].rearrange("p (n d) -> p n d", n=QT), ACT.Sigmoid).then_inc(p2_ev, 1)
                for n in range(8, 12):
                    ev2(n, sbq[:, n - 8, :], ps[:, n % 4, 0:NX], scale=SC_B).then_inc(p2_ev, 1)
                for n in range(12, 16):
                    ev2(n, sbk[:, n - 12, :], ps[:, n % 4, 0:NX]).then_inc(p2_ev, 1)
                for n in range(16, 18):
                    ev2(n, sbv[:, n - 16, :], ps[:, n % 4, :]).then_inc(p2_ev, 1)
                for n in range(18, P2N):
                    ev2(n, mg[:, n - 18, :], ps[:, n % 4, 0:NX], ACT.Sigmoid).then_inc(p2_ev, 1)
                act.wait_ge(cmp_mm, 3 * i + 2)
                act.activation(hcmp[:, :, :], ps[:, 6, 0:64].rearrange("p (v c) -> p v c", v=4), ACT.Copy).then_inc(cmp_ready, 1)
                act.wait_ge(cmp_ready, i + 1)
                for q in range(4):
                    ins = act.activation(gcmp[:, q, :], hcmp[:, q, 0:NCMP], ACT.Gelu_apprx_tanh, bias=hcmp[:, q, NCMP:NCMP + 1])
                ins.then_inc(gel_ready, 1)
                act.wait_ge(pcn_ready, 2 * i + 1)
                act.activation(scmp, scmp, ACT.Exp, scale=SC_A).then_inc(pce_ready, 1)
                act.wait_ge(pct_mm, i + 1)
                act.activation(pcT, ps[:, 4, :].rearrange("p (b q) -> p b q", b=4), ACT.Copy).then_inc(pct_ready, 1)
                zp = ps[:, 0:SBH, 0:384]
                act.wait_ge(sbz_mm, i + 1)
                act.activation(spl, zp, ACT.Abs).then_inc(sb_act, 1)
                act.wait_ge(sb_act, 5 * i + 1)
                act.activation(spl, spl, ACT.Exp, scale=-1.0).then_inc(sb_act, 1)
                act.wait_ge(sb_act, 5 * i + 2)
                act.activation(spl, spl, ACT.Ln, bias=1.0).then_inc(sb_act, 1)
                act.wait_ge(sb_dve, 2 * i + 2)
                act.activation(zs, zs, ACT.Exp).then_inc(sb_act, 1)
                act.wait_ge(sbo_mm, i + 1)
                act.activation(osb, ps[:, 0:SBH, 0:NX], ACT.Copy).then_inc(sb_act, 1)
                for s in range(2 * HEADS + 2):
                    if s < 2 * HEADS:
                        n, u, k = 40 + 16 * i + s, s % 2, P * (s % 2 + 1)
                        act.wait_ge(tr_mm, n - 1)
                        attend_exp(n, u, [((0, k), 0), ((NX, NX + k), 1)], SC_A)
                    if 1 <= s <= 2 * HEADS:
                        n, u = 40 + 16 * i + s - 1, (s - 1) % 2
                        act.wait_ge(pv_mm, n - 1)
                        attend_pt(n, u, 2 * (u + 1))
                    if s >= 2 and (s - 2) % 4 == 3:
                        n, c = 40 + 16 * i + s - 2, (s - 2) // 4
                        act.wait_ge(pv_mm, n + 1)
                        act.activation(onsa[:, c, :], ps[:, 4 + c % 2, 0:NX], ACT.Copy).then_inc(o_ready, 1)

                def out_norm(c):
                    for m in range(KC):
                        act.wait_ge(wo_mm, WON + WON * i + KC * c + m + 1)
                        if m >= 4:
                            act.wait_ge(nss_mm, WON * i + KC * c + m - 3)
                        act.activation(yres[:, m, :], ps[:, m % 4, 0:NX], ACT.Copy)
                        act.activation(sqb[:, m % 4, 0:NX], ps[:, m % 4, 0:NX], ACT.Square).then_inc(nsq_ready, 1)
                    act.wait_ge(nss_mm, WON * i + KC * c + KC)
                    act.activation(stdv[:, 0:NX], ps[:, 7, 0:NX], ACT.Sqrt, bias=eps, scale=1.0 / D).then_inc(nstd_ready, 1)

                out_norm(0)
                act.wait_ge(xo_ready, 2 * KC * i + 1 + KC)
                norm(call + 1, False, lambda k, g: lp("norm_g", 2 * KC + k, 1), None)
                for m in range(FF // P):
                    act.wait_ge(f1_mm, 32 * i + m + 1)
                    if m >= 4:
                        act.wait_ge(ffh_ready, 32 * i + m - 3)
                    act.activation(sqb[:, m % 4, 0:NX], ps[:, m % 4, 0:NX], ACT.Relu).then_inc(f1_ev, 1)
                out_norm(1)

            with act.Fori(0, 2) as i:
                layer2(i)

        @block.tensor
        def _(pe):
            def take_slab(n, shape):
                pe.wait_ge(slab_in[n % RING], 16 * (n // RING + 1))
                return slab(n, shape)

            def mm_chunk(out, w, m0, rhs, nk=KC, start=True, stop=True):
                for k in range(nk):
                    ins = pe.matmul(out, w[:, k, m0:m0 + P], rhs(k), start=start and k == 0, stop=stop and k == nk - 1)
                return ins

            def norm(call, full):
                w = 512 if full else NX
                for k in range(KC):
                    pe.wait_ge(sq_ready, KC * call + k + 1)
                    pe.matmul(ps[:, 7, 0:w], ones[:, :], sqb[:, k % 4, 0:w], start=k == 0, stop=k == KC - 1).then_inc(ssq_mm, 1)

            def modulation(l, n0):
                for s in range(12):
                    w = take_slab(n0 + s, (KC, 512))
                    for m in range(4):
                        col = 2 * (4 * s + m)
                        for k in range(KC):
                            ins = pe.matmul(ps[:, 6, col:col + 2], w[:, k, m * P:m * P + P], condv[:, k, :], start=k == 0, stop=k == KC - 1)
                    ins.then_inc(mod_mm, 1)

            def qss(g, c, w):
                pe.wait_ge(qsq_ready, g + 1)
                if g >= 1:
                    pe.wait_ge(qstd_ready, g)
                pe.matmul(ps[:, 5, 0:w], cc("headones"), sqb[:, g % 2, 0:w], start=True, stop=True).then_inc(qss_mm, 1)

            def qrot(g, c):
                pe.wait_ge(qn_ready, g + 1)
                if g >= 1:
                    pe.wait_ge(rope_ready, g)
                pe.matmul(ps[:, 6, 0:NX], cc("rot_a"), qk[:, c, 0:NX], start=True, stop=True).then_inc(rot_mm, 1)

            def block1(layer):
                full = layer == 0
                base, g0 = (0, 0) if full else (14, 5)
                n0 = 12 if full else NA + 12
                norm(2 * layer, True)
                pe.wait_ge(h_ready, KC * (2 * layer + 1))

                def bank_free(n):
                    if n >= 4:
                        pe.wait_ge(proj_ev, base + n - 3)

                w = take_slab(n0, (KC, 512))
                wq = 512 if full else NX
                for c in range(QC):
                    mm_chunk(ps[:, c, 0:wq], w, c * P, lambda k: hsrc(full, k)).then_inc(proj_mm, 1)
                w = take_slab(n0 + 1, (KC, 512))
                bank_free(4)
                mm_chunk(ps[:, 0, :], w, 0, lambda k: hsrc(True, k)).then_inc(proj_mm, 1)
                bank_free(5)
                for n in range(4):
                    for k in range(KC):
                        ins = pe.matmul(ps[:, 1, n * P:n * P + P], hT[:, n // 2, k, (n % 2) * P:(n % 2) * P + P], w[:, k, P:2 * P],
                                        start=k == 0, stop=k == KC - 1)
                ins.then_inc(proj_mm, 1)
                for n in range(8):
                    m = n + 2
                    if (full or n < BC) and m % 4 == 0:
                        w = take_slab(n0 + 1 + m // 4, (KC, 512 if full and m < 12 and not m == 8 else 256))
                    if full or n < BC:
                        bank_free(6 + n)
                        mm_chunk(ps[:, (6 + n) % 4, 0:wq], w, (m % 4) * P, lambda k: hsrc(full, k)).then_inc(proj_mm, 1)
                    if n < QKC:
                        qss(g0 + n, n, 512 if n == QC else wq)
                    if 1 <= n <= QKC:
                        qrot(g0 + n - 1, n - 1)
                pe.wait_ge(rope_ready, g0 + QKC)
                pe.matmul(ps[:, 6, :], cc("swap"), qk[:, QC, :], start=True, stop=True).then_inc(swap_mm, 1)
                pe.wait_ge(swap_ev, layer + 1)
                pe.wait_ge(proj_ev, base + (14 if full else 10))
                units = attention_units(layer)
                for s in range(len(units) + 2):
                    if s < len(units):
                        n, h, kind = units[s]
                        if s >= 2:
                            pe.wait_ge(ex_ready, n - 1)
                        o, j = (h % 2) * DH, h // 4
                        kk = qk[:, QC, :] if o == j * DH else kswap
                        u = n % 2
                        if kind == 2:
                            for t in range(QT):
                                ins = pe.matmul(ps[:, u, t * NX:t * NX + NX], qk[o:o + DH, h // 2, NX + t * P:NX + t * P + P],
                                                kk[o:o + DH, NX:512], start=True, stop=True)
                        else:
                            ins = pe.matmul(ps[:, u, :], qk[o:o + DH, h // 2, kind * P:kind * P + P], kk[o:o + DH, :],
                                            start=True, stop=full)
                            if not full:
                                c0 = P if kind == 0 else 0
                                ins = pe.matmul(ps[:, u, c0:c0 + P], ident, cc("trineg") if kind == 0 else cc("band1"), start=False, stop=True)
                        ins.then_inc(sc_mm, 1)
                    if 1 <= s <= len(units):
                        n = units[s - 1][0]
                        transposes(n, n % 2, [(b * P, b * P + P) for b in range(4)], s > 2)
                    if s >= 2:
                        n, h, kind = units[s - 2]
                        pe.wait_ge(pt_ready, n + 1)
                        o, j, u = (h % 2) * DH, h // 4, n % 2
                        ch = h // 2
                        if ch >= 2 and h % 2 == 0 and kind == 0:
                            pe.wait_ge(o_ready, 4 * layer + ch - 1)
                        ob = ps[o:o + DH, 4 + ch % 2, :]
                        if kind == 2:
                            for t in range(QT):
                                for b in range(2):
                                    ins = pe.matmul(ob[:, NX + t * P:NX + t * P + P], vtok[:, 2 + b, j * DH:j * DH + DH], probT[:, u, 2 * t + b, :],
                                                    start=b == 0, stop=b == 1)
                        else:
                            for b in range(4):
                                ins = pe.matmul(ob[:, kind * P:kind * P + P], vtok[:, b, j * DH:j * DH + DH], probT[:, u, b, :],
                                                start=b == 0, stop=b == 3)
                        ins.then_inc(pv_mm, 1)
                if full:
                    pe.wait_ge(conv_ready, 1)
                    for c in range(BC):
                        ins = pe.matmul(ps[:, 6, :], ones[:, :], cat[:, 4 + c, :], start=c == 0, stop=c == BC - 1)
                    ins.then_inc(cmu_mm, 1)
                    pe.wait_ge(o_ready, 4)
                    for c in range(BC):
                        pe.wait_ge(csq_ready, c + 1)
                        ins = pe.matmul(ps[:, 5, :], ones[:, :], sqb[:, c, :], start=c == 0, stop=c == BC - 1)
                    ins.then_inc(cvar_mm, 1)
                    pe.wait_ge(bx_ready, BC)
                else:
                    wp = take_slab(n0 + 3, (BC, P))
                    pe.wait_ge(pool_ready, BC)
                    for g in range(BC):
                        ins = pe.matmul(ps[:, 6 + g // 2, (g % 2) * NX:(g % 2) * NX + NX], wp[:, g, :], pt_pool[:, g, :], start=True, stop=True)
                    ins.then_inc(pool_mm, 1)
                    pe.wait_ge(px_ready, 1)
                pe.wait_ge(o_ready, 4 * layer + 4)
                ow = n0 + 4
                for m in range(KC):
                    if m % 4 == 0:
                        w = take_slab(ow + m // 4, (KC, 512))
                    if m >= 4:
                        pe.wait_ge(x_ready, KC * layer + m - 3)
                    mm_chunk(ps[:, m % 4, 0:wq], w, (m % 4) * P, lambda k: cat[:, k, 0:wq]).then_inc(out_mm, 1)
                norm(2 * layer + 1, full)

            def transposes(n, u, blocks, again):
                pe.wait_ge(pn_ready, n + 1)
                if again:
                    pe.wait_ge(pt_ready, n - 1)
                for b, (c0, c1) in enumerate(blocks):
                    ins = pe.transpose(ps[:, 2 + u, b * P:b * P + P], prob[:, u, c0:c1], ident)
                ins.then_inc(tr_mm, 1)

            def experts(l):
                nt = NTM if l == 0 else QT
                sems = moe[l]
                pe.wait_ge(h_ready, KC * (2 * l + 2))

                def htile(n, k):
                    return hT[:, n // 2, k, (n % 2) * P:(n % 2) * P + P]

                for n in range(nt):
                    for k in range(KC):
                        at, _ = po["rt_w"]
                        w = par[:, at + (l * KC + k) * RL:at + (l * KC + k + 1) * RL]
                        ins = pe.matmul(ps[:, 0, n * RL:(n + 1) * RL], htile(n, k), w, start=k == 0, stop=k == KC - 1)
                ins.then_inc(rt_mm, 1)
                for q in range(2 * nt):
                    if q >= 3:
                        pe.wait_ge(ht_ev, (0, 2 * NTM)[l] + q - 2)
                    for b in range(4):
                        ins = pe.transpose(ps[:, 4 + q % 3, b * P:b * P + P], htile(q // 2, 4 * (q % 2) + b), ident)
                    ins.then_inc(ht_mm, 1)
                pe.wait_ge(m_ready, l + 1)
                for n in range(nt):
                    for j in range(n + 1):
                        pe.matmul(ps[:, 1, n * NE:(n + 1) * NE], cc("tri_strict") if j == n else ones[:, :], M1[:, 2, j * NE:(j + 1) * NE],
                                  start=j == 0, stop=j == n)
                for j in range(nt):
                    ins = pe.matmul(ps[:, 1, nt * NE:(nt + 1) * NE], ones[:, :], M1[:, 2, j * NE:(j + 1) * NE], start=j == 0, stop=j == nt - 1)
                ins.then_inc(pos_mm, 1)
                pe.wait_ge(plan_ready, l + 1)
                pe.wait_ge(ht_ev, (2 * NTM, 2 * NTM + 2 * QT)[l])
                pairs = pe.value_load(blki[0:1, MAXB:MAXB + 1], min_val=1, max_val=MAXB // 2)
                pe.sem_inc(sems["gu_mm"], 2)
                pe.sem_inc(sems["y_mm"], 2)
                with pe.Fori(0, pairs) as i:
                    pe.wait_ge(sems["sel_ready"], i + 1)
                    for u in range(2):
                        for k in range(KC):
                            for n in range(nt):
                                ins = pe.matmul(ps[:, u, k * SLOTS:(k + 1) * SLOTS], htok[:, n, k * P:(k + 1) * P],
                                                sel[:, 0, n, u * SLOTS:(u + 1) * SLOTS], start=n == 0, stop=n == nt - 1)
                        ins.then_inc(sems["xg_mm"], 1)
                    for u in range(2):
                        pe.wait_ge(sems["xg_ready"], 2 * i + u + 1)
                        for w in range(2):
                            pe.wait_ge(sems["w_in"][3 * u + w], 16 * i + 16)
                            sl = slab(3 * u + w, (KC, DE))
                            for m in range(EC):
                                c0 = (w * EC + m) * SLOTS
                                ins = mm_chunk(ps[:, 2 + u, c0:c0 + SLOTS], sl, m * P, lambda k: xg[:, u, k, :])
                        ins.then_inc(sems["gu_mm"], 1)
                    for u in range(2):
                        pe.wait_ge(sems["hid_ready"], 2 * i + u + 1)
                        pe.wait_ge(sems["w_in"][3 * u + 2], 16 * i + 16)
                        pe.wait_ge(sems["y_ready"], 2 * i + u + 1)
                        sl = slab(3 * u + 2, (EC, D))
                        for c in range(2):
                            for m in range(EC):
                                ins = pe.matmul(ps[0:SLOTS, 4 + 2 * u + c, :], hid[:, u, m, :], sl[:, m, c * 512:(c + 1) * 512],
                                                start=m == 0, stop=m == EC - 1)
                        ins.then_inc(sems["y_mm"], 1)
                for n in range(nt):
                    t = (0, NTM)[l] + n
                    pe.wait_ge(mix_ready, t + 1)
                    if n >= 2:
                        pe.wait_ge(x2_ready, t - 1)
                    for k in range(KC):
                        ins = pe.transpose(ps[:, 2 * (n % 2) + k // 4, (k % 4) * P:(k % 4 + 1) * P], yg[:, n, 0, k * P:(k + 1) * P], ident)
                    ins.then_inc(yt_mm, 1)

            pe.wait_ge(inputs_in, 16 * n_in)
            pe.wait_ge(setup_done, 2)
            pe.wait_ge(cond_ready, 1)
            modulation(0, 0)
            block1(0)
            experts(0)
            modulation(1, NA)
            block1(1)
            experts(1)

            def layer2(i):
                call = 4 + 2 * i

                def take(j, shape):
                    pe.wait_ge(slab_in[j % RING], slab2_count(i, j))
                    return slab(j, shape)

                hn = lambda k: hT[:, 0, k, :]
                norm(call, False)
                pe.wait_ge(h_ready, KC * call + KC)
                evs = P2N * i

                def bank_free(n):
                    if n >= 4:
                        pe.wait_ge(p2_ev, evs + n - 3)

                def chunks(n, j, count, width=512):
                    w = take(j, (KC, width))
                    for c in range(count):
                        bank_free(n + c)
                        mm_chunk(ps[:, (n + c) % 4, 0:NX], w, c * P, hn).then_inc(p2_mm, 1)
                    return w

                chunks(0, 0, 4)
                w = chunks(4, 1, 3, COL_SB - 512)
                bank_free(7)
                for t in range(QT):
                    for k in range(KC):
                        pe.matmul(ps[:, 3, t * P:t * P + P], hT[:, 0, k, t * P:t * P + P],
                                  w[:, k, P:3 * P].rearrange("p (b d) -> p b d", b=2)[:, :, DH:P], start=k == 0, stop=k == KC - 1)
                for t in range(QT):
                    for k in range(KC):
                        ins = pe.matmul(ps[:, 3, NX + t * 24:NX + t * 24 + 24], hT[:, 0, k, t * P:t * P + P], w[:, k, 3 * P:3 * P + 24],
                                        start=k == 0, stop=k == KC - 1)
                ins.then_inc(p2_mm, 1)
                pe.wait_ge(p2_ev, evs + 7)
                for c in range(4):
                    pe.matmul(ps[:, 4 + c // 2, (c % 2) * NX:(c % 2) * NX + NX], cc("rot_b"), qp[:, c, :], start=True, stop=True).then_inc(r2_mm, 1)
                for c in range(2):
                    pe.matmul(ps[:, 6, c * NX:c * NX + NX], cc("rot_b"), kv[:, 1 + c, :], start=True, stop=True).then_inc(r2_mm, 1)
                chunks(8, 2, 4)
                pe.wait_ge(r2_ready, 10 * i + 6)
                for c, m in enumerate(("dup0", "dup1")):
                    pe.matmul(ps[:, 4, c * NX:c * NX + NX], cc(m), kv[:, 0, :], start=True, stop=True).then_inc(r2_mm, 1)
                for c in range(2):
                    pe.matmul(ps[:, 5, c * NX:c * NX + NX], cc("dup0"), kv[:, 1 + c, :], start=True, stop=True).then_inc(r2_mm, 1)
                chunks(12, 3, 4)
                w = take(4, (KC, 512))
                for t in range(QT):
                    bank_free(16 + t)
                    for k in range(KC):
                        ins = pe.matmul(ps[:, (16 + t) % 4, :], hT[:, 0, k, t * P:t * P + P], w[:, k, :], start=k == 0, stop=k == KC - 1)
                    ins.then_inc(p2_mm, 1)
                for j in range(4):
                    chunks(18 + 4 * j, 5 + j, 4)
                pe.wait_ge(r2_ready, 10 * i + 10)
                for v in range(2):
                    w = take(J_CMP + v, (CB // 2, 256))
                    for c in range(2):
                        for j in range(CB // 2):
                            ins = pe.matmul(ps[:, 6, (2 * v + c) * 16:(2 * v + c) * 16 + 16], w[:, j, c * P:c * P + P], win[:, v, j, :],
                                            start=j == 0, stop=j == CB // 2 - 1)
                    ins.then_inc(cmp_mm, 1)
                pe.wait_ge(gel_ready, i + 1)
                w2 = lambda v, c: lp("w2", (2 * v + c) * 64, 64)
                for o in range(2):
                    for c in range(2):
                        pe.matmul(ps[o * DH:o * DH + DH, 4, 0:NCMP], w2(0, c), gcmp[:, c, :], start=c == 0, stop=c == 1)
                for hh in range(4):
                    for c in range(2):
                        ins = pe.matmul(ps[32 * hh:32 * hh + NCMP, 4, 64:128], gcmp[:, 2 + c, :], w2(1, c), start=c == 0, stop=c == 1)
                ins.then_inc(cmp_mm, 1)
                pe.wait_ge(cev_ready, i + 1)
                for t in range(QT):
                    for h in range(HEADS):
                        o, c0 = (h % 2) * DH, (t * HEADS // 2 + h // 2) * 16
                        ins = pe.matmul(ps[:, 5 + h % 2, c0:c0 + NCMP], qp[o:o + DH, h // 2, t * P:t * P + P], kcmp[o:o + DH, :], start=True, stop=True)
                ins.then_inc(cs_mm, 1)
                pe.wait_ge(pcn_ready, 2 * i + 2)
                for t in range(QT):
                    for q in range(2):
                        ins = pe.transpose(ps[:, 4, (2 * t + q) * P:(2 * t + q + 1) * P],
                                           pcp[:, t, 4 * q:4 * q + 4, :].rearrange("p h c -> p (h c)"), ident)
                ins.then_inc(pct_mm, 1)
                pe.wait_ge(p2_ev, evs + P2N)
                for h in range(SBH):
                    pe.matmul(ps[:, h, 0:NX], sbk[:, h, 0:P], sbq[:, h, :], start=True, stop=True)
                    ins = pe.matmul(ps[:, h, NX:384], sbk[:, h, P:NX], sbq[:, h, P:NX], start=True, stop=True)
                ins.then_inc(sbz_mm, 1)
                pe.wait_ge(sb_dve, 2 * i + 1)
                pe.wait_ge(pct_ready, i + 1)
                for h in range(SBH):
                    b = 4 + h
                    pe.matmul(ps[:, b, 0:P], cc("negtri"), spl[:, h, 0:P], start=True, stop=True)
                    pe.matmul(ps[:, b, P:NX], cc("negtri"), spl[:, h, P:NX], start=True, stop=False)
                    pe.matmul(ps[:, b, P:NX], negones[:, :], spl[:, h, NX:384], start=False, stop=True)
                    ins = pe.matmul(ps[:, b, NX:384], cc("negtri"), spl[:, h, NX:384], start=True, stop=True)
                ins.then_inc(sbc_mm, 1)
                pe.wait_ge(sb_act, 5 * i + 4)
                for h in range(SBH):
                    pe.matmul(ps[:, h, 0:NX], sbv[:, 0, h * P:h * P + P], zs[:, h, 0:NX], start=True, stop=False)
                    ins = pe.matmul(ps[:, h, P:NX], sbv[:, 1, h * P:h * P + P], zs[:, h, NX:384], start=False, stop=True)
                ins.then_inc(sbo_mm, 1)
                pe.wait_ge(sb_act, 5 * i + 5)
                for s in range(2 * HEADS + 2):
                    if s < 2 * HEADS:
                        n, h, t = 40 + 16 * i + s, s // 2, s % 2
                        o, k = (h % 2) * DH, P * (t + 1)
                        pe.wait_ge(ex_ready, n - 1)
                        for b in range(2):
                            pe.matmul(ps[:, t, b * NX:b * NX + k], qr[o:o + DH, h // 2, t * P:t * P + P], kdup[o:o + DH, b, 0:k], start=True, stop=False)
                            ins = pe.matmul(ps[:, t, b * NX + t * P:b * NX + k], ident, cc("trineg"), start=False, stop=True)
                        ins.then_inc(sc_mm, 1)
                    if 1 <= s <= 2 * HEADS:
                        t = (s - 1) % 2
                        transposes(40 + 16 * i + s - 1, t, [(b * NX + j * P, b * NX + j * P + P) for b in range(2) for j in range(t + 1)], True)
                    if s >= 2:
                        n, h, t = 40 + 16 * i + s - 2, (s - 2) // 2, s % 2
                        o, c = (h % 2) * DH, h // 2
                        pe.wait_ge(pt_ready, n + 1)
                        if t == 0 and h % 2 == 0:
                            pe.wait_ge(o_ready, 8 + 4 * i + max(c - 1, 0))
                        ob = ps[o:o + DH, 4 + c % 2, t * P:t * P + P]
                        pe.matmul(ob, vblk[:, h % 4, :], pcT[:, 2 * t + h // 4, :], start=True, stop=False)
                        for b in range(2):
                            for j in range(t + 1):
                                ins = pe.matmul(ob, vsw[:, j, b * DH:b * DH + DH], probT[:, t, b * (t + 1) + j, :], start=False,
                                                stop=b == 1 and j == t)
                        ins.then_inc(pv_mm, 1)
                pe.wait_ge(o_ready, 8 + 4 * i + 4)
                wn, ws = take(J_NSA, (4, D)), take(J_SB, (4, D))
                for m in range(KC):
                    if m >= 4:
                        pe.wait_ge(mix2_ready, KC * i + m - 3)
                    mm_chunk(ps[:, m % 4, 0:NX], wn, m * P, lambda k: onsa[:, k, :], 4)
                    mm_chunk(ps[:, m % 4, NX:512], ws, m * P, lambda k: osb[:, k, :], 4).then_inc(y2_mm, 1)

                def out_norm(c, chunk):
                    for m in range(KC + 1):
                        if m < KC:
                            if m >= 4:
                                pe.wait_ge(nsq_ready, WON * i + KC * c + m - 3)
                            chunk(m).then_inc(wo_mm, 1)
                        if m >= 1:
                            pe.wait_ge(nsq_ready, WON * i + KC * c + m)
                            pe.matmul(ps[:, 7, 0:NX], ones[:, :], sqb[:, (m - 1) % 4, 0:NX], start=m == 1, stop=m == KC).then_inc(nss_mm, 1)

                pe.wait_ge(mix2_ready, KC * i + KC)
                wo = [take(J_OUT + j, (KC, 512)) for j in range(2)]
                out_norm(0, lambda m: mm_chunk(ps[:, m % 4, 0:NX], wo[m // 4], (m % 4) * P, lambda k: mixT[:, k, :]))
                norm(call + 1, False)
                pe.wait_ge(h_ready, KC * call + 2 * KC)
                for j in range(8):
                    w = take(J_F1 + j, (KC, 512))
                    for c in range(4):
                        m = 4 * j + c
                        if m >= 4:
                            pe.wait_ge(f1_ev, 32 * i + m - 3)
                        mm_chunk(ps[:, m % 4, 0:NX], w, c * P, hn).then_inc(f1_mm, 1)
                pe.wait_ge(ffh_ready, 32 * i + 32)
                out_norm(1, lambda m: mm_chunk(ps[:, m % 4, 0:NX], take(J_F2 + m, (32, P)), 0, lambda k: ffh[:, k, :], 32))

            pe.wait_ge(trig_done, 1)
            pe.wait_ge(x2_ready, 6)
            pe.sem_inc(wo_mm, WON)
            with pe.Fori(0, 2) as i:
                layer2(i)

        @block.vector
        def _(dve):
            chain = [0]

            def link(ins):
                chain[0] += 1
                ins.then_inc(dchain, 1)
                dve.wait_ge(dchain, chain[0])

            def step(ins, back):
                chain[0] += 1
                ins.then_inc(dchain, 1)
                if chain[0] > back:
                    dve.wait_ge(dchain, chain[0] - back)

            iota = cc("iota")

            def norm(call, full):
                w = 512 if full else NX
                dve.wait_ge(std_ready, call + 1)
                dve.reciprocal(stdv[:, 0:w], stdv[:, 0:w]).then_inc(rstd_ready, 1)
                dve.wait_ge(rstd_ready, call + 1)
                for k in range(KC):
                    dve.tensor_tensor(hsrc(full, k), src_of(full, k), g2(stdv[:, :]) if full else stdv[:, 0:NX], ALU.mult).then_inc(xn_ready, 1)

            dve.memset(gpad, 0.0).then_inc(setup_done, 1)
            dve.memset(ones[:, :], 1.0)
            dve.memset(negones[:, :], -1.0)
            dve.memset(pcp[:, :, :, :], 0.0)
            dve.memset(vblk[:, :, :], 0.0)
            dve.wait_ge(inputs_in, 16 * n_in)
            dve.tensor_scalar(mneg[:, :], cc("m01"), 1.0, -NEG, ALU.subtract, ALU.mult).then_inc(setup_done, 1)
            ang, kf = sqb[:, 0, 0:NX], sqb[:, 1, 0:NX]
            link(dve.tensor_copy(ang, E[:, 0:NX].bitcast(I32)))
            link(dve.tensor_scalar(ang, ang, cc("invf"), None, ALU.mult))
            link(dve.tensor_scalar(kf, ang, 1.0 / TWO_PI, None, ALU.mult))
            link(dve.tensor_scalar(kf, kf, MAGIC, None, ALU.add))
            link(dve.tensor_scalar(kf, kf, MAGIC, None, ALU.subtract))
            for part in (C1, C2, C3):
                link(dve.scalar_tensor_tensor(ang, kf, -part, ang, ALU.mult, ALU.add))
            link(dve.tensor_scalar(cos2, ang, TWO_PI / 4, None, ALU.add))
            link(dve.tensor_scalar(kf, cos2, TWO_PI / 2, -TWO_PI, ALU.is_gt, ALU.mult))
            link(dve.tensor_tensor(cos2, cos2, kf, ALU.add))
            link(dve.tensor_scalar(cos2, cos2, 3.1415925, -3.1415925, ALU.min, ALU.max))
            dve.tensor_scalar(sin2, ang, 3.1415925, -3.1415925, ALU.min, ALU.max).then_inc(trig_ready, 1)

            def modulation(l):
                dve.wait_ge(mod_mm, 12 * (l + 1))
                if l:
                    dve.wait_ge(x2_ready, NTM)
                bias = pc("mod_b", 48 * l, 48).unsqueeze(2).broadcast_to([P, 48, 2])
                link(dve.tensor_tensor(modv[:, :, :], ps[:, 6, 0:96].rearrange("p (m c) -> p m c", c=2), bias, ALU.add))
                for n, (dst, at) in enumerate(((scale1, 8), (scale2, 32))):
                    g = pc(("ln1_g", "ln2_g")[n], KC * l, KC).unsqueeze(2).broadcast_to([P, KC, 2])
                    ins = dve.scalar_tensor_tensor(dst[:, :, :], modv[:, at:at + KC, :], 1.0, g, ALU.add, ALU.mult)
                ins.then_inc(mod_ready, 1)

            def qk_norm(g, c, w, gain):
                r = sqb[:, 2 + g % 2, :]
                dve.wait_ge(qstd_ready, g + 1)
                link(dve.reciprocal(r[:, 0:w], r[:, 0:w]))
                dve.scalar_tensor_tensor(qk[:, c, 0:w], qk[:, c, 0:w], gain, r[:, 0:w], ALU.mult, ALU.mult).then_inc(qn_ready, 1)
                dve.wait_ge(qn_ready, g + 1)
                dve.wait_ge(rot_mm, g + 1)
                dve.tensor_tensor(r[:, 0:NX], ps[:, 6, 0:NX], cc("sin"), ALU.mult)
                link(dve.tensor_tensor(qk[:, c, 0:NX], qk[:, c, 0:NX], cc("cos"), ALU.mult))
                dve.tensor_tensor(qk[:, c, 0:NX], qk[:, c, 0:NX], r[:, 0:NX], ALU.add).then_inc(rope_ready, 1)

            def conv_taps():
                for c0 in (0, 2):
                    for t in range(TAPS):
                        for c in (c0, c0 + 1):
                            acc, src = g2(cat[:, 4 + c, :]), gpad[:, c, :, t:t + NX]
                            w = pc("conv_w", c * TAPS + t, 1)
                            if t == 0:
                                ins = dve.tensor_scalar(acc, src, w, pc("conv_b", c, 1), ALU.mult, ALU.add)
                            else:
                                ins = dve.scalar_tensor_tensor(acc, src, w, acc, ALU.mult, ALU.add)
                            yield ins

            def unit_max(n, u, views, sc):
                dve.wait_ge(sc_mm, n + 1)
                w = views.shape[1]
                return dve.tensor_reduce(mx[:, u, 0:w], views, AX_X, ALU.max), w

            def block1(layer):
                full = layer == 0
                base, g0 = (0, 0) if full else (14, 5)
                w = 512 if full else NX
                norm(2 * layer, True)
                if not full:
                    dve.memset(upad, 0.0).then_inc(setup_done, 1)
                for c in range(QKC):
                    qk_norm(g0 + c, c, 512 if c == QC else w, pc(("qn_a", "qn_c")[layer] if c < QC else ("kn_a", "kn_c")[layer]))
                taps = iter(())
                if full:
                    for c in range(BC):
                        dve.wait_ge(proj_ev, base + 11 + c)
                        g = gpad[:, c, :, HALO:HALO + NX]
                        link(dve.tensor_tensor(g, g, g2(cat[:, 4 + c, :]), ALU.mult))
                    taps = conv_taps()
                else:
                    pool_windows(base)
                units = attention_units(layer)
                for s in range(len(units) + 1):
                    if s < len(units):
                        n, h, kind = units[s]
                        u = n % 2
                        view = ps[:, u, :].rearrange("p (b k) -> p b k", b=2 if kind == 2 else 1)
                        ins, k = unit_max(n, u, view, SC_A)
                        link(ins)
                        if full:
                            dve.tensor_scalar(nb[:, u, 0:k], mx[:, u, 0:k], -SC_A, None, ALU.mult).then_inc(nb_ready, 1)
                        else:
                            link(dve.tensor_scalar(mx[:, u, 0:1], mx[:, u, 0:1], SC_A, pc("sink", h, 1), ALU.mult, ALU.max))
                            dve.tensor_scalar(nb[:, u, 0:1], mx[:, u, 0:1], -1.0, None, ALU.mult).then_inc(nb_ready, 1)
                    if s >= 1:
                        n, h, kind = units[s - 1]
                        u, k = n % 2, 2 if kind == 2 else 1
                        dve.wait_ge(ex_ready, n + 1)
                        if not full:
                            dve.wait_ge(sink_ready, n - 3 * HEADS + 1)
                            link(dve.tensor_tensor(sm[:, u, 0:1], sm[:, u, 0:1], es[:, u, :], ALU.add))
                        link(dve.reciprocal(sm[:, u, 0:k], sm[:, u, 0:k]))
                        for b in range(k):
                            p = prob[:, u, b * (512 // k):(b + 1) * (512 // k)]
                            ins = dve.tensor_scalar(p, p, sm[:, u, b:b + 1], None, ALU.mult)
                        ins.then_inc(pn_ready, 1)
                    for _ in range(6):
                        ins = next(taps, None)
                        if ins is not None:
                            step(ins, 1)
                if full:
                    for ins in taps:
                        step(ins, 1)
                    dve.wait_ge(dchain, chain[0])
                    dve.sem_inc(conv_ready, 1)
                    dve.wait_ge(cmu_mm, 1)
                    for c in range(BC):
                        ins = dve.scalar_tensor_tensor(cat[:, 4 + c, :], ps[:, 6, :], -1.0 / 512, cat[:, 4 + c, :], ALU.mult, ALU.add)
                    ins.then_inc(cd_ready, 1)
                    dve.wait_ge(cstd_ready, 1)
                    link(dve.reciprocal(stdv[:, :], stdv[:, :]))
                    for c in range(BC):
                        dve.tensor_tensor(cat[:, 4 + c, :], cat[:, 4 + c, :], stdv[:, :], ALU.mult).then_inc(cn_ready, 1)
                else:
                    dve.wait_ge(pool_mm, 1)
                    for g in range(BC):
                        ins = dve.tensor_scalar(cat[:, 4 + g, 0:NX], ps[:, 6 + g // 2, (g % 2) * NX:(g % 2) * NX + NX], pc("pool_scale", g, 1), None, ALU.mult)
                    ins.then_inc(px_ready, 1)
                for m in range(KC):
                    dve.wait_ge(out_mm, KC * layer + m + 1)
                    for g in range(TG if full else 1):
                        ins = dve.scalar_tensor_tensor(xT[:, g, m, :], ps[:, m % 4, g * NX:g * NX + NX], modv[:, 16 + m, g:g + 1], xT[:, g, m, :],
                                                       ALU.mult, ALU.add)
                    ins.then_inc(x_ready, 1)
                norm(2 * layer + 1, full)

            def pool_windows(base):
                dve.wait_ge(invcnt_ready, 16)
                for c in range(BC):
                    dve.wait_ge(proj_ev, base + 7 + c)
                    src, lo, hi, half = upad[:, c, :], 0, UP, 0
                    for lev in range(c + 1):
                        dst = pwin[:, lev % 2, :]
                        d = max(half, 1)
                        left = half if lev else 1
                        right = half
                        a, b = lo + left, hi - right
                        link(dve.tensor_tensor(dst[:, a:b], src[:, a - left:b - left], src[:, a + right:b + right], ALU.add))
                        src, lo, hi = dst, a, b
                        half = 2 * half if lev else 1
                    link(dve.tensor_tensor(pt_pool[:, c, :], src[:, PPAD:PPAD + NX], invcnt[:, c, :], ALU.mult))
                    dve.tensor_tensor(pt_pool[:, c, :], pt_pool[:, c, :], upad[:, c, PPAD:PPAD + NX], ALU.subtract).then_inc(pool_ready, 1)

            def experts(l):
                nt = NTM if l == 0 else QT
                sems = moe[l]
                dve.wait_ge(rt_mm, l + 1)
                link(dve.memset(lgp, -3e38))
                b = pc("rt_b", l * RL, RL).unsqueeze(1).broadcast_to([P, nt, RL])
                link(dve.tensor_tensor(lg[:, 0:nt, :], ps[:, 0, 0:nt * RL].rearrange("p (n r) -> p n r", n=nt), b, ALU.add))
                link(dve.tensor_copy(lgp[:, 0:nt, 0:NG], lg[:, 0:nt, 0:NG]))
                for n in range(nt):
                    link(dve.max(gm8[:, n, :], lgp[:, n, :]))
                    link(dve.max_index(gi8[:, n, :], gm8[:, n, :], lgp[:, n, :]))
                link(dve.tensor_copy(rsc[:, 4, 0:nt], gi8[:, 0:nt, 0]))
                for n in range(nt):
                    link(dve.tensor_scalar(pen[:, n, :], iota[:, 0:NG], rsc[:, 4, n:n + 1], NEG, ALU.not_equal, ALU.mult))
                    e = lg[:, n, NG:RL].rearrange("p (g e) -> p g e", g=NG)
                    link(dve.tensor_tensor(e, e, pen[:, n, :].unsqueeze(2).broadcast_to([P, NG, NE // NG]), ALU.add))
                    link(dve.max(em8[:, n, :], lg[:, n, NG:RL]))
                    link(dve.max_index(ei8[:, n, :], em8[:, n, :], lg[:, n, NG:RL]))
                link(dve.tensor_scalar(rsc[:, 0, 0:nt], gm8[:, 0:nt, 0], -1.0, None, ALU.mult))
                for k in range(2):
                    link(dve.tensor_copy(rsc[:, 5 + k, 0:nt], ei8[:, 0:nt, k]))
                dve.tensor_tensor(rsc[:, 2, 0:nt], em8[:, 0:nt, 1], em8[:, 0:nt, 0], ALU.subtract).then_inc(gmax_ready, 1)
                for k in range(2):
                    for n in range(nt):
                        link(dve.tensor_scalar(M1[:, k, n * NE:(n + 1) * NE], iota[:, 0:NE], rsc[:, 5 + k, n:n + 1], None, ALU.is_equal))
                dve.tensor_tensor(M1[:, 2, 0:nt * NE], M1[:, 0, 0:nt * NE], M1[:, 1, 0:nt * NE], ALU.add).then_inc(m_ready, 1)
                dve.wait_ge(gexp_ready, l + 1)
                link(dve.scalar_tensor_tensor(rsc[:, 8, 0:nt], rsc[:, 3, 0:nt], 1.0, rsc[:, 1, 0:nt], ALU.add, ALU.mult))
                link(dve.reciprocal(wts[:, 0:nt, 0], rsc[:, 8, 0:nt]))
                link(dve.tensor_tensor(wts[:, 0:nt, 1], wts[:, 0:nt, 0], rsc[:, 3, 0:nt], ALU.mult))
                dve.wait_ge(pos_mm, l + 1)
                cnt = ps[:, 1, nt * NE:(nt + 1) * NE]
                link(dve.tensor_scalar(cum[:, 0, :], cnt, 0.0, None, ALU.is_gt))
                for q in range(1, nt * P // SLOTS):
                    link(dve.scalar_tensor_tensor(cum[:, 0, :], cnt, float(SLOTS * q), cum[:, 0, :], ALU.is_gt, ALU.add))
                cur = cum[:, 0, :]
                for q in range(5):
                    nxt, s = cum[:, 1 + q % 2, :], 1 << q
                    link(dve.tensor_copy(nxt[:, 0:s], cur[:, 0:s]))
                    link(dve.tensor_tensor(nxt[:, s:NE], cur[:, s:NE], cur[:, 0:NE - s], ALU.add))
                    cur = nxt
                link(dve.tensor_tensor(cum[:, 3, :], cur, cum[:, 0, :], ALU.subtract))
                for n in range(nt):
                    link(dve.scalar_tensor_tensor(lg[:, n, 0:NE], cum[:, 3, :], float(SLOTS), ps[:, 1, n * NE:(n + 1) * NE], ALU.mult, ALU.add))
                for k in range(2):
                    mk = M1[:, k, 0:nt * NE].rearrange("p (n e) -> p n e", n=nt)
                    link(dve.tensor_tensor(mk, mk, lg[:, 0:nt, 0:NE], ALU.mult))
                    link(dve.tensor_reduce(slotf[:, 0:nt, k], mk, AX_X, ALU.add))
                link(dve.tensor_copy(sloti[:, 0:2 * nt].rearrange("p (n k) -> p n k", k=2), slotf[:, 0:nt, :]))
                ends = cur[0:1, :].unsqueeze(1).broadcast_to([1, MAXB, NE])
                blocks = iota[0:1, 0:MAXB].unsqueeze(2).broadcast_to([1, MAXB, NE])
                link(dve.tensor_tensor(blk_cmp, ends, blocks, ALU.is_le))
                link(dve.tensor_reduce(blkf[0:1, 0:MAXB], blk_cmp, AX_X, ALU.add))
                link(dve.tensor_scalar(blkf[0:1, 0:MAXB], blkf[0:1, 0:MAXB], float(NE - 1), None, ALU.min))
                link(dve.tensor_scalar(blkf[0:1, MAXB:MAXB + 1], cur[0:1, NE - 1:NE], 0.5, None, ALU.mult))
                link(dve.tensor_scalar(blk_cmp[:, 0, 0:MAXB // 2], iota[0:1, 0:MAXB // 2], blkf[0:1, MAXB:MAXB + 1], None, ALU.is_lt))
                link(dve.tensor_reduce(blkf[0:1, MAXB + 1:MAXB + 2], blk_cmp[:, 0, 0:MAXB // 2], AX_X, ALU.add))
                link(dve.tensor_copy(blki[0:1, MAXB:MAXB + 1], blkf[0:1, MAXB + 1:MAXB + 2]))
                link(dve.tensor_scalar(blkf[0:1, MAXB + 1:MAXB + 2], blkf[0:1, MAXB + 1:MAXB + 2], -1.0, float(MAXB // 2 + 1), ALU.mult, ALU.add))
                link(dve.tensor_copy(blki[0:1, MAXB + 1:MAXB + 2], blkf[0:1, MAXB + 1:MAXB + 2]))
                dve.tensor_copy(blki[0:1, 0:MAXB], blkf[0:1, 0:MAXB]).then_inc(plan_ready, 1)
                dve.wait_ge(plan_ready, l + 1)
                pairs = dve.value_load(blki[0:1, MAXB:MAXB + 1], min_val=1, max_val=MAXB // 2)

                def build(count):
                    for n in range(nt):
                        dve.tensor_scalar(sel[:, 0, n, :], iota, slotf[:, n, 0:1], None, ALU.is_equal).then_inc(sems["moe_chain"], 1)
                    dve.wait_ge(sems["moe_chain"], count + nt)
                    for n in range(nt):
                        dve.scalar_tensor_tensor(sel[:, 0, n, :], iota, slotf[:, n, 1:2], sel[:, 0, n, :], ALU.is_equal, ALU.add).then_inc(
                            sems["moe_chain"], 1)
                    dve.wait_ge(sems["moe_chain"], count + 2 * nt)
                    dve.tensor_scalar(slotf[:, 0:nt, :], slotf[:, 0:nt, :], float(PAIR), None, ALU.subtract).then_inc(sems["sel_ready"], 1)

                build(0)
                dve.wait_ge(sems["sel_ready"], 1)
                with dve.Fori(0, pairs) as i:
                    for u in range(2):
                        dve.wait_ge(sems["sg_ready"], 2 * i + u + 1)
                        dve.wait_ge(sems["y_mm"], 2 * i + u + 1)
                        dve.tensor_tensor(hid[:, u, :, :].rearrange("p m s -> p (m s)"), silu_g[:, u, :], ps[:, 2 + u, EC * SLOTS:2 * EC * SLOTS],
                                          ALU.mult).then_inc(sems["hid_ready"], 1)
                    dve.wait_ge(sems["xg_mm"], 2 * i + 2)
                    dve.wait_ge(sems["sel_ready"], i + 1)
                    build(2 * nt + 2 * nt * i)
                dve.wait_ge(sems["sel_ready"], pairs + 1)
                dve.sem_inc(sel_over, 1)
                for n in range(nt + 1):
                    if n < nt:
                        dve.wait_ge(yg_in[l][n], 32)
                        link(dve.tensor_scalar(yg[:, n, 0, :], yg[:, n, 0, :], wts[:, n, 0:1], None, ALU.mult))
                        dve.scalar_tensor_tensor(yg[:, n, 0, :], yg[:, n, 1, :], wts[:, n, 1:2], yg[:, n, 0, :], ALU.mult, ALU.add).then_inc(mix_ready, 1)
                    if n >= 1:
                        m, t = n - 1, (0, NTM)[l] + n - 1
                        dve.wait_ge(yt_mm, t + 1)
                        for k in range(KC):
                            x = xT[:, m // 2, k, (m % 2) * P:(m % 2) * P + P]
                            ins = dve.scalar_tensor_tensor(x, ps[:, 2 * (m % 2) + k // 4, (k % 4) * P:(k % 4 + 1) * P], modv[:, 40 + k, m // 2:m // 2 + 1], x,
                                                           ALU.mult, ALU.add)
                        ins.then_inc(x2_ready, 1)

            modulation(0)
            block1(0)
            experts(0)
            modulation(1)
            block1(1)
            experts(1)
            dve.wait_ge(x2_ready, 6)
            dve.sem_inc(xo_ready, 1)

            def layer2(i):
                call = 4 + 2 * i
                chain2 = [0]

                def link2(ins):
                    chain2[0] += 1
                    ins.then_inc(d2chain, 1)
                    dve.wait_ge(d2chain, LINKS2 * i + chain2[0])

                norm(call, False)
                for c in range(6):
                    dve.wait_ge(r2_mm, 10 * i + c // 2 * 2 + 2)
                    t = sqb[:, 3, (c % 2) * NX:(c % 2) * NX + NX]
                    src, dst = (qp[:, c, :], qr[:, c, :]) if c < 4 else (kv[:, c - 3, :], kv[:, c - 3, :])
                    dve.tensor_tensor(t, ps[:, 4 + c // 2, (c % 2) * NX:(c % 2) * NX + NX], sin2, ALU.mult)
                    link2(dve.tensor_tensor(dst, src, cos2, ALU.mult))
                    dve.tensor_tensor(dst, dst, t, ALU.add).then_inc(r2_ready, 1)
                for v in range(2):
                    dve.wait_ge(r2_mm, 10 * i + 8)
                    dve.tensor_copy(win[:, v, :, NCMP], lp("pe", v * (CB // 2), CB // 2))
                    for o in range(2):
                        rows_ = ps[o * DH:o * DH + DH, 4, v * NX:v * NX + NX].rearrange("p (c j o) -> p j c o", j=8, o=2)
                        for jh in range(2):
                            ins = dve.tensor_copy(win[o * DH:o * DH + DH, v, 8 * jh:8 * jh + 8, 0:NCMP], rows_[:, :, jh:jh + NCMP, o])
                    ins.then_inc(r2_ready, 1)
                for c in range(2):
                    dve.wait_ge(r2_mm, 10 * i + 10)
                    dve.tensor_copy(kdup[:, c, :], ps[:, 5, c * NX:c * NX + NX]).then_inc(r2_ready, 1)
                dve.wait_ge(cmp_mm, 3 * i + 3)
                dve.tensor_copy(kcmp[:, :], ps[:, 4, 0:NCMP])
                for hh in range(4):
                    ins = dve.tensor_copy(vblk[32 * hh:32 * hh + NCMP, hh, :], ps[32 * hh:32 * hh + NCMP, 4, 64:128])
                ins.then_inc(cev_ready, 1)
                dve.wait_ge(cs_mm, i + 1)
                maskc = cc("maskc").rearrange("p (q c) -> p q c", q=QT)
                visc = cc("visc").rearrange("p (q c) -> p q c", q=QT)
                rows_c = scmp.rearrange("p q h c -> p (q h) c")
                for q in range(QT):
                    for o in range(2):
                        link2(dve.tensor_tensor(scmp[:, q, o:HEADS:2, :],
                                                ps[:, 5 + o, q * 64:q * 64 + 64].rearrange("p (h c) -> p h c", h=HEADS // 2)[:, :, 0:NCMP],
                                                maskc[:, q, :].unsqueeze(1).broadcast_to([P, HEADS // 2, NCMP]), ALU.add))
                link2(dve.tensor_reduce(cst[:, 0, :], rows_c, AX_X, ALU.max))
                dve.tensor_tensor(rows_c, rows_c, cst[:, 0, :].unsqueeze(2).broadcast_to([P, QT * HEADS, NCMP]), ALU.subtract).then_inc(pcn_ready, 1)
                dve.wait_ge(pce_ready, i + 1)
                link2(dve.tensor_reduce(cst[:, 1, :], rows_c, AX_X, ALU.add))
                link2(dve.reciprocal(cst[:, 1, :], cst[:, 1, :]))
                link2(dve.tensor_tensor(cst[:, 2, :].rearrange("p (q h) -> p q h", q=QT), cst[:, 1, :].rearrange("p (q h) -> p q h", q=QT),
                                        gates[:, :, :].rearrange("p q (h g) -> p q h g", g=3)[:, :, :, 0], ALU.mult))
                link2(dve.tensor_tensor(rows_c, rows_c, cst[:, 2, :].unsqueeze(2).broadcast_to([P, QT * HEADS, NCMP]), ALU.mult))
                for q in range(QT):
                    ins = dve.tensor_tensor(pcp[:, q, :, 0:NCMP], scmp[:, q, :, :], visc[:, q, :].unsqueeze(1).broadcast_to([P, HEADS, NCMP]), ALU.mult)
                ins.then_inc(pcn_ready, 1)
                dve.wait_ge(sbz_mm, i + 1)
                dve.wait_ge(sb_act, 5 * i + 1)
                masks = mneg[:, :].unsqueeze(1).broadcast_to([P, SBH, P])
                keep = cc("m01").unsqueeze(1).broadcast_to([P, SBH, P])
                dve.tensor_tensor(zs[:, :, 0:P], ps[:, 0:SBH, 0:P], masks, ALU.add)
                dve.tensor_copy(zs[:, :, P:NX], ps[:, 0:SBH, P:NX])
                dve.tensor_tensor(zs[:, :, NX:384], ps[:, 0:SBH, NX:384], masks, ALU.add)
                dve.wait_ge(sb_act, 5 * i + 3)
                link2(dve.scalar_tensor_tensor(spl, ps[:, 0:SBH, 0:384], 0.0, spl, ALU.max, ALU.add))
                dve.tensor_tensor(spl[:, :, 0:P], spl[:, :, 0:P], keep, ALU.mult)
                dve.tensor_tensor(spl[:, :, NX:384], spl[:, :, NX:384], keep, ALU.mult).then_inc(sb_dve, 1)
                dve.wait_ge(sbc_mm, i + 1)
                dve.tensor_tensor(zs, zs, ps[:, 4:8, 0:384], ALU.add).then_inc(sb_dve, 1)
                for s in range(2 * HEADS + 1):
                    if s < 2 * HEADS:
                        n, u, k = 40 + 16 * i + s, s % 2, P * (s % 2 + 1)
                        ins, _ = unit_max(n, u, ps[:, u, :].rearrange("p (b k) -> p b k", b=2)[:, :, 0:k], SC_A)
                        link2(ins)
                        dve.tensor_scalar(nb[:, u, :], mx[:, u, :], -SC_A, None, ALU.mult).then_inc(nb_ready, 1)
                    if s >= 1:
                        n, h, u = 40 + 16 * i + s - 1, (s - 1) // 2, (s - 1) % 2
                        k = P * (u + 1)
                        dve.wait_ge(ex_ready, n + 1)
                        link2(dve.reciprocal(sm[:, u, :], sm[:, u, :]))
                        link2(dve.tensor_tensor(sm[:, u, :], sm[:, u, :], gates[:, u, 3 * h + 1:3 * h + 3], ALU.mult))
                        for b in range(2):
                            p = prob[:, u, b * NX:b * NX + k]
                            ins = dve.tensor_scalar(p, p, sm[:, u, b:b + 1], None, ALU.mult)
                        ins.then_inc(pn_ready, 1)
                for m in range(KC):
                    dve.wait_ge(y2_mm, KC * i + m + 1)
                    dve.tensor_tensor(mg[:, m, :], mg[:, m, :], ps[:, m % 4, 0:NX], ALU.mult)
                    link2(dve.tensor_tensor(mg[:, KC + m, :], mg[:, KC + m, :], ps[:, m % 4, NX:512], ALU.mult))
                    dve.tensor_tensor(mixT[:, m, :], mg[:, m, :], mg[:, KC + m, :], ALU.add).then_inc(mix2_ready, 1)

                def out_norm(c):
                    dve.wait_ge(nstd_ready, 2 * i + c + 1)
                    link2(dve.reciprocal(stdv[:, 0:NX], stdv[:, 0:NX]))
                    for k in range(KC):
                        link2(dve.scalar_tensor_tensor(yres[:, k, :], yres[:, k, :], lp("norm_g", (2 * c + 1) * KC + k, 1), stdv[:, 0:NX], ALU.mult, ALU.mult))
                        dve.tensor_tensor(xT[:, 0, k, :], xT[:, 0, k, :], yres[:, k, :], ALU.add).then_inc(xo_ready, 1)

                out_norm(0)
                norm(call + 1, False)
                for m in range(FF // P):
                    dve.wait_ge(f1_ev, 32 * i + m + 1)
                    r = sqb[:, m % 4, 0:NX]
                    dve.tensor_tensor(ffh[:, m, :], r, r, ALU.mult).then_inc(ffh_ready, 1)
                out_norm(1)
                assert chain2[0] == LINKS2, chain2[0]

            with dve.Fori(0, 2) as i:
                layer2(i)

        @block.gpsimd
        def _(pool):
            pool.wait_ge(plan_ready, 1)
            pool.memset(zrows, 0.0).then_inc(zrows_ready, 1)
            pairs = pool.value_load(blki[0:1, MAXB:MAXB + 1], min_val=1, max_val=MAXB // 2)
            pool.wait_ge(zrows_ready, 1)
            with pool.Fori(pairs, MAXB // 2 + 1) as i:
                pool.dma_start(y_rows[bass.ds(i * PAIR, PAIR), :], zrows).then_inc(tail_stored, 16)
            tail = pool.value_load(blki[0:1, MAXB + 1:MAXB + 2], min_val=1, max_val=MAXB // 2)
            pool.wait_ge(tail_stored, 16 * tail)
            pool.sem_inc(zrows_ready, 1)
            for l in range(2):
                pool.wait_ge(stored_all, l + 1)
                pool.wait_ge(sel_over, l + 1)
                for n in range(NTM if l == 0 else QT):
                    for k in range(2):
                        pool.indirect_dma_start(out=yg[:, n, k, :], out_offset=None, in_=y_rows,
                                                in_offset=bass.IndirectOffsetOnAxis(ap=sloti[:, 2 * n + k:2 * n + k + 1], axis=0)).then_inc(yg_in[l][n], 16)


def constants():
    import numpy as np

    p, f = np.arange(P)[:, None], np.arange(P)[None, :]
    t = {}
    t["ident"] = p == f
    t["headones"] = p // DH == f // DH
    half = DH // 2
    rot = np.zeros((P, P), np.float32)
    rot_b = np.zeros((P, P), np.float32)
    for m in range(P):
        d = m % DH
        if d < half:
            rot[m + half, m] = -1
        else:
            rot[m - half, m] = 1
        if d < 8:
            rot_b[m + 8, m] = -1
        elif d < 16:
            rot_b[m - 8, m] = 1
    t["rot_a"], t["rot_b"] = rot, rot_b
    t["swap"] = (p + DH) % P == f
    t["dup0"] = p == f % DH
    t["dup1"] = p == DH + f % DH
    t["tri_strict"] = p < f
    t["negtri"] = -(p >= f).astype(np.float32)
    t["trineg"] = np.where(f > p, NEG, 0.0)
    t["band1"] = np.where(f < p, NEG, 0.0)
    t["m01"] = p < f
    t["iota"] = np.broadcast_to(f, (P, P))
    tok = np.arange(NX)
    inv = np.float32(10000.0) ** (-np.arange(DH // 4, dtype=np.float32) / np.float32(DH // 4))
    ang = np.concatenate([(tok // 64).astype(np.float32)[:, None] * inv, (tok % 64).astype(np.float32)[:, None] * inv], axis=1)
    t["cos"] = np.cos(ang).T[np.arange(P) % half]
    t["sin"] = np.sin(ang).T[np.arange(P) % half]
    c, q = np.arange(NCMP)[None, None, :], np.arange(QT)[None, :, None]
    vis = CS * c + CB - 1 <= q * P + np.arange(P)[:, None, None]
    t["maskc"] = np.where(vis, 0.0, NEG).reshape(P, -1)
    t["visc"] = vis.reshape(P, -1)
    d = np.arange(P) % DH
    inv2 = np.power(np.float32(500000.0), np.arange(8, dtype=np.float32) * np.float32(-2.0 / 16))
    t["invf"] = np.where(d < 16, inv2[d % 8], 0.0)[:, None]
    t["eps"] = np.full((P, 1), EPS)
    return np.concatenate([np.asarray(t[n], np.float32).reshape(P, w) for n, w in CONSTS], axis=1)


def window_lengths():
    import numpy as np

    t = np.arange(NX)
    inv = [1.0 / (np.clip(t - w // 2 + w, 0, NX) - np.clip(t - w // 2, 0, NX)).astype(np.float32) for w in POOLS]
    return np.ascontiguousarray(np.broadcast_to(np.stack(inv)[None], (P, BC, NX)), np.float32)


def kernel(**inputs):
    import numpy as np
    import concourse.bacc as bacc
    from concourse.bass_utils import run_bass_kernel_spmd

    a = {k: np.asarray(v) for k, v in inputs.items()}

    def cols(v):
        v = v.reshape(-1, v.shape[-1] // P, P)
        return v.transpose(2, 0, 1).reshape(P, -1)

    def fill(v):
        return np.broadcast_to(v.reshape(1, -1), (P, v.size))

    cond = np.stack([a["c"][0], a["c_ctx"]])
    head = lambda v: np.tile(v[0], 2).reshape(P, 1)
    rt_w = np.concatenate([a["rt_grp_w"], a["rt_exp_w"]], axis=2)
    small = {
        "cond": cond.reshape(2, KC, P).transpose(2, 1, 0).reshape(P, -1),
        "mod_b": cols(a["mod_b"]), "ln1_g": cols(a["ln1_g"]), "ln2_g": cols(a["ln2_g"]),
        "qn_a": head(a["q_norm_a"]), "kn_a": head(a["k_norm_a"]), "qn_c": head(a["q_norm_c"]), "kn_c": head(a["k_norm_c"]),
        "conv_w": a["conv_w"][0].reshape(TAPS, BC, P).transpose(2, 1, 0).reshape(P, -1),
        "conv_b": cols(a["conv_b"]), "cln_g": cols(a["conv_ln_g"]), "cln_b": cols(a["conv_ln_b"]),
        "sink": fill(a["sink_c"]), "pool_scale": cols(a["pool_scale"]),
        "rt_w": rt_w.reshape(2, KC, P, RL).transpose(2, 0, 1, 3).reshape(P, -1),
        "rt_b": fill(np.concatenate([a["rt_grp_b"], a["rt_exp_b"]], axis=1)),
    }
    params = np.concatenate([small[n].reshape(P, w) for n, w in PARAMS], axis=1)
    layer = {
        "norm_g": a["norm_g_2"].reshape(2, 4 * KC, P).transpose(0, 2, 1),
        "pe": a["cmp_pe_2"].reshape(2, 2, CB // 2, P).transpose(0, 3, 1, 2).reshape(2, P, -1),
        "w2": a["cmp_w2_2"].reshape(2, 2, 2, P, DH).transpose(0, 3, 1, 2, 4).reshape(2, P, -1),
    }
    lparams = np.concatenate([layer[n] for n, _ in LPARAMS], axis=2)
    x_in = np.stack([a["x"][0], a["ctx"][0]]).reshape(TG, NX, KC, P).transpose(3, 0, 2, 1)
    arrays = {
        "x_in": x_in, "params": params, "consts": constants(), "invcnt": window_lengths(), "lparams": lparams,
        "pos": np.broadcast_to(a["positions_2"].astype(np.int32), (P, NX)), "mod_w": a["mod_w"],
        "w_in_ab": a["w_in_ab"][0], "w_out_ab": a["w_out_ab"][0], "w_in_cd": a["w_in_cd"][0], "w_out_cd": a["w_out_cd"][0],
        "pool_w": a["pool_w"][0], "ex_gate": a["ex_gate"], "ex_up": a["ex_up"], "ex_down": a["ex_down"], "w_in_2": a["w_in_2"],
        "cmp_w1": a["cmp_w1_2"], "w_nsa_o": a["w_nsa_o_2"], "w_sb_o": a["w_sb_o_2"], "w_out_2": a["w_out_2"],
        "w_ff1": a["w_ff1_2"], "w_ff2": a["w_ff2_2"],
    }
    arrays = {f"in_{n}": np.ascontiguousarray(v) for n, v in arrays.items()}
    nc = bacc.Bacc("TRN2", target_bir_lowering=False, num_devices=1, dynamic_dma_scratch_size=8192)
    args = [nc.dram_tensor(n, v.shape, mybir.dt.from_np(v.dtype), kind="ExternalInput").ap() for n, v in arrays.items()]
    out = nc.dram_tensor("out_T", (P, KC, NX), F32, kind="ExternalOutput").ap()
    y_rows = nc.dram_tensor("y_rows", (MAXB * SLOTS + PAIR, D), F32, kind="Internal").ap()
    hybrid_program(nc, *args, out, y_rows)
    got = run_bass_kernel_spmd(nc, [arrays], core_ids=[0]).results[0]["out_T"]
    return np.asarray(got).transpose(2, 1, 0).reshape(1, NX, D)
```

```python
from contextlib import ExitStack

import concourse.bass as bass
from concourse import mybir

F32 = mybir.dt.float32
FR = mybir.dt.float32r
I32 = mybir.dt.int32
U32 = mybir.dt.uint32
ALU = mybir.AluOpType
ACT = mybir.ActivationFunctionType
AX_X = mybir.AxisListType.X

P = 128
D = 1024
KC = D // P
NX = 256
TG = 2
QT = NX // P
EPS = 1e-6
NEG = -1e30

HEADS = 8
DH = 64
SC_A = DH ** -0.5
QC = HEADS * DH // P
QKC = QC + 1
TAPS = 31
HALO = TAPS // 2
BC = 4
POOLS = (2, 4, 8, 16)
PPAD = 8
NG, NE, DE = 4, 32, 512
EC = DE // P
RL = NG + NE
SLOTS = 64
PAIR = 2 * SLOTS
MAXB = 48

CB, CS = 32, 16
NCMP = (NX - CB) // CS + 1
CPAD = 32
SBH, SBD = 4, 128
SC_B = SBD ** -0.5
FF = 4 * D
IN_W = 512 + 6 * 64 + 24 + 3 * 512 + 2 * D
COL_SB = 512 + 6 * 64 + 24
COL_MG = COL_SB + 3 * 512
TWO_PI = 6.283185307179586
C1 = 6.28125
C2 = 0.0019350051879882812
C3 = TWO_PI - C1 - C2
LINKS2 = 157
MAGIC = 12582912.0

PARAMS = [("cond", 2 * KC), ("mod_b", 2 * 48), ("ln1_g", 2 * KC), ("ln2_g", 2 * KC), ("qn_a", 1), ("kn_a", 1),
          ("conv_w", BC * TAPS), ("conv_b", BC), ("cln_g", BC), ("cln_b", BC), ("qn_c", 1), ("kn_c", 1),
          ("sink", HEADS), ("pool_scale", BC), ("rt_w", 2 * KC * RL), ("rt_b", 2 * RL)]
CONSTS = [("ident", P), ("headones", P), ("rot_a", P), ("swap", P), ("rot_b", P), ("dup0", P), ("dup1", P),
          ("tri_strict", P), ("negtri", P), ("trineg", P), ("band1", P), ("m01", P), ("iota", P),
          ("cos", NX), ("sin", NX), ("maskc", QT * NCMP), ("visc", QT * NCMP), ("invf", 1), ("eps", 1), ("fold", 16)]
LPARAMS = [("norm_g", 4 * KC), ("pe", 2 * (CB // 2)), ("w2", 2 * 2 * 64)]


def offsets(layout):
    out, at = {}, 0
    for name, n in layout:
        out[name] = (at, n)
        at += n
    return out, at


RING = 6
SLAB = 4096


def hybrid_program(nc, xT_in, params_in, consts_in, invcnt_in, lparams_in, pos_in, mod_w, w_in_ab, w_out_ab, w_in_cd,
                   w_out_cd, pool_w, ex_gate, ex_up, ex_down, w_in_2, cmp_w1, w_nsa_o, w_sb_o, w_out_2, w_ff1, w_ff2,
                   outT, y_rows):
    po, n_par = offsets(PARAMS)
    co, n_con = offsets(CONSTS)
    lo, n_lp = offsets(LPARAMS)
    ctx = ExitStack()
    with ctx:
        address = {}

        def sb(name, shape, dt=F32):
            address[name] = -(-nc.sbuf_base // 32) * 32
            return ctx.enter_context(nc.sbuf_tensor(name, shape, dt))

        def rounded(name, shape, over, column):
            return nc.alloc_sbuf_tensor_at(name, shape, FR, offset=address[over] + 4 * column)

        def sem(name):
            return ctx.enter_context(nc.semaphore(name))

        ring = sb("ring", [P, RING, SLAB])
        xT = sb("xT", [P, TG, KC, NX])
        hT = sb("hT", [P, TG, KC, NX])
        cat = sb("cat", [P, 8, 512])
        sqb = sb("sqb", [P, 4, 512])
        E = sb("E", [P, 9216])
        par = sb("par", [P, n_par])
        con = sb("con", [P, n_con])
        lpar = sb("lpar", [P, n_lp])
        ones = sb("ones", [P, P])
        negones = sb("negones", [P, P])
        mneg = sb("mneg", [P, P])
        stdv = sb("stdv", [P, 512])
        modv = sb("modv", [P, 2, 48, 2])
        scale1 = sb("scale1", [P, 2, KC, 2])
        scale2 = sb("scale2", [P, 2, KC, 2])
        condv = sb("condv", [P, KC, 32])
        mrow = E[:, 6144:6656]
        mx = sb("mx", [P, 2, 2])
        nb = sb("nb", [P, 2, 2])
        sm = sb("sm", [P, 2, 2])
        es = sb("es", [P, 2, 1])
        ps = ctx.enter_context(nc.psum_tensor("ps", [P, 8, 512], F32))

        def pc(name, a=0, n=None):
            at, w = po[name]
            return par[:, at + a:at + (w if n is None else a + n)]

        def cc(name):
            at, w = co[name]
            return con[:, at:at + w]

        def lp(name, a, n):
            at, w = lo[name]
            return lpar[:, at + a:at + a + n]

        lpars = par[:, po["rt_w"][0]:po["rt_w"][0] + 2 * n_lp]
        assert po["rt_w"][0] + 2 * n_lp <= n_par

        ident = cc("ident")

        def e3(at, a, b):
            return E[:, at:at + a * b].rearrange("p (a b) -> p a b", a=a)

        qk = e3(0, QKC, 512)
        kswap = E[:, 2560:3072]
        vtok = e3(3072, 4, P)
        GP = NX + 2 * HALO
        gpad = E[:, 3584:3584 + BC * TG * GP].rearrange("p (c g t) -> p c g t", c=BC, g=TG)
        UP = NX + 2 * PPAD
        upad = e3(3584, BC, UP)
        pwin = e3(3584 + BC * UP, 2, UP)
        pt_pool = e3(3584 + (BC + 2) * UP, BC, NX)
        invcnt = cat[:, 4:8, NX:512]
        prob = e3(7168, 2, 512)
        probT = E[:, 8192:9216].rearrange("p (u b q) -> p u b q", u=2, b=4)
        NTM = 4
        htok = cat[:, :, :].rearrange("p c t -> p (c t)").rearrange("p (n d) -> p n d", n=NTM)
        sel = E[:, 0:NTM * PAIR].rearrange("p (n s) -> p n s", n=NTM)
        xg = E[:, 1024:2048].rearrange("p (k s) -> p k s", k=KC)
        silu_g = E[:, 2048:2048 + DE]
        htmp = E[:, 4096:4096 + DE]
        hid = E[:, 2560:2560 + EC * PAIR].rearrange("p (m s) -> p m s", m=EC)
        yb = E[:, 3072:3072 + D]
        blk_cmp = E[0:1, 1024:1024 + MAXB * NE].rearrange("p (b e) -> p b e", b=MAXB)
        zrows = E[:, 5120:5120 + D]
        yg = E[:, 0:8192].rearrange("p (n k d) -> p n k d", n=NTM, k=2)
        lg = E[:, 8192:8336].rearrange("p (n r) -> p n r", n=NTM)
        lgp = e3(8336, NTM, 8)
        gm8 = e3(8368, NTM, 8)
        em8 = e3(8400, NTM, 8)
        pen = e3(8432, NTM, NG)
        rsc = e3(8448, 12, NTM)
        cum = e3(8496, 4, NE)
        M1 = e3(8624, 3, NTM * NE)
        gi8 = sb("gi8", [P, NTM, 8], U32)
        ei8 = sb("ei8", [P, NTM, 8], U32)
        slotf = sb("slotf", [P, NTM, 2])
        sloti = sb("sloti", [P, NTM * 2], I32)
        wts = sb("wts", [P, NTM, 2])
        blkf = sb("blkf", [1, MAXB + 2])
        blki = sb("blki", [1, 2 * MAXB + 2], I32)
        NEW = MAXB + 2
        fresh = E[0:1, 2560:2560 + MAXB]
        below = E[:, 2624:2624 + MAXB // 2]
        halves = E[:, 2656:2658]
        iota2 = E[:, 4608:4608 + PAIR]
        qp = xT[:, 1, 0:4, :]
        qr = xT[:, 1, 4:8, :]
        sbq = hT[:, 1, 0:4, :]
        sbk = hT[:, 1, 4:8, :]
        kv = e3(0, 3, NX)
        kdup = e3(768, 2, NX)
        vsw = e3(1280, QT, P)
        win = [E[:, at:at + 512].rearrange("p (j c) -> p j c", j=CB // 2) for at in (1536, 8704)]
        hrow = sqb[:, 0, :]
        sbv = e3(2048, QT, 512)
        mg = e3(3072, 16, NX)
        w_hi = rounded("w_hi", [P, 2, SLAB], "E", 0)
        w_lo = [rounded(f"w_lo{r}", [P, SLAB], "ring", r * SLAB) for r in range(RING)]
        hn_hi = rounded("hn_hi", [P, KC, NX], "hT", KC * NX)
        hn_lo = rounded("hn_lo", [P, KC, NX], "hT", 0)
        ff_hi = rounded("ff_hi", [P, 8, NX], "xT", KC * NX)
        ff_lo = rounded("ff_lo", [P, 8, NX], "cat", 4 * 512)
        onsa = cat[:, 0:2, :].rearrange("p a (b t) -> p (a b) t", b=2)
        osb = cat[:, 2:4, :].rearrange("p a (b t) -> p (a b) t", b=2)
        mixT = cat[:, 4:8, :].rearrange("p a (b t) -> p (a b) t", b=2)
        trig = sb("trig", [P, 2, NX])
        cos2, sin2 = trig[:, 0, :], trig[:, 1, :]
        gates = sb("gates", [P, QT, 24])
        hcmp = sb("hcmp", [P, 4, 16])
        gcmp = sb("gcmp", [P, 4, NCMP])
        kcmp = sb("kcmp", [P, NCMP])
        vblk = sb("vblk", [P, 4, 64])
        pcp = sb("pcp", [P, QT, HEADS, CPAD])
        scmp = sqb[:, 2, 0:QT * HEADS * NCMP].rearrange("p (q h c) -> p q h c", q=QT, h=HEADS)
        pcT = sqb[:, 1, :].rearrange("p (b q) -> p b q", b=4)
        zs = E[:, 7168:7168 + SBH * 384].rearrange("p (h c) -> p h c", h=SBH)
        spl = cat[:, 4:7, :].rearrange("p a b -> p (a b)").rearrange("p (h c) -> p h c", h=SBH)
        yres = cat[:, 0:4, :].rearrange("p a (b t) -> p (a b) t", b=2)
        cst = sb("cst", [P, 3, QT * HEADS])

        inputs_in = sem("inputs_in")
        slab_in = [sem(f"slab_in{r}") for r in range(RING)]
        setup_done = sem("setup_done")
        cond_ready = sem("cond_ready")
        mod_mm = sem("mod_mm")
        mod_ev = sem("mod_ev")
        mod_fold = sem("mod_fold")
        mod_ready = sem("mod_ready")
        sq_ready = sem("sq_ready")
        ssq_mm = sem("ssq_mm")
        std_ready = sem("std_ready")
        rstd_ready = sem("rstd_ready")
        xn_ready = sem("xn_ready")
        h_ready = sem("h_ready")
        proj_mm = sem("proj_mm")
        proj_ev = sem("proj_ev")
        qsq_ready = sem("qsq_ready")
        qss_mm = sem("qss_mm")
        qstd_ready = sem("qstd_ready")
        qn_ready = sem("qn_ready")
        rot_mm = sem("rot_mm")
        rope_ready = sem("rope_ready")
        swap_mm = sem("swap_mm")
        swap_ev = sem("swap_ev")
        sc_mm = sem("sc_mm")
        nb_ready = sem("nb_ready")
        ex_ready = sem("ex_ready")
        pn_ready = sem("pn_ready")
        tr_mm = sem("tr_mm")
        pt_ready = sem("pt_ready")
        pv_mm = sem("pv_mm")
        o_ready = sem("o_ready")
        sink_ready = sem("sink_ready")
        glu_ready = sem("glu_ready")
        conv_ready = sem("conv_ready")
        cmu_mm = sem("cmu_mm")
        cd_ready = sem("cd_ready")
        csq_ready = sem("csq_ready")
        cvar_mm = sem("cvar_mm")
        cstd_ready = sem("cstd_ready")
        cn_ready = sem("cn_ready")
        bx_ready = sem("bx_ready")
        pool_ready = sem("pool_ready")
        pool_mm = sem("pool_mm")
        px_ready = sem("px_ready")
        invcnt_ready = sem("invcnt_ready")
        out_mm = sem("out_mm")
        x_ready = sem("x_ready")
        dchain = sem("dve_chain")
        achain = sem("act_chain")
        rt_mm = sem("rt_mm")
        ht_mm = sem("ht_mm")
        ht_ev = sem("ht_ev")
        gmax_ready = sem("gmax_ready")
        gexp_ready = sem("gexp_ready")
        m_ready = sem("m_ready")
        pos_mm = sem("pos_mm")
        plan_ready = sem("plan_ready")
        moe = []
        for l in range(2):
            moe.append({n: sem(f"{n}_{l}") for n in (
                "sel_ready", "xg_mm", "xg_ready", "gu_mm", "sg_ready", "hid_ready", "hidt_mm", "hidt_ready", "y_mm", "y_ready",
                "y_stored", "moe_chain")})
            moe[l]["w_in"] = [sem(f"w_in{r}_{l}") for r in range(RING)]
        stored_all = sem("stored_all")
        yg_in = [[sem(f"yg_in{l}{n}") for n in range(NTM if l == 0 else QT)] for l in range(2)]
        zrows_ready = sem("zrows_ready")
        tail_stored = sem("tail_stored")
        sel_over = sem("sel_over")
        mix_ready = sem("mix_ready")
        yt_mm = sem("yt_mm")
        x2_ready = sem("x2_ready")
        trig_done = sem("trig_done")
        trig_ready = sem("trig_ready")
        lpars_in = sem("lpars_in")
        p2_mm = sem("p2_mm")
        p2_ev = sem("p2_ev")
        r2_mm = sem("r2_mm")
        r2_ready = sem("r2_ready")
        cmp_mm = sem("cmp_mm")
        cmp_ready = sem("cmp_ready")
        gel_ready = sem("gel_ready")
        cev_ready = sem("cev_ready")
        pct_mm = sem("pct_mm")
        pct_ready = sem("pct_ready")
        cs_mm = sem("cs_mm")
        pcn_ready = sem("pcn_ready")
        pce_ready = sem("pce_ready")
        sbz_mm = sem("sbz_mm")
        sb_act = sem("sb_act")
        sb_dve = sem("sb_dve")
        sbc_mm = sem("sbc_mm")
        sbo_mm = sem("sbo_mm")
        y2_mm = sem("y2_mm")
        mgs_ready = sem("mgs_ready")
        mix2_ready = sem("mix2_ready")
        wo_mm = sem("wo_mm")
        wo_ev = sem("wo_ev")
        nsq_ready = sem("nsq_ready")
        nss_mm = sem("nss_mm")
        nstd_ready = sem("nstd_ready")
        xo_ready = sem("xo_ready")
        d2chain = sem("d2_chain")
        f1_mm = sem("f1_mm")
        f1_ev = sem("f1_ev")
        ffh_ready = sem("ffh_ready")
        ffs_ready = sem("ffs_ready")
        split_ready = sem("split_ready")
        f2_mm = sem("f2_mm")
        out_stored = sem("out_stored")
        spnop = sem("spnop")

        block = ctx.enter_context(nc.Block())
        n_in = 4

        def rows(w, c0, n):
            return w[:, c0:c0 + n].rearrange("(k p) n -> p k n", p=P)

        mod_slabs = [(rows(mod_w[j // 12], j % 12 * 512, 512), (KC, 512), (mod_mm, j + 1)) for j in range(24)]
        MOD0 = 4
        ab_slabs = [(rows(w_in_ab, 0, 512), (KC, 512), (proj_mm, 4)), (rows(w_in_ab, 512, 512), (KC, 512), (proj_mm, 8)),
                    (rows(w_in_ab, 1024, 512), (KC, 512), (proj_mm, 12)), (rows(w_in_ab, 1536, 256), (KC, 256), (proj_mm, 14)),
                    (rows(w_out_ab, 0, 512), (KC, 512), (out_mm, 4)), (rows(w_out_ab, 512, 512), (KC, 512), (out_mm, 8))]
        cd_slabs = [(rows(w_in_cd, 0, 512), (KC, 512), (proj_mm, 18)), (rows(w_in_cd, 512, 512), (KC, 512), (proj_mm, 22)),
                    (rows(w_in_cd, 1024, 256), (KC, 256), (proj_mm, 24)),
                    (pool_w.rearrange("g c d -> c g d"), (BC, P), (pool_mm, 1)),
                    (rows(w_out_cd, 0, 512), (KC, 512), (out_mm, 12)), (rows(w_out_cd, 512, 512), (KC, 512), (out_mm, 16))]
        stream_a = mod_slabs[:MOD0] + ab_slabs[:4] + mod_slabs[MOD0:] + ab_slabs[4:]
        stream_b = cd_slabs
        AB_IN, AB_OUT = MOD0, len(stream_a) - 2

        def mod_at(j):
            return j if j < MOD0 else j + 4
        NA, NB_ = len(stream_a), len(stream_b)
        assert NA % RING == 0 and NB_ % RING == 0
        N2 = 36
        USED2 = 31

        def slab(n, shape):
            k, w = shape
            return ring[:, n % RING, 0:k * w].rearrange("p (k w) -> p k w", k=k)

        def slab2_uses(s):
            return (USED2 - s + RING - 1) // RING

        def slab2_count(i, j):
            s = j % RING
            return i * (16 * slab2_uses(s)) + 16 * ((NA + NB_) // RING + j // RING + 1)

        J_IN, J_CMP, J_MG, J_NSA, J_SB, J_OUT, J_FF = 0, 5, 7, 11, 12, 13, 15
        FF_ORDER = [(1, 0)] + [x for j in range(7) for x in ((1, j + 1), (2, j))] + [(2, 7)]
        FF_OUT = [0, 4, 1, 5, 2, 6, 3, 7]
        P2N, WON = 34, 16

        def ff_used(w, j):
            if w == 1:
                return ((f1_mm, 32, 32 + 4 * j + 4),)
            return ((f2_mm, 7, 7 + j + 1),) if j < 7 else ((wo_mm, WON, WON + 2 * KC),)

        def layer_slabs(i):
            win_ = w_in_2[bass.ds(i, 1), :, :].rearrange("a (k p) n -> p (a k) n", p=P)
            wc = cmp_w1[bass.ds(i, 1), :, :, :].rearrange("a v (j p) n -> p (a v) j n", p=P)
            wn = w_nsa_o[bass.ds(i, 1), :, :].rearrange("a (k p) n -> p (a k) n", p=P)
            ws = w_sb_o[bass.ds(i, 1), :, :].rearrange("a (k p) n -> p (a k) n", p=P)
            wo = w_out_2[bass.ds(i, 1), :, :].rearrange("a (k p) n -> p (a k) n", p=P)
            f1 = w_ff1[bass.ds(i, 1), :, :].rearrange("a (k p) n -> p (a k) n", p=P)
            f2 = w_ff2[bass.ds(i, 1), :, :].rearrange("a (k p) n -> p (a k) n", p=P)
            out = [(win_[:, :, 0:512], (KC, 512), (p2_mm, P2N, 4)), (win_[:, :, 512:COL_SB], (KC, COL_SB - 512), (p2_mm, P2N, 8))]
            out += [(win_[:, :, COL_SB + 512 * j:COL_SB + 512 * j + 512], (KC, 512), (p2_mm, P2N, (12, 16, 18)[j])) for j in range(3)]
            out += [(wc[:, v], (CB // 2, 256), (cmp_mm, 4, v + 1)) for v in range(2)]
            out += [(win_[:, :, COL_MG + 512 * j:COL_MG + 512 * j + 512], (KC, 512), (p2_mm, P2N, 22 + 4 * j)) for j in range(4)]
            out += [(wn, (4, D), (y2_mm, KC, KC)), (ws, (4, D), (y2_mm, KC, KC))]
            out += [(wo[:, :, 512 * j:512 * j + 512], (KC, 512), (wo_mm, WON, WON + 4 * j + 4)) for j in range(2)]
            out += [(f1[:, :, 512 * j:512 * j + 512], (KC, 512)) + ff_used(1, j) if w == 1 else
                    (f2[:, 4 * j:4 * j + 4, :], (4, D)) + ff_used(2, j) for w, j in FF_ORDER]
            assert len(out) == USED2
            return out

        def expert_loads(l, e):
            g = ex_gate[l][bass.ds(e, 1), :, :].rearrange("a (k p) n -> p (a k) n", p=P)
            u = ex_up[l][bass.ds(e, 1), :, :].rearrange("a (k p) n -> p (a k) n", p=P)
            d = ex_down[l][bass.ds(e, 1), :, :].rearrange("a (k p) n -> p (a k) n", p=P)
            return (g, (KC, DE)), (u, (KC, DE)), (d, (EC, D))

        @block.sync
        def _(sp):
            sp.dma_start(con[:, :], consts_in).then_inc(inputs_in, 16)
            sp.dma_start(par[:, :], params_in).then_inc(inputs_in, 16)
            sp.dma_start(xT[:, :, :, :], xT_in).then_inc(inputs_in, 16)
            sp.dma_start(E[:, 0:NX].bitcast(I32), pos_in).then_inc(inputs_in, 16)

            def static_loads(stream, n0):
                for j, (src, shape, _used) in enumerate(stream):
                    n = n0 + j
                    if j >= RING:
                        s, v = stream[j - RING][2]
                        sp.wait_ge(s, v)
                    sp.dma_start(slab(n, shape), src).then_inc(slab_in[n % RING], 16)
                    if stream is stream_b and j == NB_ - 1:
                        sp.wait_ge(h_ready, 3 * KC)
                        sp.dma_start(invcnt, invcnt_in).then_inc(invcnt_ready, 16)

            def expert_stream(l, before):
                sems = moe[l]
                sp.wait_ge(plan_ready, l + 1)
                pairs = sp.value_load(blki[0:1, MAXB:MAXB + 1], min_val=1, max_val=MAXB // 2)
                for s, v in before:
                    sp.wait_ge(s, v)
                with sp.Fori(0, pairs) as i:
                    loads, new = [], []
                    for u in range(2):
                        e = sp.value_load(blki[0:1, bass.ds(u * pairs + i, 1)], min_val=0, max_val=NE - 1)
                        loads.append(expert_loads(l, e))
                        new.append(sp.value_load(blki[0:1, bass.ds(u * pairs + i + NEW, 1)], min_val=0, max_val=1))
                    for w in range(3):
                        if w < 2:
                            sp.wait_ge(sems["gu_mm"], 2 * i + w + 1)
                        else:
                            sp.wait_ge(sems["y_mm"], i + 1)
                        sp.sem_inc(spnop, 1)
                        for u in range(2):
                            src, shape = loads[u][w]
                            with sp.If(new[u] > 0):
                                sp.dma_start(slab(2 * w + u, shape), src).then_inc(sems["w_in"][2 * w + u], 16)
                            with sp.Else():
                                sp.sem_inc(sems["w_in"][2 * w + u], 16)
                sp.wait_ge(sems["gu_mm"], 2 * pairs + 2)
                sp.sem_inc(spnop, 1)
                sp.wait_ge(sems["y_mm"], pairs + 1)
                sp.sem_inc(spnop, 1)

            static_loads(stream_a, 0)
            expert_stream(0, [stream_a[NA - RING + r][2] for r in range(RING)])
            sp.wait_ge(yg_in[0][NTM - 1], 32)
            static_loads(stream_b, NA)
            expert_stream(1, [stream_b[NB_ - RING + r][2] for r in range(RING)])
            sp.wait_ge(yg_in[1][QT - 1], 32)
            sp.dma_start(lpars.rearrange("p (a n) -> p a n", a=2), lparams_in.rearrange("a p n -> p a n")).then_inc(lpars_in, 16)

            with sp.Fori(0, 2) as i:
                slabs = layer_slabs(i)
                for j, (src, shape, _used) in enumerate(slabs):
                    if j < RING:
                        last = USED2 - 1 - (USED2 - 1 - j) % RING
                        s, per, v = slabs[last][2]
                        sp.wait_ge(s, i * per + v - per)
                    else:
                        s, per, v = slabs[j - RING][2]
                        sp.wait_ge(s, i * per + v)
                    sp.sem_inc(spnop, 1)
                    sp.dma_start(slab(j, shape), src).then_inc(slab_in[j % RING], 16)
            sp.wait_ge(xo_ready, 2 * 2 * KC + KC)
            sp.dma_start(outT, xT[:, 0, :, :]).then_inc(out_stored, 16)
            sp.wait_ge(out_stored, 16)

        def g2(row):
            return row.rearrange("p (g t) -> p g t", g=TG)

        def src_of(full, k):
            return xT[:, :, k, :] if full else xT[:, 0, k, :]

        def hsrc(full, k):
            return hT[:, :, k, :] if full else hT[:, 0, k, :]

        def sq_of(full, k):
            return g2(sqb[:, k % 4, :]) if full else sqb[:, k % 4, 0:NX]

        def attention_units(layer):
            if layer == 0:
                return [(3 * h + k, h, k) for h in range(HEADS) for k in range(3)]
            return [(3 * HEADS + 2 * h + k, h, k) for h in range(HEADS) for k in range(2)]

        @block.scalar
        def _(act):
            chain = [0]

            def link(ins):
                chain[0] += 1
                ins.then_inc(achain, 1)
                act.wait_ge(achain, chain[0])

            eps = cc("eps")

            def norm_stats(call, full, ready):
                if not (isinstance(call, int) and call == 0):
                    act.wait_ge(h_ready, call * KC)
                for k in range(KC):
                    ready(k)
                    if k >= 4:
                        act.wait_ge(ssq_mm, call * KC + k - 3)
                    act.activation(sq_of(full, k), src_of(full, k), ACT.Square).then_inc(sq_ready, 1)
                act.wait_ge(ssq_mm, call * KC + KC)
                w = 512 if full else NX
                act.activation(stdv[:, 0:w], ps[:, 7, 0:w], ACT.Sqrt, bias=eps, scale=1.0 / D).then_inc(std_ready, 1)

            def modulate(call, full, scale, shift):
                for k in range(KC):
                    act.wait_ge(xn_ready, call * KC + k + 1)
                    for g in range(TG if full else 1):
                        ins = act.activation(hT[:, g, k, :], hT[:, g, k, :], ACT.Identity, scale=scale(k, g), bias=shift(k, g))
                    ins.then_inc(h_ready, 1)

            def evac(n, dst, src, func=ACT.Copy, **kw):
                act.wait_ge(proj_mm, n + 1)
                act.activation(dst, src, func, **kw).then_inc(proj_ev, 1)

            def qsq(g, c, w):
                act.wait_ge(proj_ev, proj_n["qk"][g])
                if g >= 2:
                    act.wait_ge(qss_mm, g - 1)
                act.activation(sqb[:, g % 2, 0:w], qk[:, c, 0:w], ACT.Square).then_inc(qsq_ready, 1)

            def qstd(g, w):
                act.wait_ge(qss_mm, g + 1)
                if g >= 2:
                    act.wait_ge(rope_ready, g - 1)
                act.activation(sqb[:, 2 + g % 2, 0:w], ps[:, 5, 0:w], ACT.Sqrt, bias=eps, scale=1.0 / DH).then_inc(qstd_ready, 1)

            def attend_exp(n, u, parts, sc):
                act.wait_ge(nb_ready, n + 1)
                for (c0, c1), m in parts:
                    ins = act.activation(prob[:, u, c0:c1], ps[:, u, c0:c1], ACT.Exp, bias=nb[:, u, m:m + 1], scale=sc,
                                         accum_out=sm[:, u, m:m + 1])
                ins.then_inc(ex_ready, 1)

            def attend_pt(n, u, nblk):
                act.wait_ge(tr_mm, n + 1)
                act.activation(probT[:, u, 0:nblk, :], ps[:, 2 + u, 0:nblk * P].rearrange("p (b q) -> p b q", b=nblk),
                               ACT.Copy).then_inc(pt_ready, 1)

            proj_n = {"qk": {}}
            act.wait_ge(inputs_in, 16 * n_in)
            act.wait_ge(setup_done, 1)
            act.activation(condv[:, :, 0:2], pc("cond").rearrange("p (k c) -> p k c", c=2), ACT.Silu).then_inc(cond_ready, 1)

            def trig():
                act.wait_ge(trig_ready, 1)
                act.activation(sin2, sin2, ACT.Sin)
                act.activation(cos2, cos2, ACT.Sin).then_inc(trig_done, 1)

            def block1(layer):
                base, g0 = (0, 0) if layer == 0 else (14, 5)
                full = layer == 0
                if full:
                    norm_stats(0, True, lambda k: None)
                    for j in range(MOD0):
                        act.wait_ge(mod_mm, j + 1)
                        act.activation(mrow, ps[:, 6, :], ACT.Copy).then_inc(mod_ev, 1)
                    trig()
                    act.wait_ge(mod_ready, 1)
                else:
                    act.wait_ge(x2_ready, NTM)
                    norm_stats(2, True, lambda k: None)
                modulate(2 * layer, True, lambda k, g: scale1[:, layer, k, g:g + 1], lambda k, g: modv[:, layer, k, g:g + 1])
                w = 512 if full else NX
                for c in range(QKC):
                    wc = 512 if c == QC else w
                    evac(base + c, qk[:, c, 0:wc], ps[:, c % 4, 0:wc])
                    proj_n["qk"][g0 + c] = base + c + 1
                evac(base + 5, vtok, ps[:, 1, :].rearrange("p (n d) -> p n d", n=4))
                for n in range(8):
                    if n < QKC:
                        qsq(g0 + n, n, 512 if n == QC else w)
                    if full:
                        m = base + 6 + n
                        src = g2(ps[:, (6 + n) % 4, :])
                        if n < BC:
                            act.wait_ge(setup_done, 1)
                            evac(m, gpad[:, n, :, HALO:HALO + NX], src)
                        else:
                            evac(m, g2(cat[:, n, :]), src, ACT.Sigmoid)
                    elif n < BC:
                        act.wait_ge(setup_done, 3)
                        evac(base + 6 + n, upad[:, n, PPAD:PPAD + NX], ps[:, (6 + n) % 4, 0:NX])
                    if n < QKC:
                        qstd(g0 + n, 512 if n == QC else w)
                act.wait_ge(swap_mm, layer + 1)
                act.activation(kswap, ps[:, 6, :], ACT.Copy).then_inc(swap_ev, 1)
                units = attention_units(layer)
                for s in range(len(units) + 1):
                    if s < len(units):
                        n, h, kind = units[s]
                        u = n % 2
                        if n >= 2:
                            act.wait_ge(tr_mm, n - 1)
                        if kind == 2:
                            attend_exp(n, u, [((0, 256), 0), ((256, 512), 1)], SC_A)
                        else:
                            attend_exp(n, u, [((0, 512), 0)], SC_A)
                            if layer == 1:
                                act.activation(es[:, u, :], pc("sink", h, 1), ACT.Exp, bias=nb[:, u, 0:1]).then_inc(sink_ready, 1)
                    if full and 1 <= s <= 24 - MOD0:
                        act.wait_ge(mod_mm, MOD0 + s)
                        act.activation(mrow, ps[:, 6, :], ACT.Copy).then_inc(mod_ev, 1)
                    if s >= 1:
                        n, h, kind = units[s - 1]
                        if n >= 2:
                            act.wait_ge(pv_mm, n - 1)
                        attend_pt(n, n % 2, 4)
                        if s >= 2:
                            head_out(units[s - 2], layer)
                head_out(units[-1], layer)
                if full:
                    act.wait_ge(cd_ready, 1)
                    for c in range(BC):
                        act.activation(sqb[:, c, :], cat[:, 4 + c, :], ACT.Square).then_inc(csq_ready, 1)
                    act.wait_ge(cvar_mm, 1)
                    act.activation(stdv[:, :], ps[:, 5, :], ACT.Sqrt, bias=eps, scale=1.0 / 512).then_inc(cstd_ready, 1)
                    for c in range(BC):
                        act.wait_ge(cn_ready, c + 1)
                        act.activation(cat[:, 4 + c, :], cat[:, 4 + c, :], ACT.Silu, scale=pc("cln_g", c, 1),
                                       bias=pc("cln_b", c, 1)).then_inc(bx_ready, 1)
                norm_stats(2 * layer + 1, full, lambda k: act.wait_ge(x_ready, KC * layer + k + 1))
                act.wait_ge(mod_ready, 2)
                modulate(2 * layer + 1, full, lambda k, g: scale2[:, layer, k, g:g + 1], lambda k, g: modv[:, layer, 24 + k, g:g + 1])

            def head_out(unit, layer):
                n, h, kind = unit
                last = kind == 2 if layer == 0 else kind == 1
                if h % 2 == 1 and last:
                    act.wait_ge(pv_mm, n + 1)
                    w = 512 if layer == 0 else NX
                    act.activation(cat[:, h // 2, 0:w], ps[:, 4 + (h // 2) % 2, 0:w], ACT.Copy).then_inc(o_ready, 1)

            def experts(l):
                nt = NTM if l == 0 else QT
                sems = moe[l]
                for q in range(2 * nt):
                    act.wait_ge(ht_mm, (0, 2 * NTM)[l] + q + 1)
                    act.activation(htok[:, q // 2, (q % 2) * 512:(q % 2) * 512 + 512], ps[:, 4 + q % 3, :], ACT.Copy).then_inc(ht_ev, 1)
                act.wait_ge(gmax_ready, l + 1)
                for n in range(nt):
                    act.activation(pen[:, n, :], lgp[:, n, 0:NG], ACT.Exp, bias=rsc[:, 0, n:n + 1], accum_out=rsc[:, 1, n:n + 1])
                act.activation(rsc[:, 3, 0:nt], rsc[:, 2, 0:nt], ACT.Exp).then_inc(gexp_ready, 1)
                act.wait_ge(plan_ready, l + 1)
                pairs = act.value_load(blki[0:1, MAXB:MAXB + 1], min_val=1, max_val=MAXB // 2)
                act.sem_inc(sems["y_ready"], 1)
                act.sem_inc(sems["y_stored"], 32)

                def gathered(count):
                    act.wait_ge(sems["xg_mm"], count)
                    act.activation(xg, ps[:, 0:2, :].rearrange("p b (k s) -> p (b k) s", s=PAIR), ACT.Copy).then_inc(sems["xg_ready"], 1)

                gathered(1)
                with act.Fori(0, pairs) as i:
                    act.wait_ge(sems["gu_mm"], 2 * i + 3)
                    act.activation(silu_g, ps[:, 2, :], ACT.Silu).then_inc(sems["sg_ready"], 1)
                    gathered(i + 2)
                    act.wait_ge(sems["y_mm"], i + 2)
                    act.wait_ge(sems["y_stored"], 32 * i + 32)
                    act.activation(yb, ps[:, 6:8, :].rearrange("p a b -> p (a b)"), ACT.Copy).then_inc(sems["y_ready"], 1)
                    act.wait_ge(sems["y_ready"], i + 2)
                    for u in range(2):
                        act.dma_start(y_rows[bass.ds((u * pairs + i) * SLOTS, SLOTS), :], yb[u * SLOTS:(u + 1) * SLOTS, :]).then_inc(sems["y_stored"], 16)
                act.wait_ge(sems["y_stored"], 32 * pairs + 32)
                act.sem_inc(stored_all, 1)

            block1(0)
            experts(0)
            block1(1)
            experts(1)

            def layer2(i):
                call = 4 + 2 * i
                act.wait_ge(x2_ready, 6)
                norm_stats(call, False, lambda k: act.wait_ge(xo_ready, 2 * KC * i + k + 1))

                def ev2(n, dst, src, func=ACT.Copy, **kw):
                    act.wait_ge(p2_mm, P2N * i + n + 1)
                    return act.activation(dst, src, func, **kw)

                for n in range(4):
                    ev2(n, qp[:, n, :], ps[:, n % 4, 0:NX]).then_inc(p2_ev, 1)
                for n in range(4, 7):
                    ev2(n, kv[:, n - 4, :], ps[:, n % 4, 0:NX]).then_inc(p2_ev, 1)
                ev2(7, vsw, ps[:, 3, 0:NX].rearrange("p (n d) -> p n d", n=QT))
                ev2(7, gates[:, :, :], ps[:, 3, NX:NX + 48].rearrange("p (n d) -> p n d", n=QT), ACT.Sigmoid).then_inc(p2_ev, 1)
                for n in range(8, 12):
                    ev2(n, sbq[:, n - 8, :], ps[:, n % 4, 0:NX], scale=SC_B).then_inc(p2_ev, 1)
                for n in range(12, 16):
                    ev2(n, sbk[:, n - 12, :], ps[:, n % 4, 0:NX]).then_inc(p2_ev, 1)
                for n in range(16, 18):
                    ev2(n, sbv[:, n - 16, :], ps[:, n % 4, :]).then_inc(p2_ev, 1)
                act.wait_ge(cmp_mm, 4 * i + 2)
                act.activation(hrow, ps[:, 6, :], ACT.Copy).then_inc(cmp_ready, 1)
                act.wait_ge(cmp_mm, 4 * i + 3)
                act.activation(hcmp[:, :, :], ps[:, 7, 0:64].rearrange("p (v c) -> p v c", v=4), ACT.Copy).then_inc(cmp_ready, 1)
                act.wait_ge(cmp_ready, 2 * i + 2)
                for q in range(4):
                    ins = act.activation(gcmp[:, q, :], hcmp[:, q, 0:NCMP], ACT.Gelu_apprx_tanh, bias=hcmp[:, q, NCMP:NCMP + 1])
                ins.then_inc(gel_ready, 1)
                act.wait_ge(pcn_ready, 2 * i + 1)
                act.activation(scmp, scmp, ACT.Exp, scale=SC_A).then_inc(pce_ready, 1)
                act.wait_ge(pct_mm, i + 1)
                act.activation(pcT, ps[:, 4, :].rearrange("p (b q) -> p b q", b=4), ACT.Copy).then_inc(pct_ready, 1)
                zp = ps[:, 0:SBH, 0:384]
                act.wait_ge(sbz_mm, i + 1)
                act.activation(spl, zp, ACT.Abs).then_inc(sb_act, 1)
                act.wait_ge(sb_act, 5 * i + 1)
                act.activation(spl, spl, ACT.Exp, scale=-1.0).then_inc(sb_act, 1)
                act.wait_ge(sb_act, 5 * i + 2)
                act.activation(spl, spl, ACT.Ln, bias=1.0).then_inc(sb_act, 1)
                act.wait_ge(sb_dve, 2 * i + 2)
                act.activation(zs, zs, ACT.Exp).then_inc(sb_act, 1)
                act.wait_ge(sbo_mm, i + 1)
                act.activation(osb, ps[:, 0:SBH, 0:NX], ACT.Copy).then_inc(sb_act, 1)
                for s in range(2 * HEADS + 2):
                    if s < 2 * HEADS:
                        n, u, k = 40 + 16 * i + s, s % 2, P * (s % 2 + 1)
                        act.wait_ge(tr_mm, n - 1)
                        attend_exp(n, u, [((0, k), 0), ((NX, NX + k), 1)], SC_A)
                        ev2(18 + s, mg[:, s, :], ps[:, 6 + s % 2, 0:NX]).then_inc(p2_ev, 1)
                    if 1 <= s <= 2 * HEADS:
                        n, u = 40 + 16 * i + s - 1, (s - 1) % 2
                        act.wait_ge(pv_mm, n - 1)
                        attend_pt(n, u, 2 * (u + 1))
                    if s >= 2 and (s - 2) % 4 == 3:
                        n, c = 40 + 16 * i + s - 2, (s - 2) // 4
                        act.wait_ge(pv_mm, n + 1)
                        act.activation(onsa[:, c, :], ps[:, 4 + c % 2, 0:NX], ACT.Copy).then_inc(o_ready, 1)
                act.wait_ge(p2_ev, P2N * i + P2N)
                for j in range(KC // 2):
                    m = mg.rearrange("p (b m) t -> p b m t", b=2)[:, :, 2 * j:2 * j + 2, :]
                    act.activation(m, m, ACT.Sigmoid).then_inc(mgs_ready, 1)

                def out_norm(c):
                    for n in range(KC):
                        m = n if c == 0 else FF_OUT[n]
                        y = ps[:, m % 4, 0:NX] if c == 0 else ps[:, m % 4, m // 4 * NX:m // 4 * NX + NX]
                        act.wait_ge(wo_mm, WON + WON * i + KC * c + (n if c == 0 else n | 1) + 1)
                        if n >= 4:
                            act.wait_ge(nss_mm, WON * i + KC * c + n - 3)
                        act.activation(yres[:, m, :], y, ACT.Copy)
                        act.activation(sqb[:, n % 4, 0:NX], y, ACT.Square).then_inc(nsq_ready, 1)
                    act.wait_ge(nss_mm, WON * i + KC * c + KC)
                    act.activation(stdv[:, 0:NX], ps[:, 7, 0:NX], ACT.Sqrt, bias=eps, scale=1.0 / D).then_inc(nstd_ready, 1)

                out_norm(0)
                norm_stats(call + 1, False, lambda k: act.wait_ge(xo_ready, 2 * KC * i + KC + k + 1))
                for m in range(FF // P):
                    act.wait_ge(f1_mm, 32 * i + 32 + m + 1)
                    if m >= 4:
                        act.wait_ge(ffs_ready, 32 * i + m - 3)
                    r = sqb[:, m % 4, 0:NX]
                    act.activation(r, ps[:, 4 + m % 4, 0:NX], ACT.Relu).then_inc(f1_ev, 1)
                    act.wait_ge(f1_ev, 32 * i + m + 1)
                    act.activation(r, r, ACT.Square).then_inc(ffh_ready, 1)
                out_norm(1)

            with act.Fori(0, 2) as i:
                layer2(i)

        @block.tensor
        def _(pe):
            def take_slab(n, shape):
                pe.wait_ge(slab_in[n % RING], 16 * (n // RING + 1))
                return slab(n, shape)

            def mm_chunk(out, w, m0, rhs, nk=KC, start=True, stop=True):
                for k in range(nk):
                    ins = pe.matmul(out, w[:, k, m0:m0 + P], rhs(k), start=start and k == 0, stop=stop and k == nk - 1)
                return ins

            def square_sum(call, full, k):
                w = 512 if full else NX
                pe.wait_ge(sq_ready, KC * call + k + 1)
                pe.matmul(ps[:, 7, 0:w], ones[:, :], sqb[:, k % 4, 0:w], start=k == 0, stop=k == KC - 1).then_inc(ssq_mm, 1)

            def norm(call, full):
                for k in range(KC):
                    square_sum(call, full, k)

            def mod_sum(j):
                w = take_slab(mod_at(j), (KC, 512))
                if j:
                    pe.wait_ge(mod_ev, j)
                for k in range(KC):
                    q = k % 4
                    ins = pe.matmul(ps[32 * q:32 * q + 32, 6, :], condv[:, k, :], w[:, k, :], start=k < 4, stop=k >= 4)
                ins.then_inc(mod_mm, 1)

            def mod_columns(j):
                pe.wait_ge(mod_ev, j + 1)
                bank, at = (5, 8 * j) if j < MOD0 else (7, 8 * (j - MOD0))
                for m in range(4):
                    ins = pe.matmul(ps[:, bank, at + 2 * m:at + 2 * m + 2], mrow[:, m * P:m * P + P], cc("fold")[:, 0:2], start=True, stop=True)
                ins.then_inc(mod_fold, 1)

            def qss(g, c, w):
                pe.wait_ge(qsq_ready, g + 1)
                if g >= 1:
                    pe.wait_ge(qstd_ready, g)
                pe.matmul(ps[:, 5, 0:w], cc("headones"), sqb[:, g % 2, 0:w], start=True, stop=True).then_inc(qss_mm, 1)

            def qrot(g, c):
                pe.wait_ge(qn_ready, g + 1)
                if g >= 1:
                    pe.wait_ge(rope_ready, g)
                pe.matmul(ps[:, 6, 0:NX], cc("rot_a"), qk[:, c, 0:NX], start=True, stop=True).then_inc(rot_mm, 1)

            def block1(layer):
                full = layer == 0
                base, g0 = (0, 0) if full else (14, 5)
                n0 = AB_IN if full else NA
                norm(2 * layer, True)
                if full:
                    pe.wait_ge(cond_ready, 1)
                    for j in range(MOD0):
                        mod_sum(j)
                        mod_columns(j)
                pe.wait_ge(h_ready, KC * (2 * layer + 1))

                def bank_free(n):
                    if n >= 4:
                        pe.wait_ge(proj_ev, base + n - 3)

                w = take_slab(n0, (KC, 512))
                wq = 512 if full else NX
                for c in range(QC):
                    mm_chunk(ps[:, c, 0:wq], w, c * P, lambda k: hsrc(full, k)).then_inc(proj_mm, 1)
                w = take_slab(n0 + 1, (KC, 512))
                bank_free(4)
                mm_chunk(ps[:, 0, :], w, 0, lambda k: hsrc(True, k)).then_inc(proj_mm, 1)
                bank_free(5)
                for n in range(4):
                    for k in range(KC):
                        ins = pe.matmul(ps[:, 1, n * P:n * P + P], hT[:, n // 2, k, (n % 2) * P:(n % 2) * P + P], w[:, k, P:2 * P],
                                        start=k == 0, stop=k == KC - 1)
                ins.then_inc(proj_mm, 1)
                for n in range(8):
                    m = n + 2
                    if (full or n < BC) and m % 4 == 0:
                        w = take_slab(n0 + 1 + m // 4, (KC, 512 if full and m < 12 and not m == 8 else 256))
                    if full or n < BC:
                        bank_free(6 + n)
                        mm_chunk(ps[:, (6 + n) % 4, 0:wq], w, (m % 4) * P, lambda k: hsrc(full, k)).then_inc(proj_mm, 1)
                    if n < QKC:
                        qss(g0 + n, n, 512 if n == QC else wq)
                    if 1 <= n <= QKC:
                        qrot(g0 + n - 1, n - 1)
                pe.wait_ge(rope_ready, g0 + QKC)
                pe.matmul(ps[:, 6, :], cc("swap"), qk[:, QC, :], start=True, stop=True).then_inc(swap_mm, 1)
                pe.wait_ge(swap_ev, layer + 1)
                pe.wait_ge(proj_ev, base + (14 if full else 10))
                ow = AB_OUT if full else NA + 4

                def heads_first(m0, m1):
                    w = take_slab(ow, (KC, 512))
                    for m in range(m0, m1):
                        mm_chunk(ps[:, m, 0:wq], w, m * P, lambda k: cat[:, k, 0:wq], 4, stop=False)

                units = attention_units(layer)
                for s in range(len(units) + 2):
                    if s < len(units):
                        n, h, kind = units[s]
                        if s >= 2:
                            pe.wait_ge(ex_ready, n - 1)
                        o, j = (h % 2) * DH, h // 4
                        kk = qk[:, QC, :] if o == j * DH else kswap
                        u = n % 2
                        if kind == 2:
                            for t in range(QT):
                                ins = pe.matmul(ps[:, u, t * NX:t * NX + NX], qk[o:o + DH, h // 2, NX + t * P:NX + t * P + P],
                                                kk[o:o + DH, NX:512], start=True, stop=True)
                        else:
                            ins = pe.matmul(ps[:, u, :], qk[o:o + DH, h // 2, kind * P:kind * P + P], kk[o:o + DH, :],
                                            start=True, stop=full)
                            if not full:
                                c0 = P if kind == 0 else 0
                                ins = pe.matmul(ps[:, u, c0:c0 + P], ident, cc("trineg") if kind == 0 else cc("band1"), start=False, stop=True)
                        ins.then_inc(sc_mm, 1)
                    if full and 1 <= s <= 24 - MOD0:
                        if s > 1:
                            mod_columns(MOD0 + s - 2)
                        mod_sum(MOD0 + s - 1)
                    if 1 <= s <= len(units):
                        n = units[s - 1][0]
                        transposes(n, n % 2, [(b * P, b * P + P) for b in range(4)], s > 2)
                    if s >= 2:
                        n, h, kind = units[s - 2]
                        pe.wait_ge(pt_ready, n + 1)
                        o, j, u = (h % 2) * DH, h // 4, n % 2
                        ch = h // 2
                        if ch >= 2 and h % 2 == 0 and kind == 0:
                            pe.wait_ge(o_ready, 4 * layer + ch - 1)
                        ob = ps[o:o + DH, 4 + ch % 2, :]
                        if kind == 2:
                            for t in range(QT):
                                for b in range(2):
                                    ins = pe.matmul(ob[:, NX + t * P:NX + t * P + P], vtok[:, 2 + b, j * DH:j * DH + DH], probT[:, u, 2 * t + b, :],
                                                    start=b == 0, stop=b == 1)
                        else:
                            for b in range(4):
                                ins = pe.matmul(ob[:, kind * P:kind * P + P], vtok[:, b, j * DH:j * DH + DH], probT[:, u, b, :],
                                                start=b == 0, stop=b == 3)
                        ins.then_inc(pv_mm, 1)
                if full:
                    mod_columns(23)
                    pe.wait_ge(conv_ready, 1)
                    for c in range(BC):
                        ins = pe.matmul(ps[:, 6, :], ones[:, :], cat[:, 4 + c, :], start=c == 0, stop=c == BC - 1)
                    ins.then_inc(cmu_mm, 1)
                    pe.wait_ge(o_ready, 4)
                    heads_first(0, 2)
                    for c in range(BC):
                        pe.wait_ge(csq_ready, c + 1)
                        ins = pe.matmul(ps[:, 5, :], ones[:, :], sqb[:, c, :], start=c == 0, stop=c == BC - 1)
                    ins.then_inc(cvar_mm, 1)
                    heads_first(2, 4)
                    pe.wait_ge(bx_ready, BC)
                else:
                    wp = take_slab(n0 + 3, (BC, P))
                    pe.wait_ge(pool_ready, BC)
                    for g in range(BC):
                        ins = pe.matmul(ps[:, 6 + g // 2, (g % 2) * NX:(g % 2) * NX + NX], wp[:, g, :], pt_pool[:, g, :], start=True, stop=True)
                    ins.then_inc(pool_mm, 1)
                    pe.wait_ge(px_ready, 1)
                pe.wait_ge(o_ready, 4 * layer + 4)
                for m in range(KC):
                    if m % 4 == 0:
                        w = take_slab(ow + m // 4, (KC, 512))
                    if m >= 4:
                        pe.wait_ge(x_ready, KC * layer + m - 3)
                    for k in range(4 if full and m < 4 else 0, KC):
                        ins = pe.matmul(ps[:, m % 4, 0:wq], w[:, k, (m % 4) * P:(m % 4) * P + P], cat[:, k, 0:wq], start=k == 0, stop=k == KC - 1)
                    ins.then_inc(out_mm, 1)
                    if m >= 2:
                        square_sum(2 * layer + 1, full, m - 2)
                for k in (6, 7):
                    square_sum(2 * layer + 1, full, k)

            def transposes(n, u, blocks, again):
                pe.wait_ge(pn_ready, n + 1)
                if again:
                    pe.wait_ge(pt_ready, n - 1)
                for b, (c0, c1) in enumerate(blocks):
                    ins = pe.transpose(ps[:, 2 + u, b * P:b * P + P], prob[:, u, c0:c1], ident)
                ins.then_inc(tr_mm, 1)

            def experts(l):
                nt = NTM if l == 0 else QT
                sems = moe[l]
                pe.wait_ge(h_ready, KC * (2 * l + 2))

                def htile(n, k):
                    return hT[:, n // 2, k, (n % 2) * P:(n % 2) * P + P]

                for n in range(nt):
                    for k in range(KC):
                        at, _ = po["rt_w"]
                        w = par[:, at + (l * KC + k) * RL:at + (l * KC + k + 1) * RL]
                        ins = pe.matmul(ps[:, 0, n * RL:(n + 1) * RL], htile(n, k), w, start=k == 0, stop=k == KC - 1)
                ins.then_inc(rt_mm, 1)
                for q in range(2 * nt):
                    if q >= 3:
                        pe.wait_ge(ht_ev, (0, 2 * NTM)[l] + q - 2)
                    for b in range(4):
                        ins = pe.transpose(ps[:, 4 + q % 3, b * P:b * P + P], htile(q // 2, 4 * (q % 2) + b), ident)
                    ins.then_inc(ht_mm, 1)
                pe.wait_ge(m_ready, l + 1)
                for n in range(nt):
                    for j in range(n + 1):
                        pe.matmul(ps[:, 1, n * NE:(n + 1) * NE], cc("tri_strict") if j == n else ones[:, :], M1[:, 2, j * NE:(j + 1) * NE],
                                  start=j == 0, stop=j == n)
                for j in range(nt):
                    ins = pe.matmul(ps[:, 1, nt * NE:(nt + 1) * NE], ones[:, :], M1[:, 2, j * NE:(j + 1) * NE], start=j == 0, stop=j == nt - 1)
                ins.then_inc(pos_mm, 1)
                pe.wait_ge(plan_ready, l + 1)
                pe.wait_ge(ht_ev, (2 * NTM, 2 * NTM + 2 * QT)[l])
                pairs = pe.value_load(blki[0:1, MAXB:MAXB + 1], min_val=1, max_val=MAXB // 2)
                pe.sem_inc(sems["gu_mm"], 2)
                pe.sem_inc(sems["y_mm"], 1)

                def gather(count):
                    pe.wait_ge(sems["sel_ready"], count)
                    for k in range(KC):
                        for n in range(nt):
                            ins = pe.matmul(ps[:, k // 4, (k % 4) * PAIR:(k % 4 + 1) * PAIR], htok[:, n, k * P:(k + 1) * P], sel[:, n, :],
                                            start=n == 0, stop=n == nt - 1)
                    ins.then_inc(sems["xg_mm"], 1)

                half = lambda u: slice(u * SLOTS, (u + 1) * SLOTS)
                gather(1)
                with pe.Fori(0, pairs) as i:
                    pe.wait_ge(sems["xg_ready"], i + 1)
                    for w in range(2):
                        for u in range(2):
                            pe.wait_ge(sems["w_in"][2 * w + u], 16 * i + 16)
                        for k in range(KC):
                            for u in range(2):
                                ins = pe.matmul(ps[half(u), 2 + w, :], xg[:, k, half(u)], slab(2 * w + u, (KC, DE))[:, k, :],
                                                start=k == 0, stop=k == KC - 1)
                        ins.then_inc(sems["gu_mm"], 1)
                    gather(i + 2)
                    pe.wait_ge(sems["hid_ready"], i + 1)
                    for m in range(EC):
                        ins = pe.transpose(ps[:, 4, m * P:(m + 1) * P], htmp[:, m * P:(m + 1) * P], ident)
                    ins.then_inc(sems["hidt_mm"], 1)
                    pe.wait_ge(sems["hidt_ready"], i + 1)
                    pe.wait_ge(sems["y_ready"], i + 1)
                    for u in range(2):
                        pe.wait_ge(sems["w_in"][4 + u], 16 * i + 16)
                    for m in range(EC):
                        for c in range(2):
                            for u in range(2):
                                ins = pe.matmul(ps[half(u), 6 + c, :], hid[:, m, half(u)], slab(4 + u, (EC, D))[:, m, c * 512:(c + 1) * 512],
                                                start=m == 0, stop=m == EC - 1)
                    ins.then_inc(sems["y_mm"], 1)
                for n in range(nt):
                    t = (0, NTM)[l] + n
                    pe.wait_ge(mix_ready, t + 1)
                    if n >= 2:
                        pe.wait_ge(x2_ready, t - 1)
                    for k in range(KC):
                        ins = pe.transpose(ps[:, 2 * (n % 2) + k // 4, (k % 4) * P:(k % 4 + 1) * P], yg[:, n, 0, k * P:(k + 1) * P], ident)
                    ins.then_inc(yt_mm, 1)

            pe.sem_inc(wo_mm, WON)
            pe.sem_inc(f1_mm, 32)
            pe.sem_inc(f2_mm, 7)
            pe.wait_ge(inputs_in, 16 * n_in)
            pe.wait_ge(setup_done, 2)
            block1(0)
            experts(0)
            block1(1)
            experts(1)

            def layer2(i):
                call = 4 + 2 * i

                def take(j, shape):
                    pe.wait_ge(slab_in[j % RING], slab2_count(i, j))
                    return slab(j, shape)

                hn = lambda k: hT[:, 0, k, :]
                norm(call, False)
                pe.wait_ge(h_ready, KC * call + KC)
                evs = P2N * i

                def bank_free(n):
                    if n >= 4:
                        pe.wait_ge(p2_ev, evs + n - 3)

                def chunks(n, j, count, width=512):
                    w = take(j, (KC, width))
                    for c in range(count):
                        bank_free(n + c)
                        mm_chunk(ps[:, (n + c) % 4, 0:NX], w, c * P, hn).then_inc(p2_mm, 1)
                    return w

                chunks(0, 0, 4)
                w = chunks(4, 1, 3, COL_SB - 512)
                bank_free(7)
                for t in range(QT):
                    for k in range(KC):
                        pe.matmul(ps[:, 3, t * P:t * P + P], hT[:, 0, k, t * P:t * P + P],
                                  w[:, k, P:3 * P].rearrange("p (b d) -> p b d", b=2)[:, :, DH:P], start=k == 0, stop=k == KC - 1)
                for t in range(QT):
                    for k in range(KC):
                        ins = pe.matmul(ps[:, 3, NX + t * 24:NX + t * 24 + 24], hT[:, 0, k, t * P:t * P + P], w[:, k, 3 * P:3 * P + 24],
                                        start=k == 0, stop=k == KC - 1)
                ins.then_inc(p2_mm, 1)
                pe.wait_ge(p2_ev, evs + 7)
                for c in range(4):
                    pe.matmul(ps[:, 4 + c // 2, (c % 2) * NX:(c % 2) * NX + NX], cc("rot_b"), qp[:, c, :], start=True, stop=True).then_inc(r2_mm, 1)
                for c in range(2):
                    pe.matmul(ps[:, 6, c * NX:c * NX + NX], cc("rot_b"), kv[:, 1 + c, :], start=True, stop=True).then_inc(r2_mm, 1)
                chunks(8, 2, 4)
                pe.wait_ge(r2_ready, 10 * i + 6)
                for c, m in enumerate(("dup0", "dup1")):
                    pe.matmul(ps[:, 4, c * NX:c * NX + NX], cc(m), kv[:, 0, :], start=True, stop=True).then_inc(r2_mm, 1)
                for c in range(2):
                    pe.matmul(ps[:, 5, c * NX:c * NX + NX], cc("dup0"), kv[:, 1 + c, :], start=True, stop=True).then_inc(r2_mm, 1)
                chunks(12, 3, 4)
                w = take(4, (KC, 512))
                for t in range(QT):
                    bank_free(16 + t)
                    for k in range(KC):
                        ins = pe.matmul(ps[:, (16 + t) % 4, :], hT[:, 0, k, t * P:t * P + P], w[:, k, :], start=k == 0, stop=k == KC - 1)
                    ins.then_inc(p2_mm, 1)
                pe.wait_ge(r2_ready, 10 * i + 10)
                for v in range(2):
                    w = take(J_CMP + v, (CB // 2, 256))
                    for j in range(CB // 2):
                        q = j % 4
                        ins = pe.matmul(ps[32 * q:32 * q + 32, 6, v * 256:v * 256 + 256], win[v][:, j, :], w[:, j, :], start=j < 4, stop=j >= CB // 2 - 4)
                    ins.then_inc(cmp_mm, 1)
                pe.wait_ge(cmp_ready, 2 * i + 1)
                for q in range(4):
                    ins = pe.matmul(ps[:, 7, 16 * q:16 * q + 16], hrow[:, q * P:q * P + P], cc("fold"), start=True, stop=True)
                ins.then_inc(cmp_mm, 1)
                pe.wait_ge(gel_ready, i + 1)
                w2 = lambda v, c: lp("w2", (2 * v + c) * 64, 64)
                for o in range(2):
                    for c in range(2):
                        pe.matmul(ps[o * DH:o * DH + DH, 4, 0:NCMP], w2(0, c), gcmp[:, c, :], start=c == 0, stop=c == 1)
                for hh in range(4):
                    for c in range(2):
                        ins = pe.matmul(ps[32 * hh:32 * hh + NCMP, 4, 64:128], gcmp[:, 2 + c, :], w2(1, c), start=c == 0, stop=c == 1)
                ins.then_inc(cmp_mm, 1)
                pe.wait_ge(cev_ready, i + 1)
                for t in range(QT):
                    for h in range(HEADS):
                        o, c0 = (h % 2) * DH, (t * HEADS // 2 + h // 2) * 16
                        ins = pe.matmul(ps[:, 5 + h % 2, c0:c0 + NCMP], qp[o:o + DH, h // 2, t * P:t * P + P], kcmp[o:o + DH, :], start=True, stop=True)
                ins.then_inc(cs_mm, 1)
                pe.wait_ge(pcn_ready, 2 * i + 2)
                for t in range(QT):
                    for q in range(2):
                        ins = pe.transpose(ps[:, 4, (2 * t + q) * P:(2 * t + q + 1) * P],
                                           pcp[:, t, 4 * q:4 * q + 4, :].rearrange("p h c -> p (h c)"), ident)
                ins.then_inc(pct_mm, 1)
                pe.wait_ge(p2_ev, evs + 18)
                for h in range(SBH):
                    pe.matmul(ps[:, h, 0:NX], sbk[:, h, 0:P], sbq[:, h, :], start=True, stop=True)
                    ins = pe.matmul(ps[:, h, NX:384], sbk[:, h, P:NX], sbq[:, h, P:NX], start=True, stop=True)
                ins.then_inc(sbz_mm, 1)
                pe.wait_ge(sb_dve, 2 * i + 1)
                pe.wait_ge(pct_ready, i + 1)
                for h in range(SBH):
                    b = 4 + h
                    pe.matmul(ps[:, b, 0:P], cc("negtri"), spl[:, h, 0:P], start=True, stop=True)
                    pe.matmul(ps[:, b, P:NX], cc("negtri"), spl[:, h, P:NX], start=True, stop=False)
                    pe.matmul(ps[:, b, P:NX], negones[:, :], spl[:, h, NX:384], start=False, stop=True)
                    ins = pe.matmul(ps[:, b, NX:384], cc("negtri"), spl[:, h, NX:384], start=True, stop=True)
                ins.then_inc(sbc_mm, 1)
                pe.wait_ge(sb_act, 5 * i + 4)
                for h in range(SBH):
                    pe.matmul(ps[:, h, 0:NX], sbv[:, 0, h * P:h * P + P], zs[:, h, 0:NX], start=True, stop=False)
                    ins = pe.matmul(ps[:, h, P:NX], sbv[:, 1, h * P:h * P + P], zs[:, h, NX:384], start=False, stop=True)
                ins.then_inc(sbo_mm, 1)
                pe.wait_ge(sb_act, 5 * i + 5)
                for s in range(2 * HEADS + 2):
                    if s < 2 * HEADS:
                        n, h, t = 40 + 16 * i + s, s // 2, s % 2
                        o, k = (h % 2) * DH, P * (t + 1)
                        pe.wait_ge(ex_ready, n - 1)
                        for b in range(2):
                            pe.matmul(ps[:, t, b * NX:b * NX + k], qr[o:o + DH, h // 2, t * P:t * P + P], kdup[o:o + DH, b, 0:k], start=True, stop=False)
                            ins = pe.matmul(ps[:, t, b * NX + t * P:b * NX + k], ident, cc("trineg"), start=False, stop=True)
                        ins.then_inc(sc_mm, 1)
                        w = take(J_MG + s // 4, (KC, 512))
                        if s >= 2:
                            pe.wait_ge(p2_ev, evs + 18 + s - 1)
                        mm_chunk(ps[:, 6 + s % 2, 0:NX], w, s % 4 * P, hn).then_inc(p2_mm, 1)
                    if 1 <= s <= 2 * HEADS:
                        t = (s - 1) % 2
                        transposes(40 + 16 * i + s - 1, t, [(b * NX + j * P, b * NX + j * P + P) for b in range(2) for j in range(t + 1)], True)
                    if s >= 2:
                        n, h, t = 40 + 16 * i + s - 2, (s - 2) // 2, s % 2
                        o, c = (h % 2) * DH, h // 2
                        pe.wait_ge(pt_ready, n + 1)
                        if t == 0 and h % 2 == 0:
                            pe.wait_ge(o_ready, 8 + 4 * i + max(c - 1, 0))
                        ob = ps[o:o + DH, 4 + c % 2, t * P:t * P + P]
                        pe.matmul(ob, vblk[:, h % 4, :], pcT[:, 2 * t + h // 4, :], start=True, stop=False)
                        for b in range(2):
                            for j in range(t + 1):
                                ins = pe.matmul(ob, vsw[:, j, b * DH:b * DH + DH], probT[:, t, b * (t + 1) + j, :], start=False,
                                                stop=b == 1 and j == t)
                        ins.then_inc(pv_mm, 1)
                pe.wait_ge(o_ready, 8 + 4 * i + 4)
                wn, ws = take(J_NSA, (4, D)), take(J_SB, (4, D))
                for m in range(KC):
                    if m >= 4:
                        pe.wait_ge(mix2_ready, KC * i + m - 3)
                    mm_chunk(ps[:, m % 4, 0:NX], wn, m * P, lambda k: onsa[:, k, :], 4)
                    mm_chunk(ps[:, m % 4, NX:512], ws, m * P, lambda k: osb[:, k, :], 4).then_inc(y2_mm, 1)

                def out_norm(c, chunk):
                    for m in range(KC + 1):
                        if m < KC:
                            if m >= 4:
                                pe.wait_ge(nsq_ready, WON * i + KC * c + m - 3)
                            chunk(m).then_inc(wo_mm, 1)
                        if m >= 1:
                            pe.wait_ge(nsq_ready, WON * i + KC * c + m)
                            pe.matmul(ps[:, 7, 0:NX], ones[:, :], sqb[:, (m - 1) % 4, 0:NX], start=m == 1, stop=m == KC).then_inc(nss_mm, 1)

                pe.wait_ge(mix2_ready, KC * i + KC)
                wo = [take(J_OUT + j, (KC, 512)) for j in range(2)]
                out_norm(0, lambda m: mm_chunk(ps[:, m % 4, 0:NX], wo[m // 4], (m % 4) * P, lambda k: mixT[:, k, :]))
                norm(call + 1, False)
                pe.wait_ge(h_ready, KC * call + 2 * KC)
                def three(out, hi, lo, xhi, xlo, first, last):
                    pe.matmul(out, hi, xhi, start=first, stop=False)
                    pe.matmul(out, hi, xlo, start=False, stop=False)
                    return pe.matmul(out, lo, xhi, start=False, stop=last)

                def hidden(n, j):
                    hi, lo = (w.rearrange("p (k w) -> p k w", k=KC) for w in (w_hi[:, n % 2, :], w_lo[(J_FF + n) % RING][:, :]))
                    for c in range(4):
                        m = 4 * j + c
                        if m >= 4:
                            pe.wait_ge(f1_ev, 32 * i + m - 3)
                        for k in range(KC):
                            ins = three(ps[:, 4 + m % 4, 0:NX], hi[:, k, c * P:c * P + P], lo[:, k, c * P:c * P + P], hn_hi[:, k, :], hn_lo[:, k, :],
                                        k == 0, k == KC - 1)
                        ins.then_inc(f1_mm, 1)

                def output(n, j, m):
                    hi, lo = (w.rearrange("p (k w) -> p k w", k=4) for w in (w_hi[:, n % 2, :], w_lo[(J_FF + n) % RING][:, :]))
                    for k in range(4):
                        x = (4 * j + k) % 8
                        ins = three(ps[:, m % 4, m // 4 * NX:m // 4 * NX + NX], hi[:, k, m * P:m * P + P], lo[:, k, m * P:m * P + P],
                                    ff_hi[:, x, :], ff_lo[:, x, :], j == 0 and k == 0 and m < 4, j == 7 and k == 3 and m >= 4)
                    return ins

                for n, (w, j) in enumerate(FF_ORDER):
                    pe.wait_ge(split_ready, 16 * i + n + 1)
                    if w == 1:
                        hidden(n, j)
                        continue
                    pe.wait_ge(ffs_ready, 32 * i + 4 * j + 4)
                    if j < 7:
                        for m in range(KC):
                            ins = output(n, j, m)
                        ins.then_inc(f2_mm, 1)
                    else:
                        out_norm(1, lambda m: output(n, j, FF_OUT[m]))

            pe.wait_ge(trig_done, 1)
            pe.wait_ge(x2_ready, 6)
            with pe.Fori(0, 2) as i:
                layer2(i)

        @block.vector
        def _(dve):
            chain = [0]

            def link(ins):
                chain[0] += 1
                ins.then_inc(dchain, 1)
                dve.wait_ge(dchain, chain[0])

            def step(ins, back):
                chain[0] += 1
                ins.then_inc(dchain, 1)
                if chain[0] > back:
                    dve.wait_ge(dchain, chain[0] - back)

            iota = cc("iota")

            def norm(call, full, gain=None, after=None):
                w = 512 if full else NX
                dve.wait_ge(std_ready, call + 1)
                dve.reciprocal(stdv[:, 0:w], stdv[:, 0:w]).then_inc(rstd_ready, 1)
                dve.wait_ge(rstd_ready, call + 1)
                for k in range(KC):
                    if gain is None:
                        dve.tensor_tensor(hsrc(full, k), src_of(full, k), g2(stdv[:, :]) if full else stdv[:, 0:NX], ALU.mult).then_inc(xn_ready, 1)
                    else:
                        ins = dve.scalar_tensor_tensor(hT[:, 0, k, :], xT[:, 0, k, :], gain(k), stdv[:, 0:NX], ALU.mult, ALU.mult)
                        if after is None:
                            ins.then_inc(h_ready, 1)
                        else:
                            after(ins, k)

            dve.memset(condv[:, :, :], 0.0)
            dve.memset(gpad, 0.0).then_inc(setup_done, 1)
            dve.memset(ones[:, :], 1.0)
            dve.memset(negones[:, :], -1.0)
            dve.memset(pcp[:, :, :, :], 0.0)
            dve.memset(vblk[:, :, :], 0.0)
            dve.wait_ge(inputs_in, 16 * n_in)
            dve.tensor_scalar(mneg[:, :], cc("m01"), 1.0, -NEG, ALU.subtract, ALU.mult).then_inc(setup_done, 1)
            ang, kf = E[:, NX:2 * NX], E[:, 2 * NX:3 * NX]
            link(dve.tensor_copy(ang, E[:, 0:NX].bitcast(I32)))
            link(dve.tensor_scalar(ang, ang, cc("invf"), None, ALU.mult))
            link(dve.tensor_scalar(kf, ang, 1.0 / TWO_PI, None, ALU.mult))
            link(dve.tensor_scalar(kf, kf, MAGIC, None, ALU.add))
            link(dve.tensor_scalar(kf, kf, MAGIC, None, ALU.subtract))
            for part in (C1, C2, C3):
                link(dve.scalar_tensor_tensor(ang, kf, -part, ang, ALU.mult, ALU.add))
            link(dve.tensor_scalar(cos2, ang, TWO_PI / 4, None, ALU.add))
            link(dve.tensor_scalar(kf, cos2, TWO_PI / 2, -TWO_PI, ALU.is_gt, ALU.mult))
            link(dve.tensor_tensor(cos2, cos2, kf, ALU.add))
            link(dve.tensor_scalar(cos2, cos2, 3.1415925, -3.1415925, ALU.min, ALU.max))
            dve.tensor_scalar(sin2, ang, 3.1415925, -3.1415925, ALU.min, ALU.max).then_inc(trig_ready, 1)

            def mod_bias(l, m0, m1, bank, at):
                n = m1 - m0
                bias = pc("mod_b", 48 * l + m0, n).unsqueeze(2).broadcast_to([P, n, 2])
                return dve.tensor_tensor(modv[:, l, m0:m1, :], ps[:, bank, at:at + 2 * n].rearrange("p (m c) -> p m c", c=2), bias, ALU.add)

            def mod_scale(dst, l, at, gain):
                g = pc(gain, KC * l, KC).unsqueeze(2).broadcast_to([P, KC, 2])
                return dve.scalar_tensor_tensor(dst[:, l, :, :], modv[:, l, at:at + KC, :], 1.0, g, ALU.add, ALU.mult)

            def modulation_first():
                dve.wait_ge(mod_fold, MOD0)
                link(mod_bias(0, 0, 4 * MOD0, 5, 0))
                mod_scale(scale1, 0, 8, "ln1_g").then_inc(mod_ready, 1)

            def modulation_rest():
                dve.wait_ge(mod_fold, 24)
                mod_bias(0, 4 * MOD0, 48, 7, 0)
                link(mod_bias(1, 0, 48, 7, 2 * (48 - 4 * MOD0)))
                mod_scale(scale2, 0, 32, "ln2_g")
                mod_scale(scale1, 1, 8, "ln1_g")
                mod_scale(scale2, 1, 32, "ln2_g").then_inc(mod_ready, 1)

            def qk_norm(g, c, w, gain):
                r = sqb[:, 2 + g % 2, :]
                dve.wait_ge(qstd_ready, g + 1)
                link(dve.reciprocal(r[:, 0:w], r[:, 0:w]))
                dve.scalar_tensor_tensor(qk[:, c, 0:w], qk[:, c, 0:w], gain, r[:, 0:w], ALU.mult, ALU.mult).then_inc(qn_ready, 1)
                dve.wait_ge(qn_ready, g + 1)
                dve.wait_ge(rot_mm, g + 1)
                dve.tensor_tensor(r[:, 0:NX], ps[:, 6, 0:NX], cc("sin"), ALU.mult)
                link(dve.tensor_tensor(qk[:, c, 0:NX], qk[:, c, 0:NX], cc("cos"), ALU.mult))
                dve.tensor_tensor(qk[:, c, 0:NX], qk[:, c, 0:NX], r[:, 0:NX], ALU.add).then_inc(rope_ready, 1)

            def conv_taps():
                for c0 in (0, 2):
                    for t in range(TAPS):
                        for c in (c0, c0 + 1):
                            acc, src = g2(cat[:, 4 + c, :]), gpad[:, c, :, t:t + NX]
                            w = pc("conv_w", c * TAPS + t, 1)
                            if t == 0:
                                ins = dve.tensor_scalar(acc, src, w, pc("conv_b", c, 1), ALU.mult, ALU.add)
                            else:
                                ins = dve.scalar_tensor_tensor(acc, src, w, acc, ALU.mult, ALU.add)
                            yield ins

            def unit_max(n, u, views, sc):
                dve.wait_ge(sc_mm, n + 1)
                w = views.shape[1]
                return dve.tensor_reduce(mx[:, u, 0:w], views, AX_X, ALU.max), w

            def block1(layer):
                full = layer == 0
                base, g0 = (0, 0) if full else (14, 5)
                w = 512 if full else NX
                norm(2 * layer, True)
                if full:
                    modulation_first()
                if not full:
                    dve.memset(upad, 0.0).then_inc(setup_done, 1)
                for c in range(QKC):
                    qk_norm(g0 + c, c, 512 if c == QC else w, pc(("qn_a", "qn_c")[layer] if c < QC else ("kn_a", "kn_c")[layer]))
                taps = iter(())
                if full:
                    for c in range(BC):
                        dve.wait_ge(proj_ev, base + 11 + c)
                        g = gpad[:, c, :, HALO:HALO + NX]
                        link(dve.tensor_tensor(g, g, g2(cat[:, 4 + c, :]), ALU.mult))
                    taps = conv_taps()
                else:
                    pool_windows(base)
                units = attention_units(layer)
                for s in range(len(units) + 1):
                    if s < len(units):
                        n, h, kind = units[s]
                        u = n % 2
                        view = ps[:, u, :].rearrange("p (b k) -> p b k", b=2 if kind == 2 else 1)
                        ins, k = unit_max(n, u, view, SC_A)
                        link(ins)
                        if full:
                            dve.tensor_scalar(nb[:, u, 0:k], mx[:, u, 0:k], -SC_A, None, ALU.mult).then_inc(nb_ready, 1)
                        else:
                            link(dve.tensor_scalar(mx[:, u, 0:1], mx[:, u, 0:1], SC_A, pc("sink", h, 1), ALU.mult, ALU.max))
                            dve.tensor_scalar(nb[:, u, 0:1], mx[:, u, 0:1], -1.0, None, ALU.mult).then_inc(nb_ready, 1)
                    if s >= 1:
                        n, h, kind = units[s - 1]
                        u, k = n % 2, 2 if kind == 2 else 1
                        dve.wait_ge(ex_ready, n + 1)
                        if not full:
                            dve.wait_ge(sink_ready, n - 3 * HEADS + 1)
                            link(dve.tensor_tensor(sm[:, u, 0:1], sm[:, u, 0:1], es[:, u, :], ALU.add))
                        link(dve.reciprocal(sm[:, u, 0:k], sm[:, u, 0:k]))
                        for b in range(k):
                            p = prob[:, u, b * (512 // k):(b + 1) * (512 // k)]
                            ins = dve.tensor_scalar(p, p, sm[:, u, b:b + 1], None, ALU.mult)
                        ins.then_inc(pn_ready, 1)
                    for _ in range(6):
                        ins = next(taps, None)
                        if ins is not None:
                            step(ins, 1)
                if full:
                    modulation_rest()
                    for ins in taps:
                        step(ins, 1)
                    dve.wait_ge(dchain, chain[0])
                    dve.sem_inc(conv_ready, 1)
                    dve.wait_ge(cmu_mm, 1)
                    for c in range(BC):
                        ins = dve.scalar_tensor_tensor(cat[:, 4 + c, :], ps[:, 6, :], -1.0 / 512, cat[:, 4 + c, :], ALU.mult, ALU.add)
                    ins.then_inc(cd_ready, 1)
                    dve.wait_ge(cstd_ready, 1)
                    link(dve.reciprocal(stdv[:, :], stdv[:, :]))
                    for c in range(BC):
                        dve.tensor_tensor(cat[:, 4 + c, :], cat[:, 4 + c, :], stdv[:, :], ALU.mult).then_inc(cn_ready, 1)
                else:
                    dve.wait_ge(pool_mm, 1)
                    for g in range(BC):
                        ins = dve.tensor_scalar(cat[:, 4 + g, 0:NX], ps[:, 6 + g // 2, (g % 2) * NX:(g % 2) * NX + NX], pc("pool_scale", g, 1), None, ALU.mult)
                    ins.then_inc(px_ready, 1)
                for m in range(KC):
                    dve.wait_ge(out_mm, KC * layer + m + 1)
                    for g in range(TG if full else 1):
                        ins = dve.scalar_tensor_tensor(xT[:, g, m, :], ps[:, m % 4, g * NX:g * NX + NX], modv[:, layer, 16 + m, g:g + 1], xT[:, g, m, :],
                                                       ALU.mult, ALU.add)
                    ins.then_inc(x_ready, 1)
                norm(2 * layer + 1, full)

            def pool_windows(base):
                dve.wait_ge(invcnt_ready, 16)
                for c in range(BC):
                    dve.wait_ge(proj_ev, base + 7 + c)
                    src, lo, hi, half = upad[:, c, :], 0, UP, 0
                    for lev in range(c + 1):
                        dst = pwin[:, lev % 2, :]
                        d = max(half, 1)
                        left = half if lev else 1
                        right = half
                        a, b = lo + left, hi - right
                        link(dve.tensor_tensor(dst[:, a:b], src[:, a - left:b - left], src[:, a + right:b + right], ALU.add))
                        src, lo, hi = dst, a, b
                        half = 2 * half if lev else 1
                    link(dve.tensor_tensor(pt_pool[:, c, :], src[:, PPAD:PPAD + NX], invcnt[:, c, :], ALU.mult))
                    dve.tensor_tensor(pt_pool[:, c, :], pt_pool[:, c, :], upad[:, c, PPAD:PPAD + NX], ALU.subtract).then_inc(pool_ready, 1)

            def experts(l):
                nt = NTM if l == 0 else QT
                sems = moe[l]
                dve.wait_ge(rt_mm, l + 1)
                link(dve.memset(lgp, -3e38))
                b = pc("rt_b", l * RL, RL).unsqueeze(1).broadcast_to([P, nt, RL])
                link(dve.tensor_tensor(lg[:, 0:nt, :], ps[:, 0, 0:nt * RL].rearrange("p (n r) -> p n r", n=nt), b, ALU.add))
                link(dve.tensor_copy(lgp[:, 0:nt, 0:NG], lg[:, 0:nt, 0:NG]))
                for n in range(nt):
                    link(dve.max(gm8[:, n, :], lgp[:, n, :]))
                    link(dve.max_index(gi8[:, n, :], gm8[:, n, :], lgp[:, n, :]))
                link(dve.tensor_copy(rsc[:, 4, 0:nt], gi8[:, 0:nt, 0]))
                for n in range(nt):
                    link(dve.tensor_scalar(pen[:, n, :], iota[:, 0:NG], rsc[:, 4, n:n + 1], NEG, ALU.not_equal, ALU.mult))
                    e = lg[:, n, NG:RL].rearrange("p (g e) -> p g e", g=NG)
                    link(dve.tensor_tensor(e, e, pen[:, n, :].unsqueeze(2).broadcast_to([P, NG, NE // NG]), ALU.add))
                    link(dve.max(em8[:, n, :], lg[:, n, NG:RL]))
                    link(dve.max_index(ei8[:, n, :], em8[:, n, :], lg[:, n, NG:RL]))
                link(dve.tensor_scalar(rsc[:, 0, 0:nt], gm8[:, 0:nt, 0], -1.0, None, ALU.mult))
                for k in range(2):
                    link(dve.tensor_copy(rsc[:, 5 + k, 0:nt], ei8[:, 0:nt, k]))
                dve.tensor_tensor(rsc[:, 2, 0:nt], em8[:, 0:nt, 1], em8[:, 0:nt, 0], ALU.subtract).then_inc(gmax_ready, 1)
                for k in range(2):
                    for n in range(nt):
                        link(dve.tensor_scalar(M1[:, k, n * NE:(n + 1) * NE], iota[:, 0:NE], rsc[:, 5 + k, n:n + 1], None, ALU.is_equal))
                dve.tensor_tensor(M1[:, 2, 0:nt * NE], M1[:, 0, 0:nt * NE], M1[:, 1, 0:nt * NE], ALU.add).then_inc(m_ready, 1)
                dve.wait_ge(gexp_ready, l + 1)
                link(dve.scalar_tensor_tensor(rsc[:, 8, 0:nt], rsc[:, 3, 0:nt], 1.0, rsc[:, 1, 0:nt], ALU.add, ALU.mult))
                link(dve.reciprocal(wts[:, 0:nt, 0], rsc[:, 8, 0:nt]))
                link(dve.tensor_tensor(wts[:, 0:nt, 1], wts[:, 0:nt, 0], rsc[:, 3, 0:nt], ALU.mult))
                dve.wait_ge(pos_mm, l + 1)
                cnt = ps[:, 1, nt * NE:(nt + 1) * NE]
                link(dve.tensor_scalar(cum[:, 0, :], cnt, 0.0, None, ALU.is_gt))
                for q in range(1, nt * P // SLOTS):
                    link(dve.scalar_tensor_tensor(cum[:, 0, :], cnt, float(SLOTS * q), cum[:, 0, :], ALU.is_gt, ALU.add))
                cur = cum[:, 0, :]
                for q in range(5):
                    nxt, s = cum[:, 1 + q % 2, :], 1 << q
                    link(dve.tensor_copy(nxt[:, 0:s], cur[:, 0:s]))
                    link(dve.tensor_tensor(nxt[:, s:NE], cur[:, s:NE], cur[:, 0:NE - s], ALU.add))
                    cur = nxt
                ends = cur[0:1, :].unsqueeze(1).broadcast_to([1, MAXB, NE])
                blocks = iota[0:1, 0:MAXB].unsqueeze(2).broadcast_to([1, MAXB, NE])
                link(dve.tensor_tensor(blk_cmp, ends, blocks, ALU.is_le))
                link(dve.tensor_reduce(blkf[0:1, 0:MAXB], blk_cmp, AX_X, ALU.add))
                link(dve.tensor_scalar(blkf[0:1, 0:MAXB], blkf[0:1, 0:MAXB], float(NE - 1), None, ALU.min))
                link(dve.tensor_scalar(halves[:, 0:1], cur[:, NE - 1:NE], 0.5, None, ALU.mult))
                link(dve.tensor_scalar(below, iota[:, 0:MAXB // 2], halves[:, 0:1], None, ALU.is_lt))
                link(dve.tensor_reduce(halves[:, 0:1], below, AX_X, ALU.add))
                link(dve.tensor_scalar(fresh, iota[0:1, 0:MAXB], halves[0:1, 0:1], None, ALU.is_equal))
                link(dve.memset(fresh[:, 0:1], 1.0))
                link(dve.tensor_tensor(blk_cmp[:, 0:2, :].rearrange("p a b -> p (a b)")[:, 0:MAXB - 1], blkf[0:1, 1:MAXB], blkf[0:1, 0:MAXB - 1], ALU.not_equal))
                link(dve.tensor_tensor(fresh[:, 1:MAXB], fresh[:, 1:MAXB], blk_cmp[:, 0:2, :].rearrange("p a b -> p (a b)")[:, 0:MAXB - 1], ALU.max))
                link(dve.tensor_copy(blki[0:1, NEW:NEW + MAXB], fresh))
                link(dve.tensor_copy(blki[0:1, MAXB:MAXB + 1], halves[0:1, 0:1]))
                link(dve.tensor_scalar(blkf[0:1, MAXB + 1:MAXB + 2], halves[0:1, 0:1], -1.0, float(MAXB // 2 + 1), ALU.mult, ALU.add))
                link(dve.tensor_copy(blki[0:1, MAXB + 1:MAXB + 2], blkf[0:1, MAXB + 1:MAXB + 2]))
                dve.tensor_copy(blki[0:1, 0:MAXB], blkf[0:1, 0:MAXB]).then_inc(plan_ready, 1)
                link(dve.tensor_scalar(halves[:, 1:2], halves[:, 0:1], float(SLOTS), None, ALU.mult))
                link(dve.tensor_copy(iota2[:, 0:SLOTS], iota[:, 0:SLOTS]))
                link(dve.tensor_scalar(iota2[:, SLOTS:PAIR], iota[:, 0:SLOTS], halves[:, 1:2], None, ALU.add))
                link(dve.tensor_tensor(cum[:, 3, :], cur, cum[:, 0, :], ALU.subtract))
                for n in range(nt):
                    link(dve.scalar_tensor_tensor(lg[:, n, 0:NE], cum[:, 3, :], float(SLOTS), ps[:, 1, n * NE:(n + 1) * NE], ALU.mult, ALU.add))
                for k in range(2):
                    mk = M1[:, k, 0:nt * NE].rearrange("p (n e) -> p n e", n=nt)
                    link(dve.tensor_tensor(mk, mk, lg[:, 0:nt, 0:NE], ALU.mult))
                    link(dve.tensor_reduce(slotf[:, 0:nt, k], mk, AX_X, ALU.add))
                link(dve.tensor_copy(sloti[:, 0:2 * nt].rearrange("p (n k) -> p n k", k=2), slotf[:, 0:nt, :]))
                dve.wait_ge(plan_ready, l + 1)
                pairs = dve.value_load(blki[0:1, MAXB:MAXB + 1], min_val=1, max_val=MAXB // 2)

                def build(count):
                    for n in range(nt):
                        dve.tensor_scalar(sel[:, n, :], iota2, slotf[:, n, 0:1], None, ALU.is_equal).then_inc(sems["moe_chain"], 1)
                    dve.wait_ge(sems["moe_chain"], count + nt)
                    for n in range(nt):
                        dve.scalar_tensor_tensor(sel[:, n, :], iota2, slotf[:, n, 1:2], sel[:, n, :], ALU.is_equal, ALU.add).then_inc(
                            sems["moe_chain"], 1)
                    dve.wait_ge(sems["moe_chain"], count + 2 * nt)
                    dve.tensor_scalar(slotf[:, 0:nt, :], slotf[:, 0:nt, :], float(SLOTS), None, ALU.subtract).then_inc(sems["sel_ready"], 1)

                build(0)
                with dve.Fori(0, pairs) as i:
                    dve.wait_ge(sems["sel_ready"], i + 1)
                    dve.wait_ge(sems["xg_mm"], i + 1)
                    build(2 * nt + 2 * nt * i)
                    dve.wait_ge(sems["sg_ready"], i + 1)
                    dve.wait_ge(sems["gu_mm"], 2 * i + 4)
                    dve.tensor_tensor(htmp, silu_g, ps[:, 3, :], ALU.mult).then_inc(sems["hid_ready"], 1)
                    dve.wait_ge(sems["hidt_mm"], i + 1)
                    dve.tensor_copy(hid, ps[:, 4, :].rearrange("p (m s) -> p m s", m=EC)).then_inc(sems["hidt_ready"], 1)
                dve.wait_ge(sems["xg_mm"], pairs + 1)
                dve.wait_ge(sems["sel_ready"], pairs + 1)
                dve.sem_inc(sel_over, 1)
                for n in range(nt + 1):
                    if n < nt:
                        dve.wait_ge(yg_in[l][n], 32)
                        link(dve.tensor_scalar(yg[:, n, 0, :], yg[:, n, 0, :], wts[:, n, 0:1], None, ALU.mult))
                        dve.scalar_tensor_tensor(yg[:, n, 0, :], yg[:, n, 1, :], wts[:, n, 1:2], yg[:, n, 0, :], ALU.mult, ALU.add).then_inc(mix_ready, 1)
                    if n >= 1:
                        m, t = n - 1, (0, NTM)[l] + n - 1
                        dve.wait_ge(yt_mm, t + 1)
                        for k in range(KC):
                            x = xT[:, m // 2, k, (m % 2) * P:(m % 2) * P + P]
                            ins = dve.scalar_tensor_tensor(x, ps[:, 2 * (m % 2) + k // 4, (k % 4) * P:(k % 4 + 1) * P], modv[:, l, 40 + k, m // 2:m // 2 + 1], x,
                                                           ALU.mult, ALU.add)
                        ins.then_inc(x2_ready, 1)

            block1(0)
            experts(0)
            block1(1)
            experts(1)
            dve.wait_ge(x2_ready, 6)
            dve.sem_inc(xo_ready, KC)

            def layer2(i):
                call = 4 + 2 * i
                chain2 = [0]

                def link2(ins):
                    chain2[0] += 1
                    ins.then_inc(d2chain, 1)
                    dve.wait_ge(d2chain, LINKS2 * i + chain2[0])

                dve.wait_ge(lpars_in, 16)
                link2(dve.tensor_copy(lpar[:, :], lpars[:, bass.ds(i * n_lp, n_lp)]))
                norm(call, False, lambda k: lp("norm_g", k, 1))
                for c in range(6):
                    dve.wait_ge(r2_mm, 10 * i + c // 2 * 2 + 2)
                    t = sqb[:, 3, (c % 2) * NX:(c % 2) * NX + NX]
                    src, dst = (qp[:, c, :], qr[:, c, :]) if c < 4 else (kv[:, c - 3, :], kv[:, c - 3, :])
                    dve.tensor_tensor(t, ps[:, 4 + c // 2, (c % 2) * NX:(c % 2) * NX + NX], sin2, ALU.mult)
                    link2(dve.tensor_tensor(dst, src, cos2, ALU.mult))
                    dve.tensor_tensor(dst, dst, t, ALU.add).then_inc(r2_ready, 1)
                link2(dve.memset(win[0], 0.0))
                link2(dve.memset(win[1], 0.0))
                for v in range(2):
                    dve.wait_ge(r2_mm, 10 * i + 8)
                    dve.tensor_copy(win[v][:, :, NCMP], lp("pe", v * (CB // 2), CB // 2))
                    for o in range(2):
                        rows_ = ps[o * DH:o * DH + DH, 4, v * NX:v * NX + NX].rearrange("p (c j o) -> p j c o", j=8, o=2)
                        for jh in range(2):
                            ins = dve.tensor_copy(win[v][o * DH:o * DH + DH, 8 * jh:8 * jh + 8, 0:NCMP], rows_[:, :, jh:jh + NCMP, o])
                    ins.then_inc(r2_ready, 1)
                for c in range(2):
                    dve.wait_ge(r2_mm, 10 * i + 10)
                    dve.tensor_copy(kdup[:, c, :], ps[:, 5, c * NX:c * NX + NX]).then_inc(r2_ready, 1)
                dve.wait_ge(cmp_mm, 4 * i + 4)
                dve.tensor_copy(kcmp[:, :], ps[:, 4, 0:NCMP])
                for hh in range(4):
                    ins = dve.tensor_copy(vblk[32 * hh:32 * hh + NCMP, hh, :], ps[32 * hh:32 * hh + NCMP, 4, 64:128])
                ins.then_inc(cev_ready, 1)
                dve.wait_ge(cs_mm, i + 1)
                maskc = cc("maskc").rearrange("p (q c) -> p q c", q=QT)
                visc = cc("visc").rearrange("p (q c) -> p q c", q=QT)
                rows_c = scmp.rearrange("p q h c -> p (q h) c")
                for q in range(QT):
                    for o in range(2):
                        link2(dve.tensor_tensor(scmp[:, q, o:HEADS:2, :],
                                                ps[:, 5 + o, q * 64:q * 64 + 64].rearrange("p (h c) -> p h c", h=HEADS // 2)[:, :, 0:NCMP],
                                                maskc[:, q, :].unsqueeze(1).broadcast_to([P, HEADS // 2, NCMP]), ALU.add))
                link2(dve.tensor_reduce(cst[:, 0, :], rows_c, AX_X, ALU.max))
                dve.tensor_tensor(rows_c, rows_c, cst[:, 0, :].unsqueeze(2).broadcast_to([P, QT * HEADS, NCMP]), ALU.subtract).then_inc(pcn_ready, 1)
                dve.wait_ge(pce_ready, i + 1)
                link2(dve.tensor_reduce(cst[:, 1, :], rows_c, AX_X, ALU.add))
                link2(dve.reciprocal(cst[:, 1, :], cst[:, 1, :]))
                link2(dve.tensor_tensor(cst[:, 2, :].rearrange("p (q h) -> p q h", q=QT), cst[:, 1, :].rearrange("p (q h) -> p q h", q=QT),
                                        gates[:, :, :].rearrange("p q (h g) -> p q h g", g=3)[:, :, :, 0], ALU.mult))
                link2(dve.tensor_tensor(rows_c, rows_c, cst[:, 2, :].unsqueeze(2).broadcast_to([P, QT * HEADS, NCMP]), ALU.mult))
                for q in range(QT):
                    ins = dve.tensor_tensor(pcp[:, q, :, 0:NCMP], scmp[:, q, :, :], visc[:, q, :].unsqueeze(1).broadcast_to([P, HEADS, NCMP]), ALU.mult)
                ins.then_inc(pcn_ready, 1)
                dve.wait_ge(sbz_mm, i + 1)
                dve.wait_ge(sb_act, 5 * i + 1)
                masks = mneg[:, :].unsqueeze(1).broadcast_to([P, SBH, P])
                keep = cc("m01").unsqueeze(1).broadcast_to([P, SBH, P])
                dve.tensor_tensor(zs[:, :, 0:P], ps[:, 0:SBH, 0:P], masks, ALU.add)
                dve.tensor_copy(zs[:, :, P:NX], ps[:, 0:SBH, P:NX])
                dve.tensor_tensor(zs[:, :, NX:384], ps[:, 0:SBH, NX:384], masks, ALU.add)
                dve.wait_ge(sb_act, 5 * i + 3)
                link2(dve.scalar_tensor_tensor(spl, ps[:, 0:SBH, 0:384], 0.0, spl, ALU.max, ALU.add))
                dve.tensor_tensor(spl[:, :, 0:P], spl[:, :, 0:P], keep, ALU.mult)
                dve.tensor_tensor(spl[:, :, NX:384], spl[:, :, NX:384], keep, ALU.mult).then_inc(sb_dve, 1)
                dve.wait_ge(sbc_mm, i + 1)
                dve.tensor_tensor(zs, zs, ps[:, 4:8, 0:384], ALU.add).then_inc(sb_dve, 1)
                for s in range(2 * HEADS + 1):
                    if s < 2 * HEADS:
                        n, u, k = 40 + 16 * i + s, s % 2, P * (s % 2 + 1)
                        ins, _ = unit_max(n, u, ps[:, u, :].rearrange("p (b k) -> p b k", b=2)[:, :, 0:k], SC_A)
                        link2(ins)
                        dve.tensor_scalar(nb[:, u, :], mx[:, u, :], -SC_A, None, ALU.mult).then_inc(nb_ready, 1)
                    if s >= 1:
                        n, h, u = 40 + 16 * i + s - 1, (s - 1) // 2, (s - 1) % 2
                        k = P * (u + 1)
                        dve.wait_ge(ex_ready, n + 1)
                        link2(dve.reciprocal(sm[:, u, :], sm[:, u, :]))
                        link2(dve.tensor_tensor(sm[:, u, :], sm[:, u, :], gates[:, u, 3 * h + 1:3 * h + 3], ALU.mult))
                        for b in range(2):
                            p = prob[:, u, b * NX:b * NX + k]
                            ins = dve.tensor_scalar(p, p, sm[:, u, b:b + 1], None, ALU.mult)
                        ins.then_inc(pn_ready, 1)
                for m in range(KC):
                    dve.wait_ge(y2_mm, KC * i + m + 1)
                    dve.wait_ge(mgs_ready, KC // 2 * i + m // 2 + 1)
                    dve.tensor_tensor(mg[:, m, :], mg[:, m, :], ps[:, m % 4, 0:NX], ALU.mult)
                    link2(dve.tensor_tensor(mg[:, KC + m, :], mg[:, KC + m, :], ps[:, m % 4, NX:512], ALU.mult))
                    dve.tensor_tensor(mixT[:, m, :], mg[:, m, :], mg[:, KC + m, :], ALU.add).then_inc(mix2_ready, 1)

                def out_norm(c):
                    dve.wait_ge(nstd_ready, 2 * i + c + 1)
                    link2(dve.reciprocal(stdv[:, 0:NX], stdv[:, 0:NX]))
                    for k in range(KC):
                        link2(dve.scalar_tensor_tensor(yres[:, k, :], yres[:, k, :], lp("norm_g", (2 * c + 1) * KC + k, 1), stdv[:, 0:NX], ALU.mult, ALU.mult))
                        dve.tensor_tensor(xT[:, 0, k, :], xT[:, 0, k, :], yres[:, k, :], ALU.add).then_inc(xo_ready, 1)

                def parts(hi, lo, x):
                    link2(dve.tensor_copy(hi, x))
                    return dve.tensor_tensor(lo, x, hi.bitcast(F32), ALU.subtract)

                def split_slab(n):
                    j = J_FF + n
                    dve.wait_ge(slab_in[j % RING], slab2_count(i, j))
                    if n >= 2:
                        s, per, v = ff_used(*FF_ORDER[n - 2])[0]
                        dve.wait_ge(s, i * per + v)
                    parts(w_hi[:, n % 2, :], w_lo[j % RING][:, :], ring[:, j % RING, :]).then_inc(split_ready, 1)

                def split_h(ins, k):
                    link2(ins)
                    parts(hn_hi[:, k, :], hn_lo[:, k, :], hT[:, 0, k, :]).then_inc(h_ready, 1)

                for n in range(2):
                    split_slab(n)
                out_norm(0)
                norm(call + 1, False, lambda k: lp("norm_g", 2 * KC + k, 1), split_h)
                for n, (w, j) in enumerate(FF_ORDER):
                    if w == 1:
                        if j >= 2:
                            dve.wait_ge(f2_mm, 7 * i + 7 + j - 1)
                        for m in range(4 * j, 4 * j + 4):
                            dve.wait_ge(ffh_ready, 32 * i + m + 1)
                            parts(ff_hi[:, m % 8, :], ff_lo[:, m % 8, :], sqb[:, m % 4, 0:NX]).then_inc(ffs_ready, 1)
                    if n + 2 < len(FF_ORDER):
                        split_slab(n + 2)
                out_norm(1)
                assert chain2[0] == LINKS2, chain2[0]

            with dve.Fori(0, 2) as i:
                layer2(i)

        @block.gpsimd
        def _(pool):
            pool.wait_ge(plan_ready, 1)
            pool.memset(zrows, 0.0).then_inc(zrows_ready, 1)
            pairs = pool.value_load(blki[0:1, MAXB:MAXB + 1], min_val=1, max_val=MAXB // 2)
            pool.wait_ge(zrows_ready, 1)
            with pool.Fori(pairs, MAXB // 2 + 1) as i:
                pool.dma_start(y_rows[bass.ds(i * PAIR, PAIR), :], zrows).then_inc(tail_stored, 16)
            tail = pool.value_load(blki[0:1, MAXB + 1:MAXB + 2], min_val=1, max_val=MAXB // 2)
            pool.wait_ge(tail_stored, 16 * tail)
            pool.sem_inc(zrows_ready, 1)
            for l in range(2):
                pool.wait_ge(stored_all, l + 1)
                pool.wait_ge(sel_over, l + 1)
                for n in range(NTM if l == 0 else QT):
                    for k in range(2):
                        pool.indirect_dma_start(out=yg[:, n, k, :], out_offset=None, in_=y_rows,
                                                in_offset=bass.IndirectOffsetOnAxis(ap=sloti[:, 2 * n + k:2 * n + k + 1], axis=0)).then_inc(yg_in[l][n], 16)


def constants():
    import numpy as np

    p, f = np.arange(P)[:, None], np.arange(P)[None, :]
    t = {}
    t["ident"] = p == f
    t["headones"] = p // DH == f // DH
    half = DH // 2
    rot = np.zeros((P, P), np.float32)
    rot_b = np.zeros((P, P), np.float32)
    for m in range(P):
        d = m % DH
        if d < half:
            rot[m + half, m] = -1
        else:
            rot[m - half, m] = 1
        if d < 8:
            rot_b[m + 8, m] = -1
        elif d < 16:
            rot_b[m - 8, m] = 1
    t["rot_a"], t["rot_b"] = rot, rot_b
    t["swap"] = (p + DH) % P == f
    t["dup0"] = p == f % DH
    t["dup1"] = p == DH + f % DH
    t["tri_strict"] = p < f
    t["negtri"] = -(p >= f).astype(np.float32)
    t["trineg"] = np.where(f > p, NEG, 0.0)
    t["band1"] = np.where(f < p, NEG, 0.0)
    t["m01"] = p < f
    t["iota"] = np.broadcast_to(f, (P, P))
    tok = np.arange(NX)
    inv = np.float32(10000.0) ** (-np.arange(DH // 4, dtype=np.float32) / np.float32(DH // 4))
    ang = np.concatenate([(tok // 64).astype(np.float32)[:, None] * inv, (tok % 64).astype(np.float32)[:, None] * inv], axis=1)
    t["cos"] = np.cos(ang).T[np.arange(P) % half]
    t["sin"] = np.sin(ang).T[np.arange(P) % half]
    c, q = np.arange(NCMP)[None, None, :], np.arange(QT)[None, :, None]
    vis = CS * c + CB - 1 <= q * P + np.arange(P)[:, None, None]
    t["maskc"] = np.where(vis, 0.0, NEG).reshape(P, -1)
    t["visc"] = vis.reshape(P, -1)
    d = np.arange(P) % DH
    inv2 = np.power(np.float32(500000.0), np.arange(8, dtype=np.float32) * np.float32(-2.0 / 16))
    t["invf"] = np.where(d < 16, inv2[d % 8], 0.0)[:, None]
    t["eps"] = np.full((P, 1), EPS)
    t["fold"] = p % 32 == np.arange(16)[None, :]
    return np.concatenate([np.asarray(t[n], np.float32).reshape(P, w) for n, w in CONSTS], axis=1)


def window_lengths():
    import numpy as np

    t = np.arange(NX)
    inv = [1.0 / (np.clip(t - w // 2 + w, 0, NX) - np.clip(t - w // 2, 0, NX)).astype(np.float32) for w in POOLS]
    return np.ascontiguousarray(np.broadcast_to(np.stack(inv)[None], (P, BC, NX)), np.float32)


def kernel(**inputs):
    import numpy as np
    import concourse.bacc as bacc
    from concourse.bass_utils import run_bass_kernel_spmd

    a = {k: np.asarray(v) for k, v in inputs.items()}

    def cols(v):
        v = v.reshape(-1, v.shape[-1] // P, P)
        return v.transpose(2, 0, 1).reshape(P, -1)

    def fill(v):
        return np.broadcast_to(v.reshape(1, -1), (P, v.size))

    cond = np.stack([a["c"][0], a["c_ctx"]])
    head = lambda v: np.tile(v[0], 2).reshape(P, 1)
    rt_w = np.concatenate([a["rt_grp_w"], a["rt_exp_w"]], axis=2)
    small = {
        "cond": cond.reshape(2, KC, P).transpose(2, 1, 0).reshape(P, -1),
        "mod_b": cols(a["mod_b"]), "ln1_g": cols(a["ln1_g"]), "ln2_g": cols(a["ln2_g"]),
        "qn_a": head(a["q_norm_a"]), "kn_a": head(a["k_norm_a"]), "qn_c": head(a["q_norm_c"]), "kn_c": head(a["k_norm_c"]),
        "conv_w": a["conv_w"][0].reshape(TAPS, BC, P).transpose(2, 1, 0).reshape(P, -1),
        "conv_b": cols(a["conv_b"]), "cln_g": cols(a["conv_ln_g"]), "cln_b": cols(a["conv_ln_b"]),
        "sink": fill(a["sink_c"]), "pool_scale": cols(a["pool_scale"]),
        "rt_w": rt_w.reshape(2, KC, P, RL).transpose(2, 0, 1, 3).reshape(P, -1),
        "rt_b": fill(np.concatenate([a["rt_grp_b"], a["rt_exp_b"]], axis=1)),
    }
    params = np.concatenate([small[n].reshape(P, w) for n, w in PARAMS], axis=1)
    layer = {
        "norm_g": a["norm_g_2"].reshape(2, 4 * KC, P).transpose(0, 2, 1),
        "pe": a["cmp_pe_2"].reshape(2, 2, CB // 2, P).transpose(0, 3, 1, 2).reshape(2, P, -1),
        "w2": a["cmp_w2_2"].reshape(2, 2, 2, P, DH).transpose(0, 3, 1, 2, 4).reshape(2, P, -1),
    }
    lparams = np.concatenate([layer[n] for n, _ in LPARAMS], axis=2)
    x_in = np.stack([a["x"][0], a["ctx"][0]]).reshape(TG, NX, KC, P).transpose(3, 0, 2, 1)
    arrays = {
        "x_in": x_in, "params": params, "consts": constants(), "invcnt": window_lengths(), "lparams": lparams,
        "pos": np.broadcast_to(a["positions_2"].astype(np.int32), (P, NX)), "mod_w": a["mod_w"],
        "w_in_ab": a["w_in_ab"][0], "w_out_ab": a["w_out_ab"][0], "w_in_cd": a["w_in_cd"][0], "w_out_cd": a["w_out_cd"][0],
        "pool_w": a["pool_w"][0], "ex_gate": a["ex_gate"], "ex_up": a["ex_up"], "ex_down": a["ex_down"], "w_in_2": a["w_in_2"],
        "cmp_w1": a["cmp_w1_2"], "w_nsa_o": a["w_nsa_o_2"], "w_sb_o": a["w_sb_o_2"], "w_out_2": a["w_out_2"],
        "w_ff1": a["w_ff1_2"], "w_ff2": a["w_ff2_2"],
    }
    arrays = {f"in_{n}": np.ascontiguousarray(v) for n, v in arrays.items()}
    nc = bacc.Bacc("TRN2", target_bir_lowering=False, num_devices=1, dynamic_dma_scratch_size=8192)
    args = [nc.dram_tensor(n, v.shape, mybir.dt.from_np(v.dtype), kind="ExternalInput").ap() for n, v in arrays.items()]
    out = nc.dram_tensor("out_T", (P, KC, NX), F32, kind="ExternalOutput").ap()
    y_rows = nc.dram_tensor("y_rows", (MAXB * SLOTS + PAIR, D), F32, kind="Internal").ap()
    hybrid_program(nc, *args, out, y_rows)
    got = run_bass_kernel_spmd(nc, [arrays], core_ids=[0]).results[0]["out_T"]
    return np.asarray(got).transpose(2, 1, 0).reshape(1, NX, D)
```

```python
from contextlib import ExitStack

import concourse.bass as bass
from concourse import mybir

F32 = mybir.dt.float32
FR = mybir.dt.float32r
I32 = mybir.dt.int32
U32 = mybir.dt.uint32
ALU = mybir.AluOpType
ACT = mybir.ActivationFunctionType
AX_X = mybir.AxisListType.X

P = 128
D = 1024
KC = D // P
NX = 256
TG = 2
QT = NX // P
EPS = 1e-6
NEG = -1e30

HEADS = 8
DH = 64
SC_A = DH ** -0.5
QC = HEADS * DH // P
QKC = QC + 1
TAPS = 31
HALO = TAPS // 2
BC = 4
POOLS = (2, 4, 8, 16)
PPAD = 8
NG, NE, DE = 4, 32, 512
EC = DE // P
RL = NG + NE
SLOTS = 64
PAIR = 2 * SLOTS
MAXB = 48

CB, CS = 32, 16
NCMP = (NX - CB) // CS + 1
CPAD = 32
SBH, SBD = 4, 128
SC_B = SBD ** -0.5
FF = 4 * D
IN_W = 512 + 6 * 64 + 24 + 3 * 512 + 2 * D
COL_SB = 512 + 6 * 64 + 24
COL_MG = COL_SB + 3 * 512
TWO_PI = 6.283185307179586
C1 = 6.28125
C2 = 0.0019350051879882812
C3 = TWO_PI - C1 - C2
LINKS2 = 157
MAGIC = 12582912.0

PARAMS = [("cond", 2 * KC), ("mod_b", 2 * 48), ("ln1_g", 2 * KC), ("ln2_g", 2 * KC), ("qn_a", 1), ("kn_a", 1),
          ("conv_w", BC * TAPS), ("conv_b", BC), ("cln_g", BC), ("cln_b", BC), ("qn_c", 1), ("kn_c", 1),
          ("sink", HEADS), ("pool_scale", BC), ("rt_w", 2 * KC * RL), ("rt_b", 2 * RL)]
CONSTS = [("ident", P), ("headones", P), ("rot_a", P), ("swap", P), ("rot_b", P), ("dup0", P), ("dup1", P),
          ("tri_strict", P), ("negtri", P), ("trineg", P), ("band1", P), ("m01", P), ("iota", P),
          ("cos", NX), ("sin", NX), ("maskc", QT * NCMP), ("visc", QT * NCMP), ("invf", 1), ("eps", 1), ("fold", 16)]
LPARAMS = [("norm_g", 4 * KC), ("pe", 2 * (CB // 2)), ("w2", 2 * 2 * 64)]


def offsets(layout):
    out, at = {}, 0
    for name, n in layout:
        out[name] = (at, n)
        at += n
    return out, at


RING = 6
SLAB = 4096


def hybrid_program(nc, xT_in, params_in, consts_in, invcnt_in, lparams_in, pos_in, mod_w, w_in_ab, w_out_ab, w_in_cd,
                   w_out_cd, pool_w, ex_gate, ex_up, ex_down, w_in_2, cmp_w1, w_nsa_o, w_sb_o, w_out_2, w_ff1, w_ff2,
                   outT, y_rows):
    po, n_par = offsets(PARAMS)
    co, n_con = offsets(CONSTS)
    lo, n_lp = offsets(LPARAMS)
    ctx = ExitStack()
    with ctx:
        address = {}

        def sb(name, shape, dt=F32):
            address[name] = -(-nc.sbuf_base // 32) * 32
            return ctx.enter_context(nc.sbuf_tensor(name, shape, dt))

        def rounded(name, shape, over, column):
            return nc.alloc_sbuf_tensor_at(name, shape, FR, offset=address[over] + 4 * column)

        def sem(name):
            return ctx.enter_context(nc.semaphore(name))

        ring = sb("ring", [P, RING, SLAB])
        xT = sb("xT", [P, TG, KC, NX])
        hT = sb("hT", [P, TG, KC, NX])
        cat = sb("cat", [P, 8, 512])
        sqb = sb("sqb", [P, 4, 512])
        E = sb("E", [P, 9216])
        par = sb("par", [P, n_par])
        con = sb("con", [P, n_con])
        lpar = sb("lpar", [P, n_lp])
        ones = sb("ones", [P, P])
        negones = sb("negones", [P, P])
        mneg = sb("mneg", [P, P])
        stdv = sb("stdv", [P, 512])
        modv = sb("modv", [P, 2, 48, 2])
        scale1 = sb("scale1", [P, 2, KC, 2])
        scale2 = sb("scale2", [P, 2, KC, 2])
        condv = sb("condv", [P, KC, 32])
        mrow = E[:, 6144:6656]
        mx = sb("mx", [P, 3, 2])
        nb = sb("nb", [P, 3, 2])
        sm = sb("sm", [P, 3, 2])
        es = sb("es", [P, 3, 1])
        ps = ctx.enter_context(nc.psum_tensor("ps", [P, 8, 512], F32))

        def pc(name, a=0, n=None):
            at, w = po[name]
            return par[:, at + a:at + (w if n is None else a + n)]

        def cc(name):
            at, w = co[name]
            return con[:, at:at + w]

        def lp(name, a, n):
            at, w = lo[name]
            return lpar[:, at + a:at + a + n]

        lpars = par[:, po["rt_w"][0]:po["rt_w"][0] + 2 * n_lp]
        assert po["rt_w"][0] + 2 * n_lp <= n_par

        ident = cc("ident")

        def e3(at, a, b):
            return E[:, at:at + a * b].rearrange("p (a b) -> p a b", a=a)

        qk = e3(0, QKC, 512)
        kswap = E[:, 2560:3072]
        vtok = e3(3072, 4, P)
        GP = NX + 2 * HALO
        gpad = E[:, 3584:3584 + BC * TG * GP].rearrange("p (c g t) -> p c g t", c=BC, g=TG)
        UP = NX + 2 * PPAD
        upad = e3(3584, BC, UP)
        pwin = e3(3584 + BC * UP, 2, UP)
        pt_pool = e3(3584 + (BC + 2) * UP, BC, NX)
        invcnt = cat[:, 4:8, NX:512]
        prob3 = e3(6656, 3, 512)
        prob = prob3[:, 1:3, :]
        probT = E[:, 8192:9216].rearrange("p (u b q) -> p u b q", u=2, b=4)
        NTM = 4
        tok_hi = rounded("tok_hi", [P, NTM, D], "cat", 0)
        tok_lo = [rounded("tok_lo0", [P, QT, D], "E", 6144), rounded("tok_lo1", [P, QT, D], "sqb", 0)]
        sel = rounded("sel", [P, NTM, PAIR], "E", 0)
        xtok = hT[:, 0, 0:4, :].rearrange("p k t -> p (k t)")
        xg = E[:, 1024:2048].rearrange("p (k s) -> p k s", k=KC)
        silu_g = E[:, 2048:2048 + DE]
        htmp = E[:, 4096:4096 + DE]
        hid = E[:, 2560:2560 + EC * PAIR].rearrange("p (m s) -> p m s", m=EC)
        yb = E[:, 3072:3072 + D]
        blk_cmp = E[0:1, 3072:3072 + MAXB * NE].rearrange("p (b e) -> p b e", b=MAXB)
        zrows = E[:, 5120:5120 + D]
        rtp = E[:, 5120:5632]
        yg = E[:, 0:8192].rearrange("p (n k d) -> p n k d", n=NTM, k=2)
        lg = E[:, 8192:8336].rearrange("p (n r) -> p n r", n=NTM)
        lgp = e3(8336, NTM, 8)
        gm8 = e3(8368, NTM, 8)
        em8 = e3(8400, NTM, 8)
        pen = e3(8432, NTM, NG)
        rsc = e3(8448, 12, NTM)
        cum = e3(8496, 4, NE)
        M1 = e3(8624, 3, NTM * NE)
        gi8 = sb("gi8", [P, NTM, 8], U32)
        ei8 = sb("ei8", [P, NTM, 8], U32)
        slotf = sb("slotf", [P, NTM, 2])
        sloti = sb("sloti", [P, NTM * 2], I32)
        wts = sb("wts", [P, NTM, 2])
        blkf = sb("blkf", [1, MAXB + 2])
        blki = sb("blki", [1, 2 * MAXB + 3], I32)
        NEW = MAXB + 2
        fresh = E[0:1, 2560:2560 + MAXB + 1]
        below = E[:, 2624:2624 + MAXB // 2]
        halves = E[:, 2656:2658]
        iota2 = E[:, 4608:4608 + PAIR]
        lane_step = E[:, 4736:4736 + PAIR]
        qp = xT[:, 1, 0:4, :]
        qr = xT[:, 1, 4:8, :]
        sbq = hT[:, 1, 0:4, :]
        sbk = hT[:, 1, 4:8, :]
        kv = e3(0, 3, NX)
        kdup = e3(768, 2, NX)
        vsw = e3(1280, QT, P)
        win = [E[:, at:at + 512].rearrange("p (j c) -> p j c", j=CB // 2) for at in (1536, 8704)]
        hrow = sqb[:, 0, :]
        sbv = e3(2048, QT, 512)
        mg = e3(3072, 16, NX)
        w_hi = rounded("w_hi", [P, 2, SLAB], "E", 0)
        w_lo = [rounded(f"w_lo{r}", [P, SLAB], "ring", r * SLAB) for r in range(RING)]
        hn_hi = rounded("hn_hi", [P, KC, NX], "hT", KC * NX)
        hn_lo = rounded("hn_lo", [P, KC, NX], "hT", 0)
        ff_hi = rounded("ff_hi", [P, 8, NX], "xT", KC * NX)
        ff_lo = rounded("ff_lo", [P, 8, NX], "cat", 4 * 512)
        onsa = cat[:, 0:2, :].rearrange("p a (b t) -> p (a b) t", b=2)
        osb = cat[:, 2:4, :].rearrange("p a (b t) -> p (a b) t", b=2)
        mixT = cat[:, 4:8, :].rearrange("p a (b t) -> p (a b) t", b=2)
        trig = sb("trig", [P, 2, NX])
        cos2, sin2 = trig[:, 0, :], trig[:, 1, :]
        gates = sb("gates", [P, QT, 24])
        hcmp = sb("hcmp", [P, 4, 16])
        gcmp = sb("gcmp", [P, 4, NCMP])
        kcmp = sb("kcmp", [P, NCMP])
        vblk = sb("vblk", [P, 4, 64])
        pcp = sb("pcp", [P, QT, HEADS, CPAD])
        scmp = sqb[:, 2, 0:QT * HEADS * NCMP].rearrange("p (q h c) -> p q h c", q=QT, h=HEADS)
        pcT = sqb[:, 1, :].rearrange("p (b q) -> p b q", b=4)
        zs = E[:, 7168:7168 + SBH * 384].rearrange("p (h c) -> p h c", h=SBH)
        spl = cat[:, 4:7, :].rearrange("p a b -> p (a b)").rearrange("p (h c) -> p h c", h=SBH)
        yres = cat[:, 0:4, :].rearrange("p a (b t) -> p (a b) t", b=2)
        cst = sb("cst", [P, 3, QT * HEADS])

        inputs_in = sem("inputs_in")
        slab_in = [sem(f"slab_in{r}") for r in range(RING)]
        setup_done = sem("setup_done")
        cond_ready = sem("cond_ready")
        mod_mm = sem("mod_mm")
        mod_ev = sem("mod_ev")
        mod_fold = sem("mod_fold")
        mod_ready = sem("mod_ready")
        sq_ready = sem("sq_ready")
        ssq_mm = sem("ssq_mm")
        std_ready = sem("std_ready")
        rstd_ready = sem("rstd_ready")
        xn_ready = sem("xn_ready")
        h_ready = sem("h_ready")
        proj_mm = sem("proj_mm")
        proj_ev = sem("proj_ev")
        qsq_ready = sem("qsq_ready")
        qss_mm = sem("qss_mm")
        qstd_ready = sem("qstd_ready")
        qn_ready = sem("qn_ready")
        rot_mm = sem("rot_mm")
        rope_ready = sem("rope_ready")
        swap_mm = sem("swap_mm")
        swap_ev = sem("swap_ev")
        sc_mm = sem("sc_mm")
        nb_ready = sem("nb_ready")
        ex_ready = sem("ex_ready")
        pn_ready = sem("pn_ready")
        tr_mm = sem("tr_mm")
        pt_ready = sem("pt_ready")
        pv_mm = sem("pv_mm")
        o_ready = sem("o_ready")
        sink_ready = sem("sink_ready")
        conv_ready = sem("conv_ready")
        cmu_mm = sem("cmu_mm")
        cd_ready = sem("cd_ready")
        csq_ready = sem("csq_ready")
        cvar_mm = sem("cvar_mm")
        cstd_ready = sem("cstd_ready")
        cn_ready = sem("cn_ready")
        bx_ready = sem("bx_ready")
        pool_ready = sem("pool_ready")
        pool_mm = sem("pool_mm")
        px_ready = sem("px_ready")
        invcnt_ready = sem("invcnt_ready")
        out_mm = sem("out_mm")
        x_ready = sem("x_ready")
        dchain = sem("dve_chain")
        achain = sem("act_chain")
        rt_mm = sem("rt_mm")
        rt_ev = sem("rt_ev")
        lg_mm = sem("lg_mm")
        hi_ready = sem("hi_ready")
        ht_mm = sem("ht_mm")
        ht_ev = sem("ht_ev")
        gmax_ready = sem("gmax_ready")
        gexp_ready = sem("gexp_ready")
        m_ready = sem("m_ready")
        pos_mm = sem("pos_mm")
        plan_ready = sem("plan_ready")
        moe = []
        for l in range(2):
            moe.append({n: sem(f"{n}_{l}") for n in (
                "sel_ready", "xtok_mm", "xtok_ready", "xg_mm", "xg_ready", "gu_mm", "sg_ready", "hid_ready", "hidt_mm", "hidt_ready", "y_mm", "y_ready",
                "y_stored", "moe_chain")})
            moe[l]["w_in"] = [sem(f"w_in{r}_{l}") for r in range(RING)]
        guess_in = sem("guess_in")
        stored_all = sem("stored_all")
        yg_in = [[sem(f"yg_in{l}{n}") for n in range(NTM if l == 0 else QT)] for l in range(2)]
        zrows_ready = sem("zrows_ready")
        tail_stored = sem("tail_stored")
        sel_over = sem("sel_over")
        mix_ready = sem("mix_ready")
        yt_mm = sem("yt_mm")
        x2_ready = sem("x2_ready")
        trig_done = sem("trig_done")
        trig_ready = sem("trig_ready")
        lpars_in = sem("lpars_in")
        p2_mm = sem("p2_mm")
        p2_ev = sem("p2_ev")
        r2_mm = sem("r2_mm")
        r2_ready = sem("r2_ready")
        cmp_mm = sem("cmp_mm")
        cmp_ready = sem("cmp_ready")
        gel_ready = sem("gel_ready")
        cev_ready = sem("cev_ready")
        pct_mm = sem("pct_mm")
        pct_ready = sem("pct_ready")
        cs_mm = sem("cs_mm")
        pcn_ready = sem("pcn_ready")
        pce_ready = sem("pce_ready")
        sbz_mm = sem("sbz_mm")
        sb_act = sem("sb_act")
        sb_dve = sem("sb_dve")
        sbc_mm = sem("sbc_mm")
        sbo_mm = sem("sbo_mm")
        y2_mm = sem("y2_mm")
        mgs_ready = sem("mgs_ready")
        mix2_ready = sem("mix2_ready")
        wo_mm = sem("wo_mm")
        nsq_ready = sem("nsq_ready")
        nss_mm = sem("nss_mm")
        nstd_ready = sem("nstd_ready")
        xo_ready = sem("xo_ready")
        d2chain = sem("d2_chain")
        f1_mm = sem("f1_mm")
        f1_ev = sem("f1_ev")
        ffh_ready = sem("ffh_ready")
        ffs_ready = sem("ffs_ready")
        split_ready = sem("split_ready")
        f2_mm = sem("f2_mm")
        out_stored = sem("out_stored")
        spnop = sem("spnop")
        block = ctx.enter_context(nc.Block())
        n_in = 4

        def rows(w, c0, n):
            return w[:, c0:c0 + n].rearrange("(k p) n -> p k n", p=P)

        mod_slabs = [(rows(mod_w[j // 12], j % 12 * 512, 512), (KC, 512), (mod_mm, j + 1)) for j in range(24)]
        MOD0 = 4
        ab_slabs = [(rows(w_in_ab, 0, 512), (KC, 512), (proj_mm, 4)), (rows(w_in_ab, 512, 512), (KC, 512), (proj_mm, 8)),
                    (rows(w_in_ab, 1024, 512), (KC, 512), (proj_mm, 12)), (rows(w_in_ab, 1536, 256), (KC, 256), (proj_mm, 14)),
                    (rows(w_out_ab, 0, 512), (KC, 512), (out_mm, 4)), (rows(w_out_ab, 512, 512), (KC, 512), (out_mm, 8))]
        cd_slabs = [(rows(w_in_cd, 0, 512), (KC, 512), (proj_mm, 18)), (rows(w_in_cd, 512, 512), (KC, 512), (proj_mm, 22)),
                    (rows(w_in_cd, 1024, 256), (KC, 256), (proj_mm, 24)),
                    (pool_w.rearrange("g c d -> c g d"), (BC, P), (pool_mm, 1)),
                    (rows(w_out_cd, 0, 512), (KC, 512), (out_mm, 12)), (rows(w_out_cd, 512, 512), (KC, 512), (out_mm, 16))]
        stream_a = mod_slabs[:MOD0] + ab_slabs[:4] + mod_slabs[MOD0:] + ab_slabs[4:]
        stream_b = cd_slabs
        AB_IN, AB_OUT = MOD0, len(stream_a) - 2

        def mod_at(j):
            return j if j < MOD0 else j + 4
        NA, NB_ = len(stream_a), len(stream_b)
        assert NA % RING == 0 and NB_ % RING == 0
        USED2 = 31

        def slab(n, shape):
            k, w = shape
            return ring[:, n % RING, 0:k * w].rearrange("p (k w) -> p k w", k=k)

        def slab2_uses(s):
            return (USED2 - s + RING - 1) // RING

        def slab2_count(i, j):
            s = j % RING
            return i * (16 * slab2_uses(s)) + 16 * ((NA + NB_) // RING + j // RING + 1)

        J_IN, J_CMP, J_SBV, J_MG, J_NSA, J_SB, J_OUT, J_FF = 0, 4, 6, 7, 11, 12, 13, 15
        FF_ORDER = [(1, 0)] + [x for j in range(7) for x in ((1, j + 1), (2, j))] + [(2, 7)]
        FF_OUT = [0, 4, 1, 5, 2, 6, 3, 7]
        P2N, WON = 34, 16

        def ff_used(w, j):
            if w == 1:
                return ((f1_mm, 32, 32 + 4 * j + 4),)
            return ((f2_mm, 7, 7 + j + 1),) if j < 7 else ((wo_mm, WON, WON + 2 * KC),)

        def layer_slabs(i):
            win_ = w_in_2[bass.ds(i, 1), :, :].rearrange("a (k p) n -> p (a k) n", p=P)
            wc = cmp_w1[bass.ds(i, 1), :, :, :].rearrange("a v (j p) n -> p (a v) j n", p=P)
            wn = w_nsa_o[bass.ds(i, 1), :, :].rearrange("a (k p) n -> p (a k) n", p=P)
            ws = w_sb_o[bass.ds(i, 1), :, :].rearrange("a (k p) n -> p (a k) n", p=P)
            wo = w_out_2[bass.ds(i, 1), :, :].rearrange("a (k p) n -> p (a k) n", p=P)
            f1 = w_ff1[bass.ds(i, 1), :, :].rearrange("a (k p) n -> p (a k) n", p=P)
            f2 = w_ff2[bass.ds(i, 1), :, :].rearrange("a (k p) n -> p (a k) n", p=P)
            out = [(win_[:, :, 0:512], (KC, 512), (p2_mm, P2N, 4)), (win_[:, :, 512:COL_SB], (KC, COL_SB - 512), (p2_mm, P2N, 8))]
            sb_in = [(win_[:, :, COL_SB + 512 * j:COL_SB + 512 * j + 512], (KC, 512), (p2_mm, P2N, (12, 16, 18)[j])) for j in range(3)]
            out += sb_in[:2] + [(wc[:, v], (CB // 2, 256), (cmp_mm, 4, v + 1)) for v in range(2)] + sb_in[2:]
            out += [(win_[:, :, COL_MG + 512 * j:COL_MG + 512 * j + 512], (KC, 512), (p2_mm, P2N, 22 + 4 * j)) for j in range(4)]
            out += [(wn, (4, D), (y2_mm, KC, KC)), (ws, (4, D), (y2_mm, KC, KC))]
            out += [(wo[:, :, 512 * j:512 * j + 512], (KC, 512), (wo_mm, WON, WON + 4 * j + 4)) for j in range(2)]
            out += [(f1[:, :, 512 * j:512 * j + 512], (KC, 512)) + ff_used(1, j) if w == 1 else
                    (f2[:, 4 * j:4 * j + 4, :], (4, D)) + ff_used(2, j) for w, j in FF_ORDER]
            assert len(out) == USED2
            return out

        def tok_bank(q):
            return 3 + q % 5

        def tok_cols(q):
            return slice((q % 2) * 512, (q % 2) * 512 + 512)

        def lane_block(u, pairs, i):
            if u == 0:
                return i
            return nc.s_assert_within(2 * pairs - 1 - i, 1, MAXB - 1, skip_runtime_bounds_check_because="i is below pairs, so the block is pairs at least")

        def expert_loads(l, e):
            g = ex_gate[l][bass.ds(e, 1), :, :].rearrange("a (k p) n -> p (a k) n", p=P)
            u = ex_up[l][bass.ds(e, 1), :, :].rearrange("a (k p) n -> p (a k) n", p=P)
            d = ex_down[l][bass.ds(e, 1), :, :].rearrange("a (k p) n -> p (a k) n", p=P)
            return (g, (KC, DE)), (u, (KC, DE)), (d, (EC, D))

        @block.sync
        def _(sp):
            sp.dma_start(con[:, :], consts_in).then_inc(inputs_in, 16)
            sp.dma_start(par[:, :], params_in).then_inc(inputs_in, 16)
            sp.dma_start(xT[:, :, :, :], xT_in).then_inc(inputs_in, 16)
            sp.dma_start(E[:, 0:NX].bitcast(I32), pos_in).then_inc(inputs_in, 16)

            def static_loads(stream, n0):
                for j, (src, shape, _used) in enumerate(stream):
                    n = n0 + j
                    if j >= RING:
                        s, v = stream[j - RING][2]
                        sp.wait_ge(s, v)
                    sp.dma_start(slab(n, shape), src).then_inc(slab_in[n % RING], 16)
                    if stream is stream_b and j == NB_ - 1:
                        sp.wait_ge(h_ready, 3 * KC)
                        sp.dma_start(invcnt, invcnt_in).then_inc(invcnt_ready, 16)

            def expert_stream(l, before):
                sems = moe[l]
                for w in range(3):
                    for u, e in enumerate((0, NE - 1)):
                        s, v = before[2 * w + u]
                        sp.wait_ge(s, v)
                        src, shape = expert_loads(l, e)[w]
                        sp.dma_start(slab(2 * w + u, shape), src).then_inc(guess_in, 16)
                sp.wait_ge(plan_ready, l + 1)
                pairs = sp.value_load(blki[0:1, MAXB:MAXB + 1], min_val=1, max_val=MAXB // 2)
                sp.wait_ge(guess_in, 96 * l + 96)
                with sp.Fori(0, pairs) as i:
                    loads, new = [], []
                    for u in range(2):
                        b = lane_block(u, pairs, i)
                        e = sp.value_load(blki[0:1, bass.ds(b, 1)], min_val=0, max_val=NE - 1)
                        loads.append(expert_loads(l, e))
                        new.append(sp.value_load(blki[0:1, bass.ds(b + (NEW + u), 1)], min_val=0, max_val=1))
                    for w in range(3):
                        if w < 2:
                            sp.wait_ge(sems["gu_mm"], 2 * i + w + 1)
                        else:
                            sp.wait_ge(sems["y_mm"], i + 1)
                        sp.sem_inc(spnop, 1)
                        for u in range(2):
                            src, shape = loads[u][w]
                            with sp.If(new[u] > 0):
                                sp.dma_start(slab(2 * w + u, shape), src).then_inc(sems["w_in"][2 * w + u], 16)
                            with sp.Else():
                                sp.sem_inc(sems["w_in"][2 * w + u], 16)
                sp.wait_ge(sems["gu_mm"], 2 * pairs + 2)
                sp.sem_inc(spnop, 1)
                sp.wait_ge(sems["y_mm"], pairs + 1)
                sp.sem_inc(spnop, 1)

            static_loads(stream_a, 0)
            expert_stream(0, [stream_a[NA - RING + r][2] for r in range(RING)])
            sp.wait_ge(yg_in[0][NTM - 1], 32)
            static_loads(stream_b, NA)
            expert_stream(1, [stream_b[NB_ - RING + r][2] for r in range(RING)])
            sp.wait_ge(yg_in[1][QT - 1], 32)
            sp.dma_start(lpars.rearrange("p (a n) -> p a n", a=2), lparams_in.rearrange("a p n -> p a n")).then_inc(lpars_in, 16)

            with sp.Fori(0, 2) as i:
                slabs = layer_slabs(i)
                for j, (src, shape, _used) in enumerate(slabs):
                    if j < RING:
                        last = USED2 - 1 - (USED2 - 1 - j) % RING
                        s, per, v = slabs[last][2]
                        sp.wait_ge(s, i * per + v - per)
                    else:
                        s, per, v = slabs[j - RING][2]
                        sp.wait_ge(s, i * per + v)
                    sp.sem_inc(spnop, 1)
                    sp.dma_start(slab(j, shape), src).then_inc(slab_in[j % RING], 16)
            sp.wait_ge(xo_ready, 2 * 2 * KC + KC)
            sp.dma_start(outT, xT[:, 0, :, :]).then_inc(out_stored, 16)
            sp.wait_ge(out_stored, 16)

        def g2(row):
            return row.rearrange("p (g t) -> p g t", g=TG)

        def src_of(full, k):
            return xT[:, :, k, :] if full else xT[:, 0, k, :]

        def hsrc(full, k):
            return hT[:, :, k, :] if full else hT[:, 0, k, :]

        def sq_of(full, k):
            return g2(sqb[:, k % 4, :]) if full else sqb[:, k % 4, 0:NX]

        def unit_place(layer, n):
            if layer == 0:
                return n % 2, prob[:, n % 2, :], n % 2
            return (0, 1, 6)[n % 3], prob3[:, n % 3, :], n % 3

        def attention_units(layer):
            if layer == 0:
                return [(3 * h + k, h, k) for h in range(HEADS) for k in range(3)]
            return [(3 * HEADS + 2 * h + k, h, k) for h in range(HEADS) for k in range(2)]

        @block.scalar
        def _(act):
            chain = [0]

            def link(ins):
                chain[0] += 1
                ins.then_inc(achain, 1)
                act.wait_ge(achain, chain[0])

            eps = cc("eps")

            def norm_stats(call, full, ready):
                if not (isinstance(call, int) and call == 0):
                    act.wait_ge(h_ready, call * KC)
                for k in range(KC):
                    ready(k)
                    if k >= 4:
                        act.wait_ge(ssq_mm, call * KC + k - 3)
                    act.activation(sq_of(full, k), src_of(full, k), ACT.Square).then_inc(sq_ready, 1)
                act.wait_ge(ssq_mm, call * KC + KC)
                w = 512 if full else NX
                act.activation(stdv[:, 0:w], ps[:, 7, 0:w], ACT.Sqrt, bias=eps, scale=1.0 / D).then_inc(std_ready, 1)

            def modulate(call, full, scale, shift):
                for k in range(KC):
                    act.wait_ge(xn_ready, call * KC + k + 1)
                    for g in range(TG if full else 1):
                        ins = act.activation(hT[:, g, k, :], hT[:, g, k, :], ACT.Identity, scale=scale(k, g), bias=shift(k, g))
                    ins.then_inc(h_ready, 1)

            def evac(n, dst, src, func=ACT.Copy, **kw):
                act.wait_ge(proj_mm, n + 1)
                act.activation(dst, src, func, **kw).then_inc(proj_ev, 1)

            def qsq(g, c, w):
                act.wait_ge(proj_ev, proj_n["qk"][g])
                if g >= 2:
                    act.wait_ge(qss_mm, g - 1)
                act.activation(sqb[:, g % 2, 0:w], qk[:, c, 0:w], ACT.Square).then_inc(qsq_ready, 1)

            def qstd(g, w):
                act.wait_ge(qss_mm, g + 1)
                if g >= 2:
                    act.wait_ge(rope_ready, g - 1)
                act.activation(sqb[:, 2 + g % 2, 0:w], ps[:, 5, 0:w], ACT.Sqrt, bias=eps, scale=1.0 / DH).then_inc(qstd_ready, 1)

            def attend_exp(n, bank, p, u, parts, sc):
                act.wait_ge(nb_ready, n + 1)
                for (c0, c1), m in parts:
                    ins = act.activation(p[:, c0:c1], ps[:, bank, c0:c1], ACT.Exp, bias=nb[:, u, m:m + 1], scale=sc,
                                         accum_out=sm[:, u, m:m + 1])
                ins.then_inc(ex_ready, 1)

            def attend_pt(n, u, nblk):
                act.wait_ge(tr_mm, n + 1)
                act.activation(probT[:, u, 0:nblk, :], ps[:, 2 + u, 0:nblk * P].rearrange("p (b q) -> p b q", b=nblk),
                               ACT.Copy).then_inc(pt_ready, 1)

            proj_n = {"qk": {}}
            act.wait_ge(inputs_in, 16 * n_in)
            act.wait_ge(setup_done, 1)
            act.activation(condv[:, :, 0:2], pc("cond").rearrange("p (k c) -> p k c", c=2), ACT.Silu).then_inc(cond_ready, 1)

            def trig():
                act.wait_ge(trig_ready, 1)
                act.activation(sin2, sin2, ACT.Sin)
                act.activation(cos2, cos2, ACT.Sin).then_inc(trig_done, 1)

            def block1(layer):
                base, g0 = (0, 0) if layer == 0 else (14, 5)
                full = layer == 0
                if full:
                    norm_stats(0, True, lambda k: None)
                    for j in range(MOD0):
                        act.wait_ge(mod_mm, j + 1)
                        act.activation(mrow, ps[:, 6, :], ACT.Copy).then_inc(mod_ev, 1)
                    trig()
                    act.wait_ge(mod_ready, 1)
                else:
                    act.wait_ge(x2_ready, NTM)
                    norm_stats(2, True, lambda k: None)
                modulate(2 * layer, True, lambda k, g: scale1[:, layer, k, g:g + 1], lambda k, g: modv[:, layer, k, g:g + 1])
                w = 512 if full else NX
                for c in range(QKC):
                    wc = 512 if c == QC else w
                    evac(base + c, qk[:, c, 0:wc], ps[:, c % 4, 0:wc])
                    proj_n["qk"][g0 + c] = base + c + 1
                evac(base + 5, vtok, ps[:, 1, :].rearrange("p (n d) -> p n d", n=4))
                for n in range(8):
                    if n < QKC:
                        qsq(g0 + n, n, 512 if n == QC else w)
                    if full:
                        m = base + 6 + n
                        src = g2(ps[:, (6 + n) % 4, :])
                        if n < BC:
                            act.wait_ge(setup_done, 1)
                            evac(m, gpad[:, n, :, HALO:HALO + NX], src)
                        else:
                            evac(m, g2(cat[:, n, :]), src, ACT.Sigmoid)
                    elif n < BC:
                        act.wait_ge(setup_done, 3)
                        evac(base + 6 + n, upad[:, n, PPAD:PPAD + NX], ps[:, (6 + n) % 4, 0:NX])
                    if n < QKC:
                        qstd(g0 + n, 512 if n == QC else w)
                act.wait_ge(swap_mm, layer + 1)
                act.activation(kswap, ps[:, 6, :], ACT.Copy).then_inc(swap_ev, 1)
                units = attention_units(layer)
                lag = 1 + layer
                for s in range(len(units) + lag):
                    if s < len(units):
                        n, h, kind = units[s]
                        bank, p, u = unit_place(layer, n)
                        if n >= 2:
                            act.wait_ge(tr_mm, n - lag)
                        if kind == 2:
                            attend_exp(n, bank, p, u, [((0, 256), 0), ((256, 512), 1)], SC_A)
                        else:
                            attend_exp(n, bank, p, u, [((0, 512), 0)], SC_A)
                            if layer == 1:
                                act.activation(es[:, u, :], pc("sink", h, 1), ACT.Exp, bias=nb[:, u, 0:1]).then_inc(sink_ready, 1)
                    if full and 1 <= s <= 24 - MOD0:
                        act.wait_ge(mod_mm, MOD0 + s)
                        act.activation(mrow, ps[:, 6, :], ACT.Copy).then_inc(mod_ev, 1)
                    if s >= lag:
                        n, h, kind = units[s - lag]
                        if n >= 2:
                            act.wait_ge(pv_mm, n - 1)
                        attend_pt(n, n % 2, 4)
                        if s > lag:
                            head_out(units[s - lag - 1], layer)
                head_out(units[-1], layer)
                if full:
                    act.wait_ge(cd_ready, 1)
                    for c in range(BC):
                        act.activation(sqb[:, c, :], cat[:, 4 + c, :], ACT.Square).then_inc(csq_ready, 1)
                    act.wait_ge(cvar_mm, 1)
                    act.activation(stdv[:, :], ps[:, 5, :], ACT.Sqrt, bias=eps, scale=1.0 / 512).then_inc(cstd_ready, 1)
                    for c in range(BC):
                        act.wait_ge(cn_ready, c + 1)
                        act.activation(cat[:, 4 + c, :], cat[:, 4 + c, :], ACT.Silu, scale=pc("cln_g", c, 1),
                                       bias=pc("cln_b", c, 1)).then_inc(bx_ready, 1)
                norm_stats(2 * layer + 1, full, lambda k: act.wait_ge(x_ready, KC * layer + k + 1))
                act.wait_ge(mod_ready, 2)
                modulate(2 * layer + 1, full, lambda k, g: scale2[:, layer, k, g:g + 1], lambda k, g: modv[:, layer, 24 + k, g:g + 1])

            def head_out(unit, layer):
                n, h, kind = unit
                last = kind == 2 if layer == 0 else kind == 1
                if h % 2 == 1 and last:
                    act.wait_ge(pv_mm, n + 1)
                    w = 512 if layer == 0 else NX
                    act.activation(cat[:, h // 2, 0:w], ps[:, 4 + (h // 2) % 2, 0:w], ACT.Copy).then_inc(o_ready, 1)

            def experts(l):
                nt = NTM if l == 0 else QT
                sems = moe[l]
                w = nt * P
                act.wait_ge(rt_mm, l + 1)
                for u in range(2):
                    ins = act.activation(rtp[64 * u:64 * u + RL, 0:w], ps[64 * u:64 * u + RL, 0, 0:w], ACT.Copy)
                ins.then_inc(rt_ev, 1)
                for q in range(2 * nt):
                    act.wait_ge(ht_mm, (0, 2 * NTM)[l] + q + 1)
                    act.activation(tok_hi[:, q // 2, tok_cols(q)], ps[:, tok_bank(q), :], ACT.Copy).then_inc(hi_ready, 1)
                act.wait_ge(gmax_ready, l + 1)
                for n in range(nt):
                    act.activation(pen[:, n, :], lgp[:, n, 0:NG], ACT.Exp, bias=rsc[:, 0, n:n + 1], accum_out=rsc[:, 1, n:n + 1])
                act.activation(rsc[:, 3, 0:nt], rsc[:, 2, 0:nt], ACT.Exp).then_inc(gexp_ready, 1)
                def gathered(count):
                    act.wait_ge(sems["xtok_mm"], count)
                    act.activation(xtok, ps[:, 0:2, :].rearrange("p b n -> p (b n)"), ACT.Copy).then_inc(sems["xtok_ready"], 1)
                    act.wait_ge(sems["xg_mm"], count)
                    act.activation(xg, ps[:, 0:2, :].rearrange("p b (k s) -> p (b k) s", s=PAIR), ACT.Copy).then_inc(sems["xg_ready"], 1)

                gathered(1)
                act.wait_ge(plan_ready, l + 1)
                pairs = act.value_load(blki[0:1, MAXB:MAXB + 1], min_val=1, max_val=MAXB // 2)
                act.sem_inc(sems["y_ready"], 1)
                act.sem_inc(sems["y_stored"], 32)

                def pair(i, last):
                    act.wait_ge(sems["gu_mm"], 2 * i + 3)
                    act.activation(silu_g, ps[:, 2, :], ACT.Silu).then_inc(sems["sg_ready"], 1)
                    if not last:
                        gathered(i + 2)
                    act.wait_ge(sems["y_mm"], i + 2)
                    act.wait_ge(sems["y_stored"], 32 * i + 32)
                    act.activation(yb, ps[:, 6:8, :].rearrange("p a b -> p (a b)"), ACT.Copy).then_inc(sems["y_ready"], 1)
                    act.wait_ge(sems["y_ready"], i + 2)
                    for u in range(2):
                        act.dma_start(y_rows[bass.ds(lane_block(u, pairs, i) * SLOTS, SLOTS), :], yb[u * SLOTS:(u + 1) * SLOTS, :]).then_inc(sems["y_stored"], 16)

                with act.Fori(0, pairs - 1) as i:
                    pair(i, False)
                pair(pairs - 1, True)
                act.wait_ge(sems["y_stored"], 32 * pairs + 32)
                act.sem_inc(stored_all, 1)

            block1(0)
            experts(0)
            block1(1)
            experts(1)

            def layer2(i):
                call = 4 + 2 * i
                act.wait_ge(x2_ready, 6)
                norm_stats(call, False, lambda k: act.wait_ge(xo_ready, 2 * KC * i + k + 1))

                def ev2(n, dst, src, func=ACT.Copy, **kw):
                    act.wait_ge(p2_mm, P2N * i + n + 1)
                    return act.activation(dst, src, func, **kw)

                for n in range(4):
                    ev2(n, qp[:, n, :], ps[:, n % 4, 0:NX]).then_inc(p2_ev, 1)
                for n in range(4, 7):
                    ev2(n, kv[:, n - 4, :], ps[:, n % 4, 0:NX]).then_inc(p2_ev, 1)
                ev2(7, vsw, ps[:, 3, 0:NX].rearrange("p (n d) -> p n d", n=QT))
                ev2(7, gates[:, :, :], ps[:, 3, NX:NX + 48].rearrange("p (n d) -> p n d", n=QT), ACT.Sigmoid).then_inc(p2_ev, 1)
                for n in range(8, 12):
                    ev2(n, sbq[:, n - 8, :], ps[:, n % 4, 0:NX], scale=SC_B).then_inc(p2_ev, 1)
                for n in range(12, 16):
                    ev2(n, sbk[:, n - 12, :], ps[:, n % 4, 0:NX]).then_inc(p2_ev, 1)
                act.wait_ge(cmp_mm, 4 * i + 2)
                act.activation(hrow, ps[:, 6, :], ACT.Copy).then_inc(cmp_ready, 1)
                ev2(16, sbv[:, 0, :], ps[:, 0, :]).then_inc(p2_ev, 1)
                act.wait_ge(cmp_mm, 4 * i + 3)
                act.activation(hcmp[:, :, :], ps[:, 7, 0:64].rearrange("p (v c) -> p v c", v=4), ACT.Copy).then_inc(cmp_ready, 1)
                act.wait_ge(cmp_ready, 2 * i + 2)
                for q in range(4):
                    ins = act.activation(gcmp[:, q, :], hcmp[:, q, 0:NCMP], ACT.Gelu_apprx_tanh, bias=hcmp[:, q, NCMP:NCMP + 1])
                ins.then_inc(gel_ready, 1)
                ev2(17, sbv[:, 1, :], ps[:, 1, :]).then_inc(p2_ev, 1)
                act.wait_ge(pcn_ready, 2 * i + 1)
                act.activation(scmp, scmp, ACT.Exp, scale=SC_A).then_inc(pce_ready, 1)
                zp = ps[:, 0:SBH, 0:384]
                act.wait_ge(sbz_mm, i + 1)
                act.activation(spl, zp, ACT.Abs).then_inc(sb_act, 1)
                act.wait_ge(sb_act, 5 * i + 1)
                act.activation(spl, spl, ACT.Exp, scale=-1.0).then_inc(sb_act, 1)
                act.wait_ge(sb_act, 5 * i + 2)
                act.activation(spl, spl, ACT.Ln, bias=1.0).then_inc(sb_act, 1)
                act.wait_ge(pct_mm, i + 1)
                act.activation(pcT, ps[:, 4, :].rearrange("p (b q) -> p b q", b=4), ACT.Copy).then_inc(pct_ready, 1)
                for m in range(2):
                    ev2(18 + m, mg[:, m, :], ps[:, 6 + m, 0:NX]).then_inc(p2_ev, 1)
                act.wait_ge(sb_dve, 2 * i + 2)
                act.activation(zs, zs, ACT.Exp).then_inc(sb_act, 1)
                act.wait_ge(sbo_mm, i + 1)
                act.activation(osb, ps[:, 0:SBH, 0:NX], ACT.Copy).then_inc(sb_act, 1)
                for s in range(2 * HEADS + 2):
                    if s < 2 * HEADS:
                        n, u, k = 40 + 16 * i + s, s % 2, P * (s % 2 + 1)
                        act.wait_ge(tr_mm, n - 1)
                        attend_exp(n, u, prob[:, u, :], u, [((0, k), 0), ((NX, NX + k), 1)], SC_A)
                    if s < 2 * HEADS - 2:
                        ev2(20 + s, mg[:, s + 2, :], ps[:, 6 + s % 2, 0:NX]).then_inc(p2_ev, 1)
                    if 1 <= s <= 2 * HEADS:
                        n, u = 40 + 16 * i + s - 1, (s - 1) % 2
                        act.wait_ge(pv_mm, n - 1)
                        attend_pt(n, u, 2 * (u + 1))
                    if s >= 2 and (s - 2) % 4 == 3:
                        n, c = 40 + 16 * i + s - 2, (s - 2) // 4
                        act.wait_ge(pv_mm, n + 1)
                        act.activation(onsa[:, c, :], ps[:, 4 + c % 2, 0:NX], ACT.Copy).then_inc(o_ready, 1)
                act.wait_ge(p2_ev, P2N * i + P2N)
                for j in range(KC // 2):
                    m = mg.rearrange("p (b m) t -> p b m t", b=2)[:, :, 2 * j:2 * j + 2, :]
                    act.activation(m, m, ACT.Sigmoid).then_inc(mgs_ready, 1)

                def out_norm(c):
                    for n in range(KC):
                        m = n if c == 0 else FF_OUT[n]
                        y = ps[:, m % 4, 0:NX] if c == 0 else ps[:, m % 4, m // 4 * NX:m // 4 * NX + NX]
                        act.wait_ge(wo_mm, WON + WON * i + KC * c + (n if c == 0 else n | 1) + 1)
                        if n >= 4:
                            act.wait_ge(nss_mm, WON * i + KC * c + n - 3)
                        act.activation(yres[:, m, :], y, ACT.Copy)
                        act.activation(sqb[:, n % 4, 0:NX], y, ACT.Square).then_inc(nsq_ready, 1)
                    act.wait_ge(nss_mm, WON * i + KC * c + KC)
                    act.activation(stdv[:, 0:NX], ps[:, 7, 0:NX], ACT.Sqrt, bias=eps, scale=1.0 / D).then_inc(nstd_ready, 1)

                out_norm(0)
                norm_stats(call + 1, False, lambda k: act.wait_ge(xo_ready, 2 * KC * i + KC + k + 1))
                for m in range(FF // P):
                    act.wait_ge(f1_mm, 32 * i + 32 + m + 1)
                    if m >= 4:
                        act.wait_ge(ffs_ready, 32 * i + m - 3)
                    r = sqb[:, m % 4, 0:NX]
                    act.activation(r, ps[:, 4 + m % 4, 0:NX], ACT.Relu).then_inc(f1_ev, 1)
                    act.wait_ge(f1_ev, 32 * i + m + 1)
                    act.activation(r, r, ACT.Square).then_inc(ffh_ready, 1)
                out_norm(1)

            with act.Fori(0, 2) as i:
                layer2(i)

        @block.tensor
        def _(pe):
            def take_slab(n, shape):
                pe.wait_ge(slab_in[n % RING], 16 * (n // RING + 1))
                return slab(n, shape)

            def mm_chunk(out, w, m0, rhs, nk=KC, start=True, stop=True):
                for k in range(nk):
                    ins = pe.matmul(out, w[:, k, m0:m0 + P], rhs(k), start=start and k == 0, stop=stop and k == nk - 1)
                return ins

            def square_sum(call, full, k):
                w = 512 if full else NX
                pe.wait_ge(sq_ready, KC * call + k + 1)
                pe.matmul(ps[:, 7, 0:w], ones[:, :], sqb[:, k % 4, 0:w], start=k == 0, stop=k == KC - 1).then_inc(ssq_mm, 1)

            def norm(call, full):
                for k in range(KC):
                    square_sum(call, full, k)

            def mod_sum(j):
                w = take_slab(mod_at(j), (KC, 512))
                if j:
                    pe.wait_ge(mod_ev, j)
                for k in range(KC):
                    q = k % 4
                    ins = pe.matmul(ps[32 * q:32 * q + 32, 6, :], condv[:, k, :], w[:, k, :], start=k < 4, stop=k >= 4)
                ins.then_inc(mod_mm, 1)

            def mod_columns(j):
                pe.wait_ge(mod_ev, j + 1)
                bank, at = (5, 8 * j) if j < MOD0 else (7, 8 * (j - MOD0))
                for m in range(4):
                    ins = pe.matmul(ps[:, bank, at + 2 * m:at + 2 * m + 2], mrow[:, m * P:m * P + P], cc("fold")[:, 0:2], start=True, stop=True)
                ins.then_inc(mod_fold, 1)

            def qss(g, c, w):
                pe.wait_ge(qsq_ready, g + 1)
                if g >= 1:
                    pe.wait_ge(qstd_ready, g)
                pe.matmul(ps[:, 5, 0:w], cc("headones"), sqb[:, g % 2, 0:w], start=True, stop=True).then_inc(qss_mm, 1)

            def qrot(g, c):
                pe.wait_ge(qn_ready, g + 1)
                if g >= 1:
                    pe.wait_ge(rope_ready, g)
                pe.matmul(ps[:, 6, 0:NX], cc("rot_a"), qk[:, c, 0:NX], start=True, stop=True).then_inc(rot_mm, 1)

            def block1(layer):
                full = layer == 0
                base, g0 = (0, 0) if full else (14, 5)
                n0 = AB_IN if full else NA
                norm(2 * layer, True)
                if full:
                    pe.wait_ge(cond_ready, 1)
                    for j in range(MOD0):
                        mod_sum(j)
                        mod_columns(j)

                def normed(k):
                    pe.wait_ge(h_ready, KC * 2 * layer + k + 1)
                    return hsrc(full, k)

                def bank_free(n):
                    if n >= 4:
                        pe.wait_ge(proj_ev, base + n - 3)

                w = take_slab(n0, (KC, 512))
                wq = 512 if full else NX
                for c in range(QC):
                    mm_chunk(ps[:, c, 0:wq], w, c * P, normed if c == 0 else lambda k: hsrc(full, k)).then_inc(proj_mm, 1)
                w = take_slab(n0 + 1, (KC, 512))
                bank_free(4)
                mm_chunk(ps[:, 0, :], w, 0, lambda k: hsrc(True, k)).then_inc(proj_mm, 1)
                bank_free(5)
                for n in range(4):
                    for k in range(KC):
                        ins = pe.matmul(ps[:, 1, n * P:n * P + P], hT[:, n // 2, k, (n % 2) * P:(n % 2) * P + P], w[:, k, P:2 * P],
                                        start=k == 0, stop=k == KC - 1)
                ins.then_inc(proj_mm, 1)
                for n in range(8):
                    m = n + 2
                    if (full or n < BC) and m % 4 == 0:
                        w = take_slab(n0 + 1 + m // 4, (KC, 512 if full and m < 12 and not m == 8 else 256))
                    if full or n < BC:
                        bank_free(6 + n)
                        mm_chunk(ps[:, (6 + n) % 4, 0:wq], w, (m % 4) * P, lambda k: hsrc(full, k)).then_inc(proj_mm, 1)
                    if n < QKC:
                        qss(g0 + n, n, 512 if n == QC else wq)
                    if 1 <= n <= QKC:
                        qrot(g0 + n - 1, n - 1)
                pe.wait_ge(rope_ready, g0 + QKC)
                pe.matmul(ps[:, 6, :], cc("swap"), qk[:, QC, :], start=True, stop=True).then_inc(swap_mm, 1)
                pe.wait_ge(swap_ev, layer + 1)
                pe.wait_ge(proj_ev, base + (14 if full else 10))
                ow = AB_OUT if full else NA + 4

                def heads_first(m0, m1):
                    w = take_slab(ow, (KC, 512))
                    for m in range(m0, m1):
                        mm_chunk(ps[:, m, 0:wq], w, m * P, lambda k: cat[:, k, 0:wq], 4, stop=False)

                units = attention_units(layer)
                lag = 1 + layer
                for s in range(len(units) + lag + 1):
                    if s < len(units):
                        n, h, kind = units[s]
                        bank, _, _ = unit_place(layer, n)
                        if s > lag:
                            pe.wait_ge(ex_ready, n - lag)
                        o, j = (h % 2) * DH, h // 4
                        kk = qk[:, QC, :] if o == j * DH else kswap
                        if kind == 2:
                            for t in range(QT):
                                ins = pe.matmul(ps[:, bank, t * NX:t * NX + NX], qk[o:o + DH, h // 2, NX + t * P:NX + t * P + P],
                                                kk[o:o + DH, NX:512], start=True, stop=True)
                        else:
                            ins = pe.matmul(ps[:, bank, :], qk[o:o + DH, h // 2, kind * P:kind * P + P], kk[o:o + DH, :],
                                            start=True, stop=full)
                            if not full:
                                c0 = P if kind == 0 else 0
                                ins = pe.matmul(ps[:, bank, c0:c0 + P], ident, cc("trineg") if kind == 0 else cc("band1"), start=False, stop=True)
                        ins.then_inc(sc_mm, 1)
                    if full and 1 <= s <= 24 - MOD0:
                        if s > 1:
                            mod_columns(MOD0 + s - 2)
                        mod_sum(MOD0 + s - 1)
                    if lag <= s < len(units) + lag:
                        n = units[s - lag][0]
                        transposes(n, n % 2, unit_place(layer, n)[1], [(b * P, b * P + P) for b in range(4)], s > lag + 1)
                    if s > lag:
                        n, h, kind = units[s - lag - 1]
                        pe.wait_ge(pt_ready, n + 1)
                        o, j, u = (h % 2) * DH, h // 4, n % 2
                        ch = h // 2
                        if ch >= 2 and h % 2 == 0 and kind == 0:
                            pe.wait_ge(o_ready, 4 * layer + ch - 1)
                        ob = ps[o:o + DH, 4 + ch % 2, :]
                        if kind == 2:
                            for t in range(QT):
                                for b in range(2):
                                    ins = pe.matmul(ob[:, NX + t * P:NX + t * P + P], vtok[:, 2 + b, j * DH:j * DH + DH], probT[:, u, 2 * t + b, :],
                                                    start=b == 0, stop=b == 1)
                        else:
                            for b in range(4):
                                ins = pe.matmul(ob[:, kind * P:kind * P + P], vtok[:, b, j * DH:j * DH + DH], probT[:, u, b, :],
                                                start=b == 0, stop=b == 3)
                        ins.then_inc(pv_mm, 1)
                if full:
                    mod_columns(23)
                    pe.wait_ge(conv_ready, 1)
                    for c in range(BC):
                        ins = pe.matmul(ps[:, 6, :], ones[:, :], cat[:, 4 + c, :], start=c == 0, stop=c == BC - 1)
                    ins.then_inc(cmu_mm, 1)
                    pe.wait_ge(o_ready, 4)
                    heads_first(0, 2)
                    for c in range(BC):
                        pe.wait_ge(csq_ready, c + 1)
                        ins = pe.matmul(ps[:, 5, :], ones[:, :], sqb[:, c, :], start=c == 0, stop=c == BC - 1)
                    ins.then_inc(cvar_mm, 1)
                    heads_first(2, 4)
                    pe.wait_ge(bx_ready, BC)
                else:
                    wp = take_slab(n0 + 3, (BC, P))
                    pe.wait_ge(pool_ready, BC)
                    for g in range(BC):
                        ins = pe.matmul(ps[:, 6 + g // 2, (g % 2) * NX:(g % 2) * NX + NX], wp[:, g, :], pt_pool[:, g, :], start=True, stop=True)
                    ins.then_inc(pool_mm, 1)
                    pe.wait_ge(px_ready, 1)
                pe.wait_ge(o_ready, 4 * layer + 4)
                for m in range(KC):
                    if m % 4 == 0:
                        w = take_slab(ow + m // 4, (KC, 512))
                    if m >= 4:
                        pe.wait_ge(x_ready, KC * layer + m - 3)
                    for k in range(4 if full and m < 4 else 0, KC):
                        ins = pe.matmul(ps[:, m % 4, 0:wq], w[:, k, (m % 4) * P:(m % 4) * P + P], cat[:, k, 0:wq], start=k == 0, stop=k == KC - 1)
                    ins.then_inc(out_mm, 1)
                    if m >= 2:
                        square_sum(2 * layer + 1, full, m - 2)
                for k in (6, 7):
                    square_sum(2 * layer + 1, full, k)

            def transposes(n, u, p, blocks, again):
                pe.wait_ge(pn_ready, n + 1)
                if again:
                    pe.wait_ge(pt_ready, n - 1)
                for b, (c0, c1) in enumerate(blocks):
                    ins = pe.transpose(ps[:, 2 + u, b * P:b * P + P], p[:, c0:c1], ident)
                ins.then_inc(tr_mm, 1)

            def experts(l):
                nt = NTM if l == 0 else QT
                sems = moe[l]
                def htile(n, k):
                    return hT[:, n // 2, k, (n % 2) * P:(n % 2) * P + P]

                at, _ = po["rt_w"]
                rows_ = lambda u: slice(64 * u, 64 * u + RL)
                for k in range(KC):
                    pe.wait_ge(h_ready, KC * (2 * l + 1) + k + 1)
                    out = ps[rows_(k % 2), 0, 0:nt * P]
                    ins = pe.matmul(out.rearrange("p (g t) -> p g t", g=TG) if l == 0 else out,
                                    par[:, at + (l * KC + k) * RL:at + (l * KC + k + 1) * RL], hsrc(l == 0, k), start=k < 2, stop=k >= KC - 2)
                ins.then_inc(rt_mm, 1)

                def tokens(q):
                    if q >= 5:
                        pe.wait_ge(ht_ev, (0, 2 * NTM)[l] + q - 4)
                    for b in range(4):
                        ins = pe.transpose(ps[:, tok_bank(q), b * P:b * P + P], htile(q // 2, 4 * (q % 2) + b), ident)
                    ins.then_inc(ht_mm, 1)

                for q in range(3):
                    tokens(q)
                pe.wait_ge(rt_ev, l + 1)
                for n in range(nt):
                    for u in range(2):
                        ins = pe.transpose(ps[:, 2 * u, n * RL:(n + 1) * RL], rtp[rows_(u), n * P:(n + 1) * P], ident[rows_(u), rows_(u)])
                ins.then_inc(lg_mm, 1)
                for q in range(3, 2 * nt):
                    tokens(q)
                pe.wait_ge(m_ready, l + 1)
                pe.matmul(ps[:, 1, 0:nt * NE], cc("tri_strict"), M1[:, 2, 0:nt * NE], start=True, stop=False)
                pe.matmul(ps[:, 1, nt * NE:(nt + 1) * NE], ones[:, :], M1[:, 2, 0:NE], start=False, stop=False)
                for j in range(nt):
                    n = nt - 1 if j == 0 else nt
                    later = M1[:, 2, j * NE:(j + 1) * NE].unsqueeze(1).broadcast_to([P, n - j, NE])
                    ins = pe.matmul(ps[:, 1, (j + 1) * NE:(n + 1) * NE].rearrange("p (n e) -> p n e", e=NE), ones[:, :], later, start=False, stop=j == nt - 1)
                ins.then_inc(pos_mm, 1)
                def gather(count):
                    pe.wait_ge(sems["sel_ready"], count)
                    for c in range(2):
                        for n in range(nt):
                            for j, part in enumerate((tok_hi[:, n, :], tok_lo[n // 2][:, n % 2, :])):
                                ins = pe.matmul(ps[:, c, :], sel[:, n, :], part[:, c * 512:c * 512 + 512], start=n == 0 and j == 0,
                                                stop=n == nt - 1 and j == 1)
                    ins.then_inc(sems["xtok_mm"], 1)

                def turn(count):
                    pe.wait_ge(sems["xtok_ready"], count)
                    for k in range(KC):
                        ins = pe.transpose(ps[:, k // 4, (k % 4) * PAIR:(k % 4 + 1) * PAIR], xtok[:, k * P:(k + 1) * P], ident)
                    ins.then_inc(sems["xg_mm"], 1)

                pe.wait_ge(ht_ev, (2 * NTM, 2 * NTM + 2 * QT)[l])
                gather(1)
                turn(1)
                pe.wait_ge(plan_ready, l + 1)
                pairs = pe.value_load(blki[0:1, MAXB:MAXB + 1], min_val=1, max_val=MAXB // 2)
                pe.sem_inc(sems["gu_mm"], 2)
                pe.sem_inc(sems["y_mm"], 1)
                half = lambda u: slice(u * SLOTS, (u + 1) * SLOTS)
                def pair(i, last):
                    pe.wait_ge(sems["xg_ready"], i + 1)
                    for w in range(2):
                        for u in range(2):
                            pe.wait_ge(sems["w_in"][2 * w + u], 16 * i + 16)
                        for k in range(KC):
                            for u in range(2):
                                ins = pe.matmul(ps[half(u), 2 + w, :], xg[:, k, half(u)], slab(2 * w + u, (KC, DE))[:, k, :],
                                                start=k == 0, stop=k == KC - 1)
                        ins.then_inc(sems["gu_mm"], 1)
                    if not last:
                        gather(i + 2)
                    pe.wait_ge(sems["hid_ready"], i + 1)
                    for m in range(EC):
                        ins = pe.transpose(ps[:, 4, m * P:(m + 1) * P], htmp[:, m * P:(m + 1) * P], ident)
                    ins.then_inc(sems["hidt_mm"], 1)
                    if not last:
                        turn(i + 2)
                    pe.wait_ge(sems["hidt_ready"], i + 1)
                    pe.wait_ge(sems["y_ready"], i + 1)
                    for u in range(2):
                        pe.wait_ge(sems["w_in"][4 + u], 16 * i + 16)
                    for m in range(EC):
                        for c in range(2):
                            for u in range(2):
                                ins = pe.matmul(ps[half(u), 6 + c, :], hid[:, m, half(u)], slab(4 + u, (EC, D))[:, m, c * 512:(c + 1) * 512],
                                                start=m == 0, stop=m == EC - 1)
                    ins.then_inc(sems["y_mm"], 1)
                with pe.Fori(0, pairs - 1) as i:
                    pair(i, False)
                pair(pairs - 1, True)
                for n in range(nt):
                    t = (0, NTM)[l] + n
                    pe.wait_ge(mix_ready, t + 1)
                    if n >= 2:
                        pe.wait_ge(x2_ready, t - 1)
                    for k in range(KC):
                        ins = pe.transpose(ps[:, 2 * (n % 2) + k // 4, (k % 4) * P:(k % 4 + 1) * P], yg[:, n, 0, k * P:(k + 1) * P], ident)
                    ins.then_inc(yt_mm, 1)

            pe.sem_inc(wo_mm, WON)
            pe.sem_inc(f1_mm, 32)
            pe.sem_inc(f2_mm, 7)
            pe.wait_ge(inputs_in, 16 * n_in)
            pe.wait_ge(setup_done, 2)
            block1(0)
            experts(0)
            block1(1)
            experts(1)

            def layer2(i):
                call = 4 + 2 * i

                def take(j, shape):
                    pe.wait_ge(slab_in[j % RING], slab2_count(i, j))
                    return slab(j, shape)

                hn = lambda k: hT[:, 0, k, :]
                norm(call, False)

                def normed(k):
                    pe.wait_ge(h_ready, KC * call + k + 1)
                    return hn(k)

                evs = P2N * i

                def bank_free(n):
                    if n >= 4:
                        pe.wait_ge(p2_ev, evs + n - 3)

                def chunks(n, j, count, width=512):
                    w = take(j, (KC, width))
                    for c in range(count):
                        bank_free(n + c)
                        mm_chunk(ps[:, (n + c) % 4, 0:NX], w, c * P, normed if n + c == 0 else hn).then_inc(p2_mm, 1)
                    return w

                chunks(0, 0, 4)
                w = chunks(4, 1, 3, COL_SB - 512)
                bank_free(7)
                for t in range(QT):
                    for k in range(KC):
                        pe.matmul(ps[:, 3, t * P:t * P + P], hT[:, 0, k, t * P:t * P + P],
                                  w[:, k, P:3 * P].rearrange("p (b d) -> p b d", b=2)[:, :, DH:P], start=k == 0, stop=k == KC - 1)
                for t in range(QT):
                    for k in range(KC):
                        ins = pe.matmul(ps[:, 3, NX + t * 24:NX + t * 24 + 24], hT[:, 0, k, t * P:t * P + P], w[:, k, 3 * P:3 * P + 24],
                                        start=k == 0, stop=k == KC - 1)
                ins.then_inc(p2_mm, 1)
                pe.wait_ge(p2_ev, evs + 7)
                for c in range(4):
                    pe.matmul(ps[:, 4 + c // 2, (c % 2) * NX:(c % 2) * NX + NX], cc("rot_b"), qp[:, c, :], start=True, stop=True).then_inc(r2_mm, 1)
                for c in range(2):
                    pe.matmul(ps[:, 6, c * NX:c * NX + NX], cc("rot_b"), kv[:, 1 + c, :], start=True, stop=True).then_inc(r2_mm, 1)
                chunks(8, 2, 4)
                pe.wait_ge(r2_ready, 10 * i + 6)
                for c, m in enumerate(("dup0", "dup1")):
                    pe.matmul(ps[:, 4, c * NX:c * NX + NX], cc(m), kv[:, 0, :], start=True, stop=True).then_inc(r2_mm, 1)
                for c in range(2):
                    pe.matmul(ps[:, 5, c * NX:c * NX + NX], cc("dup0"), kv[:, 1 + c, :], start=True, stop=True).then_inc(r2_mm, 1)
                chunks(12, 3, 4)
                def sb_values(t):
                    w = take(J_SBV, (KC, 512))
                    bank_free(16 + t)
                    for k in range(KC):
                        ins = pe.matmul(ps[:, t, :], hT[:, 0, k, t * P:t * P + P], w[:, k, :], start=k == 0, stop=k == KC - 1)
                    ins.then_inc(p2_mm, 1)

                pe.wait_ge(r2_ready, 10 * i + 10)
                for v in range(2):
                    w = take(J_CMP + v, (CB // 2, 256))
                    for j in range(CB // 2):
                        q = j % 4
                        ins = pe.matmul(ps[32 * q:32 * q + 32, 6, v * 256:v * 256 + 256], win[v][:, j, :], w[:, j, :], start=j < 4, stop=j >= CB // 2 - 4)
                    ins.then_inc(cmp_mm, 1)
                sb_values(0)
                pe.wait_ge(cmp_ready, 2 * i + 1)
                for q in range(4):
                    ins = pe.matmul(ps[:, 7, 16 * q:16 * q + 16], hrow[:, q * P:q * P + P], cc("fold"), start=True, stop=True)
                ins.then_inc(cmp_mm, 1)
                sb_values(1)
                pe.wait_ge(gel_ready, i + 1)
                w2 = lambda v, c: lp("w2", (2 * v + c) * 64, 64)
                for o in range(2):
                    for c in range(2):
                        pe.matmul(ps[o * DH:o * DH + DH, 4, 0:NCMP], w2(0, c), gcmp[:, c, :], start=c == 0, stop=c == 1)
                for hh in range(4):
                    for c in range(2):
                        ins = pe.matmul(ps[32 * hh:32 * hh + NCMP, 4, 64:128], gcmp[:, 2 + c, :], w2(1, c), start=c == 0, stop=c == 1)
                ins.then_inc(cmp_mm, 1)
                pe.wait_ge(cev_ready, i + 1)
                for t in range(QT):
                    for h in range(HEADS):
                        o, c0 = (h % 2) * DH, (t * HEADS // 2 + h // 2) * 16
                        ins = pe.matmul(ps[:, 5 + h % 2, c0:c0 + NCMP], qp[o:o + DH, h // 2, t * P:t * P + P], kcmp[o:o + DH, :], start=True, stop=True)
                ins.then_inc(cs_mm, 1)
                pe.wait_ge(p2_ev, evs + 18)
                for h in range(SBH):
                    pe.matmul(ps[:, h, 0:NX], sbk[:, h, 0:P], sbq[:, h, :], start=True, stop=True)
                    ins = pe.matmul(ps[:, h, NX:384], sbk[:, h, P:NX], sbq[:, h, P:NX], start=True, stop=True)
                ins.then_inc(sbz_mm, 1)
                pe.wait_ge(pcn_ready, 2 * i + 2)
                for t in range(QT):
                    for q in range(2):
                        ins = pe.transpose(ps[:, 4, (2 * t + q) * P:(2 * t + q + 1) * P],
                                           pcp[:, t, 4 * q:4 * q + 4, :].rearrange("p h c -> p (h c)"), ident)
                ins.then_inc(pct_mm, 1)
                w = take(J_MG, (KC, 512))
                for m in range(2):
                    mm_chunk(ps[:, 6 + m, 0:NX], w, m * P, hn).then_inc(p2_mm, 1)
                pe.wait_ge(sb_dve, 2 * i + 1)
                pe.wait_ge(pct_ready, i + 1)
                pe.wait_ge(p2_ev, evs + 20)
                for h in range(SBH):
                    b = 4 + h
                    pe.matmul(ps[:, b, 0:P], cc("negtri"), spl[:, h, 0:P], start=True, stop=True)
                    pe.matmul(ps[:, b, P:NX], cc("negtri"), spl[:, h, P:NX], start=True, stop=False)
                    pe.matmul(ps[:, b, P:NX], negones[:, :], spl[:, h, NX:384], start=False, stop=True)
                    ins = pe.matmul(ps[:, b, NX:384], cc("negtri"), spl[:, h, NX:384], start=True, stop=True)
                ins.then_inc(sbc_mm, 1)
                pe.wait_ge(sb_act, 5 * i + 4)
                for h in range(SBH):
                    pe.matmul(ps[:, h, 0:NX], sbv[:, 0, h * P:h * P + P], zs[:, h, 0:NX], start=True, stop=False)
                    ins = pe.matmul(ps[:, h, P:NX], sbv[:, 1, h * P:h * P + P], zs[:, h, NX:384], start=False, stop=True)
                ins.then_inc(sbo_mm, 1)
                pe.wait_ge(sb_act, 5 * i + 5)
                for s in range(2 * HEADS + 2):
                    if s < 2 * HEADS:
                        n, h, t = 40 + 16 * i + s, s // 2, s % 2
                        o, k = (h % 2) * DH, P * (t + 1)
                        pe.wait_ge(ex_ready, n - 1)
                        for b in range(2):
                            pe.matmul(ps[:, t, b * NX:b * NX + k], qr[o:o + DH, h // 2, t * P:t * P + P], kdup[o:o + DH, b, 0:k], start=True, stop=False)
                            ins = pe.matmul(ps[:, t, b * NX + t * P:b * NX + k], ident, cc("trineg"), start=False, stop=True)
                        ins.then_inc(sc_mm, 1)
                    if s < 2 * HEADS - 2:
                        w = take(J_MG + (s + 2) // 4, (KC, 512))
                        pe.wait_ge(p2_ev, evs + 18 + s + 1)
                        mm_chunk(ps[:, 6 + s % 2, 0:NX], w, (s + 2) % 4 * P, hn).then_inc(p2_mm, 1)
                    if 1 <= s <= 2 * HEADS:
                        t = (s - 1) % 2
                        transposes(40 + 16 * i + s - 1, t, prob[:, t, :], [(b * NX + j * P, b * NX + j * P + P) for b in range(2) for j in range(t + 1)], True)
                    if s >= 2:
                        n, h, t = 40 + 16 * i + s - 2, (s - 2) // 2, s % 2
                        o, c = (h % 2) * DH, h // 2
                        pe.wait_ge(pt_ready, n + 1)
                        if t == 0 and h % 2 == 0:
                            pe.wait_ge(o_ready, 8 + 4 * i + max(c - 1, 0))
                        ob = ps[o:o + DH, 4 + c % 2, t * P:t * P + P]
                        pe.matmul(ob, vblk[:, h % 4, :], pcT[:, 2 * t + h // 4, :], start=True, stop=False)
                        for b in range(2):
                            for j in range(t + 1):
                                ins = pe.matmul(ob, vsw[:, j, b * DH:b * DH + DH], probT[:, t, b * (t + 1) + j, :], start=False,
                                                stop=b == 1 and j == t)
                        ins.then_inc(pv_mm, 1)
                wn, ws = take(J_NSA, (4, D)), take(J_SB, (4, D))
                for m in range(KC):
                    if m >= 4:
                        pe.wait_ge(mix2_ready, KC * i + m - 3)
                    mm_chunk(ps[:, m % 4, NX:512], ws, m * P, lambda k: osb[:, k, :], 4)
                    if m == 0:
                        pe.wait_ge(o_ready, 8 + 4 * i + 4)
                    mm_chunk(ps[:, m % 4, 0:NX], wn, m * P, lambda k: onsa[:, k, :], 4).then_inc(y2_mm, 1)

                def out_norm(c, chunk):
                    for m in range(KC + 1):
                        if m < KC:
                            if m >= 4:
                                pe.wait_ge(nsq_ready, WON * i + KC * c + m - 3)
                            chunk(m).then_inc(wo_mm, 1)
                        if m >= 1:
                            pe.wait_ge(nsq_ready, WON * i + KC * c + m)
                            pe.matmul(ps[:, 7, 0:NX], ones[:, :], sqb[:, (m - 1) % 4, 0:NX], start=m == 1, stop=m == KC).then_inc(nss_mm, 1)


                def mixed(k):
                    pe.wait_ge(mix2_ready, KC * i + max(k, 4) + 1)
                    return mixT[:, k, :]

                wo = [take(J_OUT + j, (KC, 512)) for j in range(2)]
                out_norm(0, lambda m: mm_chunk(ps[:, m % 4, 0:NX], wo[m // 4], (m % 4) * P, mixed if m == 0 else lambda k: mixT[:, k, :]))
                norm(call + 1, False)

                def three(out, hi, lo, xhi, xlo, first, last):
                    pe.matmul(out, hi, xhi, start=first, stop=False)
                    pe.matmul(out, hi, xlo, start=False, stop=False)
                    return pe.matmul(out, lo, xhi, start=False, stop=last)

                def hidden(n, j):
                    hi, lo = (w.rearrange("p (k w) -> p k w", k=KC) for w in (w_hi[:, n % 2, :], w_lo[(J_FF + n) % RING][:, :]))

                    def part(c, k):
                        return three(ps[:, 4 + c, 0:NX], hi[:, k, c * P:c * P + P], lo[:, k, c * P:c * P + P], hn_hi[:, k, :], hn_lo[:, k, :],
                                     k == 0, k == KC - 1)

                    together = 3 if j == 0 else 0
                    for k in range(KC if together else 0):
                        pe.wait_ge(h_ready, KC * call + KC + k + 1)
                        for c in range(together):
                            ins = part(c, k)
                            if k == KC - 1:
                                ins.then_inc(f1_mm, 1)
                    for c in range(together, 4):
                        if j >= 1:
                            pe.wait_ge(f1_ev, 32 * i + 4 * j + c - 3)
                        for k in range(KC):
                            ins = part(c, k)
                        ins.then_inc(f1_mm, 1)

                def output(n, j, m):
                    hi, lo = (w.rearrange("p (k w) -> p k w", k=4) for w in (w_hi[:, n % 2, :], w_lo[(J_FF + n) % RING][:, :]))
                    for k in range(4):
                        x = (4 * j + k) % 8
                        ins = three(ps[:, m % 4, m // 4 * NX:m // 4 * NX + NX], hi[:, k, m * P:m * P + P], lo[:, k, m * P:m * P + P],
                                    ff_hi[:, x, :], ff_lo[:, x, :], j == 0 and k == 0 and m < 4, j == 7 and k == 3 and m >= 4)
                    return ins

                for n, (w, j) in enumerate(FF_ORDER):
                    pe.wait_ge(split_ready, 16 * i + n + 1)
                    if w == 1:
                        hidden(n, j)
                        continue
                    pe.wait_ge(ffs_ready, 32 * i + 4 * j + 4)
                    if j < 7:
                        for m in range(KC):
                            ins = output(n, j, m)
                        ins.then_inc(f2_mm, 1)
                    else:
                        out_norm(1, lambda m: output(n, j, FF_OUT[m]))

            pe.wait_ge(trig_done, 1)
            pe.wait_ge(x2_ready, 6)
            with pe.Fori(0, 2) as i:
                layer2(i)

        @block.vector
        def _(dve):
            chain = [0]

            def link(ins):
                chain[0] += 1
                ins.then_inc(dchain, 1)
                dve.wait_ge(dchain, chain[0])

            def step(ins, back):
                chain[0] += 1
                ins.then_inc(dchain, 1)
                if chain[0] > back:
                    dve.wait_ge(dchain, chain[0] - back)

            iota = cc("iota")

            def norm(call, full, gain=None, after=None):
                w = 512 if full else NX
                dve.wait_ge(std_ready, call + 1)
                dve.reciprocal(stdv[:, 0:w], stdv[:, 0:w]).then_inc(rstd_ready, 1)
                dve.wait_ge(rstd_ready, call + 1)
                for k in range(KC):
                    if gain is None:
                        dve.tensor_tensor(hsrc(full, k), src_of(full, k), g2(stdv[:, :]) if full else stdv[:, 0:NX], ALU.mult).then_inc(xn_ready, 1)
                    else:
                        ins = dve.scalar_tensor_tensor(hT[:, 0, k, :], xT[:, 0, k, :], gain(k), stdv[:, 0:NX], ALU.mult, ALU.mult)
                        if after is None:
                            ins.then_inc(h_ready, 1)
                        else:
                            after(ins, k)

            dve.memset(condv[:, :, :], 0.0)
            dve.memset(gpad, 0.0).then_inc(setup_done, 1)
            dve.memset(ones[:, :], 1.0)
            dve.memset(negones[:, :], -1.0)
            dve.memset(pcp[:, :, :, :], 0.0)
            dve.memset(vblk[:, :, :], 0.0)
            dve.wait_ge(inputs_in, 16 * n_in)
            dve.tensor_scalar(mneg[:, :], cc("m01"), 1.0, -NEG, ALU.subtract, ALU.mult).then_inc(setup_done, 1)
            ang, kf = E[:, NX:2 * NX], E[:, 2 * NX:3 * NX]
            link(dve.tensor_copy(ang, E[:, 0:NX].bitcast(I32)))
            link(dve.tensor_scalar(ang, ang, cc("invf"), None, ALU.mult))
            link(dve.tensor_scalar(kf, ang, 1.0 / TWO_PI, None, ALU.mult))
            link(dve.tensor_scalar(kf, kf, MAGIC, None, ALU.add))
            link(dve.tensor_scalar(kf, kf, MAGIC, None, ALU.subtract))
            for part in (C1, C2, C3):
                link(dve.scalar_tensor_tensor(ang, kf, -part, ang, ALU.mult, ALU.add))
            link(dve.tensor_scalar(cos2, ang, TWO_PI / 4, None, ALU.add))
            link(dve.tensor_scalar(kf, cos2, TWO_PI / 2, -TWO_PI, ALU.is_gt, ALU.mult))
            link(dve.tensor_tensor(cos2, cos2, kf, ALU.add))
            link(dve.tensor_scalar(cos2, cos2, 3.1415925, -3.1415925, ALU.min, ALU.max))
            dve.tensor_scalar(sin2, ang, 3.1415925, -3.1415925, ALU.min, ALU.max).then_inc(trig_ready, 1)

            def mod_bias(l, m0, m1, bank, at):
                n = m1 - m0
                bias = pc("mod_b", 48 * l + m0, n).unsqueeze(2).broadcast_to([P, n, 2])
                return dve.tensor_tensor(modv[:, l, m0:m1, :], ps[:, bank, at:at + 2 * n].rearrange("p (m c) -> p m c", c=2), bias, ALU.add)

            def mod_scale(dst, l, at, gain):
                g = pc(gain, KC * l, KC).unsqueeze(2).broadcast_to([P, KC, 2])
                return dve.scalar_tensor_tensor(dst[:, l, :, :], modv[:, l, at:at + KC, :], 1.0, g, ALU.add, ALU.mult)

            def modulation_first():
                dve.wait_ge(mod_fold, MOD0)
                link(mod_bias(0, 0, 4 * MOD0, 5, 0))
                mod_scale(scale1, 0, 8, "ln1_g").then_inc(mod_ready, 1)

            def modulation_rest():
                dve.wait_ge(mod_fold, 24)
                mod_bias(0, 4 * MOD0, 48, 7, 0)
                link(mod_bias(1, 0, 48, 7, 2 * (48 - 4 * MOD0)))
                mod_scale(scale2, 0, 32, "ln2_g")
                mod_scale(scale1, 1, 8, "ln1_g")
                mod_scale(scale2, 1, 32, "ln2_g").then_inc(mod_ready, 1)

            def qk_norm(g, c, w, gain):
                r = sqb[:, 2 + g % 2, :]
                dve.wait_ge(qstd_ready, g + 1)
                link(dve.reciprocal(r[:, 0:w], r[:, 0:w]))
                dve.scalar_tensor_tensor(qk[:, c, 0:w], qk[:, c, 0:w], gain, r[:, 0:w], ALU.mult, ALU.mult).then_inc(qn_ready, 1)
                dve.wait_ge(qn_ready, g + 1)
                dve.wait_ge(rot_mm, g + 1)
                dve.tensor_tensor(r[:, 0:NX], ps[:, 6, 0:NX], cc("sin"), ALU.mult)
                link(dve.tensor_tensor(qk[:, c, 0:NX], qk[:, c, 0:NX], cc("cos"), ALU.mult))
                dve.tensor_tensor(qk[:, c, 0:NX], qk[:, c, 0:NX], r[:, 0:NX], ALU.add).then_inc(rope_ready, 1)

            def conv_taps():
                for c0 in (0, 2):
                    for t in range(TAPS):
                        for c in (c0, c0 + 1):
                            acc, src = g2(cat[:, 4 + c, :]), gpad[:, c, :, t:t + NX]
                            w = pc("conv_w", c * TAPS + t, 1)
                            if t == 0:
                                ins = dve.tensor_scalar(acc, src, w, pc("conv_b", c, 1), ALU.mult, ALU.add)
                            else:
                                ins = dve.scalar_tensor_tensor(acc, src, w, acc, ALU.mult, ALU.add)
                            yield ins

            def unit_max(n, u, views, sc):
                dve.wait_ge(sc_mm, n + 1)
                w = views.shape[1]
                return dve.tensor_reduce(mx[:, u, 0:w], views, AX_X, ALU.max), w

            def block1(layer):
                full = layer == 0
                base, g0 = (0, 0) if full else (14, 5)
                w = 512 if full else NX
                norm(2 * layer, True)
                if full:
                    modulation_first()
                if not full:
                    dve.memset(upad, 0.0).then_inc(setup_done, 1)
                for c in range(QKC):
                    qk_norm(g0 + c, c, 512 if c == QC else w, pc(("qn_a", "qn_c")[layer] if c < QC else ("kn_a", "kn_c")[layer]))
                taps = iter(())
                if full:
                    for c in range(BC):
                        dve.wait_ge(proj_ev, base + 11 + c)
                        g = gpad[:, c, :, HALO:HALO + NX]
                        link(dve.tensor_tensor(g, g, g2(cat[:, 4 + c, :]), ALU.mult))
                    taps = conv_taps()
                units = attention_units(layer)
                for s in range(len(units) + 1):
                    if s < len(units):
                        n, h, kind = units[s]
                        bank, _, u = unit_place(layer, n)
                        view = ps[:, bank, :].rearrange("p (b k) -> p b k", b=2 if kind == 2 else 1)
                        ins, k = unit_max(n, u, view, SC_A)
                        link(ins)
                        if full:
                            dve.tensor_scalar(nb[:, u, 0:k], mx[:, u, 0:k], -SC_A, None, ALU.mult).then_inc(nb_ready, 1)
                        else:
                            link(dve.tensor_scalar(mx[:, u, 0:1], mx[:, u, 0:1], SC_A, pc("sink", h, 1), ALU.mult, ALU.max))
                            dve.tensor_scalar(nb[:, u, 0:1], mx[:, u, 0:1], -1.0, None, ALU.mult).then_inc(nb_ready, 1)
                    if s >= 1:
                        n, h, kind = units[s - 1]
                        _, p, u = unit_place(layer, n)
                        k = 2 if kind == 2 else 1
                        dve.wait_ge(ex_ready, n + 1)
                        if not full:
                            dve.wait_ge(sink_ready, n - 3 * HEADS + 1)
                            link(dve.tensor_tensor(sm[:, u, 0:1], sm[:, u, 0:1], es[:, u, :], ALU.add))
                        link(dve.reciprocal(sm[:, u, 0:k], sm[:, u, 0:k]))
                        for b in range(k):
                            part = p[:, b * (512 // k):(b + 1) * (512 // k)]
                            ins = dve.tensor_scalar(part, part, sm[:, u, b:b + 1], None, ALU.mult)
                        ins.then_inc(pn_ready, 1)
                    if not full and s % 4 == 3:
                        pool_windows(base, s // 4)
                    for _ in range(5):
                        ins = next(taps, None)
                        if ins is not None:
                            step(ins, 1)
                if full:
                    modulation_rest()
                    for ins in taps:
                        step(ins, 1)
                    dve.wait_ge(dchain, chain[0])
                    dve.sem_inc(conv_ready, 1)
                    dve.wait_ge(cmu_mm, 1)
                    for c in range(BC):
                        ins = dve.scalar_tensor_tensor(cat[:, 4 + c, :], ps[:, 6, :], -1.0 / 512, cat[:, 4 + c, :], ALU.mult, ALU.add)
                    ins.then_inc(cd_ready, 1)
                    dve.wait_ge(cstd_ready, 1)
                    link(dve.reciprocal(stdv[:, :], stdv[:, :]))
                    for c in range(BC):
                        dve.tensor_tensor(cat[:, 4 + c, :], cat[:, 4 + c, :], stdv[:, :], ALU.mult).then_inc(cn_ready, 1)
                else:
                    dve.wait_ge(pool_mm, 1)
                    for g in range(BC):
                        ins = dve.tensor_scalar(cat[:, 4 + g, 0:NX], ps[:, 6 + g // 2, (g % 2) * NX:(g % 2) * NX + NX], pc("pool_scale", g, 1), None, ALU.mult)
                    ins.then_inc(px_ready, 1)
                for m in range(KC):
                    dve.wait_ge(out_mm, KC * layer + m + 1)
                    for g in range(TG if full else 1):
                        ins = dve.scalar_tensor_tensor(xT[:, g, m, :], ps[:, m % 4, g * NX:g * NX + NX], modv[:, layer, 16 + m, g:g + 1], xT[:, g, m, :],
                                                       ALU.mult, ALU.add)
                    ins.then_inc(x_ready, 1)
                norm(2 * layer + 1, full)

            def pool_windows(base, c):
                dve.wait_ge(invcnt_ready, 16)
                dve.wait_ge(proj_ev, base + 7 + c)
                src, lo, hi, half = upad[:, c, :], 0, UP, 0
                for lev in range(c + 1):
                    dst = pwin[:, lev % 2, :]
                    d = max(half, 1)
                    left = half if lev else 1
                    right = half
                    a, b = lo + left, hi - right
                    link(dve.tensor_tensor(dst[:, a:b], src[:, a - left:b - left], src[:, a + right:b + right], ALU.add))
                    src, lo, hi = dst, a, b
                    half = 2 * half if lev else 1
                link(dve.tensor_tensor(pt_pool[:, c, :], src[:, PPAD:PPAD + NX], invcnt[:, c, :], ALU.mult))
                dve.tensor_tensor(pt_pool[:, c, :], pt_pool[:, c, :], upad[:, c, PPAD:PPAD + NX], ALU.subtract).then_inc(pool_ready, 1)

            def experts(l):
                nt = NTM if l == 0 else QT
                sems = moe[l]
                def low_part(q):
                    dve.wait_ge(hi_ready, (0, 2 * NTM)[l] + q + 1)
                    dve.tensor_tensor(tok_lo[q // 4][:, q // 2 % 2, tok_cols(q)], ps[:, tok_bank(q), :], tok_hi[:, q // 2, tok_cols(q)].bitcast(F32),
                                      ALU.subtract).then_inc(ht_ev, 1)

                for q in range(3):
                    low_part(q)
                dve.memset(lgp, -3e38)
                dve.wait_ge(lg_mm, l + 1)
                b = pc("rt_b", l * RL, RL).unsqueeze(1).broadcast_to([P, nt, RL])
                link(dve.tensor_tensor(lg[:, 0:nt, :], ps[:, 0, 0:nt * RL].rearrange("p (n r) -> p n r", n=nt), b, ALU.add))
                link(dve.tensor_tensor(lg[:, 0:nt, :], ps[:, 2, 0:nt * RL].rearrange("p (n r) -> p n r", n=nt), lg[:, 0:nt, :], ALU.add))
                link(dve.tensor_copy(lgp[:, 0:nt, 0:NG], lg[:, 0:nt, 0:NG]))

                def tiles(op):
                    for n in range(nt):
                        ins = op(n)
                    link(ins)

                experts_of = lambda n: lg[:, n, NG:RL].rearrange("p (g e) -> p g e", g=NG)
                tiles(lambda n: dve.max(gm8[:, n, :], lgp[:, n, :]))
                tiles(lambda n: dve.max_index(gi8[:, n, :], gm8[:, n, :], lgp[:, n, :]))
                link(dve.tensor_copy(rsc[:, 4, 0:nt], gi8[:, 0:nt, 0]))
                tiles(lambda n: dve.tensor_scalar(pen[:, n, :], iota[:, 0:NG], rsc[:, 4, n:n + 1], NEG, ALU.not_equal, ALU.mult))
                tiles(lambda n: dve.tensor_tensor(experts_of(n), experts_of(n), pen[:, n, :].unsqueeze(2).broadcast_to([P, NG, NE // NG]), ALU.add))
                tiles(lambda n: dve.max(em8[:, n, :], lg[:, n, NG:RL]))
                tiles(lambda n: dve.max_index(ei8[:, n, :], em8[:, n, :], lg[:, n, NG:RL]))
                dve.tensor_scalar(rsc[:, 0, 0:nt], gm8[:, 0:nt, 0], -1.0, None, ALU.mult)
                for k in range(2):
                    ins = dve.tensor_copy(rsc[:, 5 + k, 0:nt], ei8[:, 0:nt, k])
                link(ins)
                dve.tensor_tensor(rsc[:, 2, 0:nt], em8[:, 0:nt, 1], em8[:, 0:nt, 0], ALU.subtract).then_inc(gmax_ready, 1)
                for k in range(2):
                    tiles(lambda n: dve.tensor_scalar(M1[:, k, n * NE:(n + 1) * NE], iota[:, 0:NE], rsc[:, 5 + k, n:n + 1], None, ALU.is_equal))
                dve.tensor_tensor(M1[:, 2, 0:nt * NE], M1[:, 0, 0:nt * NE], M1[:, 1, 0:nt * NE], ALU.add).then_inc(m_ready, 1)
                for q in range(3, 2 * nt):
                    low_part(q)
                dve.wait_ge(gexp_ready, l + 1)
                link(dve.scalar_tensor_tensor(rsc[:, 8, 0:nt], rsc[:, 3, 0:nt], 1.0, rsc[:, 1, 0:nt], ALU.add, ALU.mult))
                link(dve.reciprocal(wts[:, 0:nt, 0], rsc[:, 8, 0:nt]))
                link(dve.tensor_tensor(wts[:, 0:nt, 1], wts[:, 0:nt, 0], rsc[:, 3, 0:nt], ALU.mult))
                dve.wait_ge(pos_mm, l + 1)
                cnt = ps[:, 1, nt * NE:(nt + 1) * NE]
                nq = nt * P // SLOTS
                over = E[:, 1024:1024 + NE * nq].rearrange("p (e q) -> p e q", e=NE)
                link(dve.scalar_tensor_tensor(over, iota[:, 0:nq].unsqueeze(1).broadcast_to([P, NE, nq]), float(SLOTS),
                                              cnt.unsqueeze(2).broadcast_to([P, NE, nq]), ALU.mult, ALU.is_lt))
                link(dve.tensor_reduce(cum[:, 0, :], over, AX_X, ALU.add))
                cur = cum[:, 0, :]
                for q in range(5):
                    nxt, s = cum[:, 1 + q % 2, :], 1 << q
                    dve.tensor_copy(nxt[:, 0:s], cur[:, 0:s])
                    link(dve.tensor_tensor(nxt[:, s:NE], cur[:, s:NE], cur[:, 0:NE - s], ALU.add))
                    cur = nxt
                link(dve.tensor_scalar(halves[:, 0:1], cur[:, NE - 1:NE], 0.5, None, ALU.mult))
                link(dve.tensor_scalar(below, iota[:, 0:MAXB // 2], halves[:, 0:1], None, ALU.is_lt))
                link(dve.tensor_reduce(halves[:, 0:1], below, AX_X, ALU.add))
                dve.memset(lane_step[:, 0:SLOTS], float(SLOTS))
                dve.memset(lane_step[:, SLOTS:PAIR], -float(SLOTS))
                link(dve.tensor_scalar(halves[:, 1:2], halves[:, 0:1], float(PAIR), -float(SLOTS), ALU.mult, ALU.add))
                link(dve.tensor_copy(iota2[:, 0:SLOTS], iota[:, 0:SLOTS]))
                link(dve.tensor_scalar(iota2[:, SLOTS:PAIR], iota[:, 0:SLOTS], halves[:, 1:2], None, ALU.add))
                link(dve.tensor_tensor(cum[:, 3, :], cur, cum[:, 0, :], ALU.subtract))
                tiles(lambda n: dve.scalar_tensor_tensor(lg[:, n, 0:NE], cum[:, 3, :], float(SLOTS), ps[:, 1, n * NE:(n + 1) * NE], ALU.mult, ALU.add))
                mk = [M1[:, k, 0:nt * NE].rearrange("p (n e) -> p n e", n=nt) for k in range(2)]
                for k in range(2):
                    ins = dve.tensor_tensor(mk[k], mk[k], lg[:, 0:nt, 0:NE], ALU.mult)
                link(ins)
                for k in range(2):
                    ins = dve.tensor_reduce(slotf[:, 0:nt, k], mk[k], AX_X, ALU.add)
                link(ins)
                link(dve.tensor_copy(sloti[:, 0:2 * nt].rearrange("p (n k) -> p n k", k=2), slotf[:, 0:nt, :]))
                def build(count):
                    for n in range(nt):
                        dve.tensor_scalar(sel[:, n, :], iota2, slotf[:, n, 0:1], None, ALU.is_equal).then_inc(sems["moe_chain"], 1)
                    dve.wait_ge(sems["moe_chain"], count + nt)
                    for n in range(nt):
                        dve.scalar_tensor_tensor(sel[:, n, :], iota2, slotf[:, n, 1:2], sel[:, n, :].bitcast(F32), ALU.is_equal, ALU.add).then_inc(
                            sems["moe_chain"], 1)
                    dve.wait_ge(sems["moe_chain"], count + 2 * nt)
                    dve.tensor_tensor(iota2, iota2, lane_step, ALU.add).then_inc(sems["sel_ready"], 1)

                build(0)
                ends = cur[0:1, :].unsqueeze(1).broadcast_to([1, MAXB, NE])
                blocks = iota[0:1, 0:MAXB].unsqueeze(2).broadcast_to([1, MAXB, NE])
                link(dve.tensor_tensor(blk_cmp, ends, blocks, ALU.is_le))
                link(dve.tensor_reduce(blkf[0:1, 0:MAXB], blk_cmp, AX_X, ALU.add))
                link(dve.tensor_scalar(blkf[0:1, 0:MAXB], blkf[0:1, 0:MAXB], float(NE - 1), None, ALU.min))
                link(dve.memset(blkf[0:1, MAXB:MAXB + 1], float(NE - 1)))
                dve.tensor_scalar(fresh[:, 0:1], blkf[0:1, 0:1], 0.0, None, ALU.not_equal)
                link(dve.tensor_tensor(fresh[:, 1:MAXB + 1], blkf[0:1, 1:MAXB + 1], blkf[0:1, 0:MAXB], ALU.not_equal))
                link(dve.tensor_copy(blki[0:1, NEW:NEW + MAXB + 1], fresh))
                link(dve.tensor_copy(blki[0:1, MAXB:MAXB + 1], halves[0:1, 0:1]))
                link(dve.tensor_scalar(blkf[0:1, MAXB + 1:MAXB + 2], halves[0:1, 0:1], -1.0, float(MAXB // 2 + 1), ALU.mult, ALU.add))
                link(dve.tensor_copy(blki[0:1, MAXB + 1:MAXB + 2], blkf[0:1, MAXB + 1:MAXB + 2]))
                dve.tensor_copy(blki[0:1, 0:MAXB], blkf[0:1, 0:MAXB]).then_inc(plan_ready, 1)
                dve.wait_ge(plan_ready, l + 1)
                pairs = dve.value_load(blki[0:1, MAXB:MAXB + 1], min_val=1, max_val=MAXB // 2)

                def pair(i, last):
                    if not last:
                        dve.wait_ge(sems["sel_ready"], i + 1)
                        dve.wait_ge(sems["xtok_mm"], i + 1)
                        build(2 * nt + 2 * nt * i)
                    dve.wait_ge(sems["sg_ready"], i + 1)
                    dve.wait_ge(sems["gu_mm"], 2 * i + 4)
                    dve.tensor_tensor(htmp, silu_g, ps[:, 3, :], ALU.mult).then_inc(sems["hid_ready"], 1)
                    dve.wait_ge(sems["hidt_mm"], i + 1)
                    dve.tensor_copy(hid, ps[:, 4, :].rearrange("p (m s) -> p m s", m=EC)).then_inc(sems["hidt_ready"], 1)

                with dve.Fori(0, pairs - 1) as i:
                    pair(i, False)
                pair(pairs - 1, True)
                dve.sem_inc(sel_over, 1)
                for n in range(nt + 1):
                    if n < nt:
                        dve.wait_ge(yg_in[l][n], 32)
                        link(dve.tensor_scalar(yg[:, n, 0, :], yg[:, n, 0, :], wts[:, n, 0:1], None, ALU.mult))
                        dve.scalar_tensor_tensor(yg[:, n, 0, :], yg[:, n, 1, :], wts[:, n, 1:2], yg[:, n, 0, :], ALU.mult, ALU.add).then_inc(mix_ready, 1)
                    if n >= 1:
                        m, t = n - 1, (0, NTM)[l] + n - 1
                        dve.wait_ge(yt_mm, t + 1)
                        for k in range(KC):
                            x = xT[:, m // 2, k, (m % 2) * P:(m % 2) * P + P]
                            ins = dve.scalar_tensor_tensor(x, ps[:, 2 * (m % 2) + k // 4, (k % 4) * P:(k % 4 + 1) * P], modv[:, l, 40 + k, m // 2:m // 2 + 1], x,
                                                           ALU.mult, ALU.add)
                        ins.then_inc(x2_ready, 1)

            block1(0)
            experts(0)
            block1(1)
            experts(1)
            dve.wait_ge(x2_ready, 6)
            dve.sem_inc(xo_ready, KC)

            def layer2(i):
                call = 4 + 2 * i
                chain2 = [0]

                def link2(ins):
                    chain2[0] += 1
                    ins.then_inc(d2chain, 1)
                    dve.wait_ge(d2chain, LINKS2 * i + chain2[0])

                dve.wait_ge(lpars_in, 16)
                link2(dve.tensor_copy(lpar[:, :], lpars[:, bass.ds(i * n_lp, n_lp)]))
                norm(call, False, lambda k: lp("norm_g", k, 1))
                for c in range(6):
                    dve.wait_ge(r2_mm, 10 * i + c // 2 * 2 + 2)
                    t = sqb[:, 3, (c % 2) * NX:(c % 2) * NX + NX]
                    src, dst = (qp[:, c, :], qr[:, c, :]) if c < 4 else (kv[:, c - 3, :], kv[:, c - 3, :])
                    dve.tensor_tensor(t, ps[:, 4 + c // 2, (c % 2) * NX:(c % 2) * NX + NX], sin2, ALU.mult)
                    link2(dve.tensor_tensor(dst, src, cos2, ALU.mult))
                    dve.tensor_tensor(dst, dst, t, ALU.add).then_inc(r2_ready, 1)
                link2(dve.memset(win[0], 0.0))
                link2(dve.memset(win[1], 0.0))
                for v in range(2):
                    dve.wait_ge(r2_mm, 10 * i + 8)
                    dve.tensor_copy(win[v][:, :, NCMP], lp("pe", v * (CB // 2), CB // 2))
                    for o in range(2):
                        rows_ = ps[o * DH:o * DH + DH, 4, v * NX:v * NX + NX].rearrange("p (c j o) -> p j c o", j=8, o=2)
                        for jh in range(2):
                            ins = dve.tensor_copy(win[v][o * DH:o * DH + DH, 8 * jh:8 * jh + 8, 0:NCMP], rows_[:, :, jh:jh + NCMP, o])
                    ins.then_inc(r2_ready, 1)
                for c in range(2):
                    dve.wait_ge(r2_mm, 10 * i + 10)
                    dve.tensor_copy(kdup[:, c, :], ps[:, 5, c * NX:c * NX + NX]).then_inc(r2_ready, 1)
                dve.wait_ge(cmp_mm, 4 * i + 4)
                dve.tensor_copy(kcmp[:, :], ps[:, 4, 0:NCMP])
                for hh in range(4):
                    ins = dve.tensor_copy(vblk[32 * hh:32 * hh + NCMP, hh, :], ps[32 * hh:32 * hh + NCMP, 4, 64:128])
                ins.then_inc(cev_ready, 1)
                dve.wait_ge(cs_mm, i + 1)
                maskc = cc("maskc").rearrange("p (q c) -> p q c", q=QT)
                visc = cc("visc").rearrange("p (q c) -> p q c", q=QT)
                rows_c = scmp.rearrange("p q h c -> p (q h) c")
                for q in range(QT):
                    for o in range(2):
                        link2(dve.tensor_tensor(scmp[:, q, o:HEADS:2, :],
                                                ps[:, 5 + o, q * 64:q * 64 + 64].rearrange("p (h c) -> p h c", h=HEADS // 2)[:, :, 0:NCMP],
                                                maskc[:, q, :].unsqueeze(1).broadcast_to([P, HEADS // 2, NCMP]), ALU.add))
                link2(dve.tensor_reduce(cst[:, 0, :], rows_c, AX_X, ALU.max))
                dve.tensor_tensor(rows_c, rows_c, cst[:, 0, :].unsqueeze(2).broadcast_to([P, QT * HEADS, NCMP]), ALU.subtract).then_inc(pcn_ready, 1)
                dve.wait_ge(pce_ready, i + 1)
                link2(dve.tensor_reduce(cst[:, 1, :], rows_c, AX_X, ALU.add))
                link2(dve.reciprocal(cst[:, 1, :], cst[:, 1, :]))
                link2(dve.tensor_tensor(cst[:, 2, :].rearrange("p (q h) -> p q h", q=QT), cst[:, 1, :].rearrange("p (q h) -> p q h", q=QT),
                                        gates[:, :, :].rearrange("p q (h g) -> p q h g", g=3)[:, :, :, 0], ALU.mult))
                link2(dve.tensor_tensor(rows_c, rows_c, cst[:, 2, :].unsqueeze(2).broadcast_to([P, QT * HEADS, NCMP]), ALU.mult))
                for q in range(QT):
                    ins = dve.tensor_tensor(pcp[:, q, :, 0:NCMP], scmp[:, q, :, :], visc[:, q, :].unsqueeze(1).broadcast_to([P, HEADS, NCMP]), ALU.mult)
                ins.then_inc(pcn_ready, 1)
                dve.wait_ge(sbz_mm, i + 1)
                dve.wait_ge(sb_act, 5 * i + 1)
                masks = mneg[:, :].unsqueeze(1).broadcast_to([P, SBH, P])
                keep = cc("m01").unsqueeze(1).broadcast_to([P, SBH, P])
                dve.tensor_tensor(zs[:, :, 0:P], ps[:, 0:SBH, 0:P], masks, ALU.add)
                dve.tensor_copy(zs[:, :, P:NX], ps[:, 0:SBH, P:NX])
                dve.tensor_tensor(zs[:, :, NX:384], ps[:, 0:SBH, NX:384], masks, ALU.add)
                dve.wait_ge(sb_act, 5 * i + 3)
                link2(dve.scalar_tensor_tensor(spl, ps[:, 0:SBH, 0:384], 0.0, spl, ALU.max, ALU.add))
                dve.tensor_tensor(spl[:, :, 0:P], spl[:, :, 0:P], keep, ALU.mult)
                dve.tensor_tensor(spl[:, :, NX:384], spl[:, :, NX:384], keep, ALU.mult).then_inc(sb_dve, 1)
                dve.wait_ge(sbc_mm, i + 1)
                dve.tensor_tensor(zs, zs, ps[:, 4:8, 0:384], ALU.add).then_inc(sb_dve, 1)
                for s in range(2 * HEADS + 1):
                    if s < 2 * HEADS:
                        n, u, k = 40 + 16 * i + s, s % 2, P * (s % 2 + 1)
                        ins, _ = unit_max(n, u, ps[:, u, :].rearrange("p (b k) -> p b k", b=2)[:, :, 0:k], SC_A)
                        link2(ins)
                        dve.tensor_scalar(nb[:, u, :], mx[:, u, :], -SC_A, None, ALU.mult).then_inc(nb_ready, 1)
                    if s >= 1:
                        n, h, u = 40 + 16 * i + s - 1, (s - 1) // 2, (s - 1) % 2
                        k = P * (u + 1)
                        dve.wait_ge(ex_ready, n + 1)
                        link2(dve.reciprocal(sm[:, u, :], sm[:, u, :]))
                        link2(dve.tensor_tensor(sm[:, u, :], sm[:, u, :], gates[:, u, 3 * h + 1:3 * h + 3], ALU.mult))
                        for b in range(2):
                            p = prob[:, u, b * NX:b * NX + k]
                            ins = dve.tensor_scalar(p, p, sm[:, u, b:b + 1], None, ALU.mult)
                        ins.then_inc(pn_ready, 1)
                for m in range(KC):
                    dve.wait_ge(y2_mm, KC * i + m + 1)
                    dve.wait_ge(mgs_ready, KC // 2 * i + m // 2 + 1)
                    dve.tensor_tensor(mg[:, m, :], mg[:, m, :], ps[:, m % 4, 0:NX], ALU.mult)
                    link2(dve.tensor_tensor(mg[:, KC + m, :], mg[:, KC + m, :], ps[:, m % 4, NX:512], ALU.mult))
                    dve.tensor_tensor(mixT[:, m, :], mg[:, m, :], mg[:, KC + m, :], ALU.add).then_inc(mix2_ready, 1)

                def out_norm(c):
                    dve.wait_ge(nstd_ready, 2 * i + c + 1)
                    link2(dve.reciprocal(stdv[:, 0:NX], stdv[:, 0:NX]))
                    for k in range(KC):
                        link2(dve.scalar_tensor_tensor(yres[:, k, :], yres[:, k, :], lp("norm_g", (2 * c + 1) * KC + k, 1), stdv[:, 0:NX], ALU.mult, ALU.mult))
                        dve.tensor_tensor(xT[:, 0, k, :], xT[:, 0, k, :], yres[:, k, :], ALU.add).then_inc(xo_ready, 1)

                def parts(hi, lo, x):
                    link2(dve.tensor_copy(hi, x))
                    return dve.tensor_tensor(lo, x, hi.bitcast(F32), ALU.subtract)

                def split_slab(n):
                    j = J_FF + n
                    dve.wait_ge(slab_in[j % RING], slab2_count(i, j))
                    if n >= 2:
                        s, per, v = ff_used(*FF_ORDER[n - 2])[0]
                        dve.wait_ge(s, i * per + v)
                    parts(w_hi[:, n % 2, :], w_lo[j % RING][:, :], ring[:, j % RING, :]).then_inc(split_ready, 1)

                def split_h(ins, k):
                    link2(ins)
                    parts(hn_hi[:, k, :], hn_lo[:, k, :], hT[:, 0, k, :]).then_inc(h_ready, 1)

                for n in range(2):
                    split_slab(n)
                out_norm(0)
                norm(call + 1, False, lambda k: lp("norm_g", 2 * KC + k, 1), split_h)
                for n, (w, j) in enumerate(FF_ORDER):
                    if w == 1:
                        if j >= 2:
                            dve.wait_ge(f2_mm, 7 * i + 7 + j - 1)
                        for m in range(4 * j, 4 * j + 4):
                            dve.wait_ge(ffh_ready, 32 * i + m + 1)
                            parts(ff_hi[:, m % 8, :], ff_lo[:, m % 8, :], sqb[:, m % 4, 0:NX]).then_inc(ffs_ready, 1)
                    if n + 2 < len(FF_ORDER):
                        split_slab(n + 2)
                out_norm(1)
                assert chain2[0] == LINKS2, chain2[0]

            with dve.Fori(0, 2) as i:
                layer2(i)

        @block.gpsimd
        def _(pool):
            pool.wait_ge(plan_ready, 1)
            pool.memset(zrows, 0.0).then_inc(zrows_ready, 1)
            pairs = pool.value_load(blki[0:1, MAXB:MAXB + 1], min_val=1, max_val=MAXB // 2)
            pool.wait_ge(zrows_ready, 1)
            with pool.Fori(pairs, MAXB // 2 + 1) as i:
                pool.dma_start(y_rows[bass.ds(i * PAIR, PAIR), :], zrows).then_inc(tail_stored, 16)
            tail = pool.value_load(blki[0:1, MAXB + 1:MAXB + 2], min_val=1, max_val=MAXB // 2)
            pool.wait_ge(tail_stored, 16 * tail)
            pool.sem_inc(zrows_ready, 1)
            for l in range(2):
                pool.wait_ge(stored_all, l + 1)
                pool.wait_ge(sel_over, l + 1)
                for n in range(NTM if l == 0 else QT):
                    for k in range(2):
                        pool.indirect_dma_start(out=yg[:, n, k, :], out_offset=None, in_=y_rows,
                                                in_offset=bass.IndirectOffsetOnAxis(ap=sloti[:, 2 * n + k:2 * n + k + 1], axis=0)).then_inc(yg_in[l][n], 16)


def constants():
    import numpy as np

    p, f = np.arange(P)[:, None], np.arange(P)[None, :]
    t = {}
    t["ident"] = p == f
    t["headones"] = p // DH == f // DH
    half = DH // 2
    rot = np.zeros((P, P), np.float32)
    rot_b = np.zeros((P, P), np.float32)
    for m in range(P):
        d = m % DH
        if d < half:
            rot[m + half, m] = -1
        else:
            rot[m - half, m] = 1
        if d < 8:
            rot_b[m + 8, m] = -1
        elif d < 16:
            rot_b[m - 8, m] = 1
    t["rot_a"], t["rot_b"] = rot, rot_b
    t["swap"] = (p + DH) % P == f
    t["dup0"] = p == f % DH
    t["dup1"] = p == DH + f % DH
    t["tri_strict"] = p < f
    t["negtri"] = -(p >= f).astype(np.float32)
    t["trineg"] = np.where(f > p, NEG, 0.0)
    t["band1"] = np.where(f < p, NEG, 0.0)
    t["m01"] = p < f
    t["iota"] = np.broadcast_to(f, (P, P))
    tok = np.arange(NX)
    inv = np.float32(10000.0) ** (-np.arange(DH // 4, dtype=np.float32) / np.float32(DH // 4))
    ang = np.concatenate([(tok // 64).astype(np.float32)[:, None] * inv, (tok % 64).astype(np.float32)[:, None] * inv], axis=1)
    t["cos"] = np.cos(ang).T[np.arange(P) % half]
    t["sin"] = np.sin(ang).T[np.arange(P) % half]
    c, q = np.arange(NCMP)[None, None, :], np.arange(QT)[None, :, None]
    vis = CS * c + CB - 1 <= q * P + np.arange(P)[:, None, None]
    t["maskc"] = np.where(vis, 0.0, NEG).reshape(P, -1)
    t["visc"] = vis.reshape(P, -1)
    d = np.arange(P) % DH
    inv2 = np.power(np.float32(500000.0), np.arange(8, dtype=np.float32) * np.float32(-2.0 / 16))
    t["invf"] = np.where(d < 16, inv2[d % 8], 0.0)[:, None]
    t["eps"] = np.full((P, 1), EPS)
    t["fold"] = p % 32 == np.arange(16)[None, :]
    return np.concatenate([np.asarray(t[n], np.float32).reshape(P, w) for n, w in CONSTS], axis=1)


def window_lengths():
    import numpy as np

    t = np.arange(NX)
    inv = [1.0 / (np.clip(t - w // 2 + w, 0, NX) - np.clip(t - w // 2, 0, NX)).astype(np.float32) for w in POOLS]
    return np.ascontiguousarray(np.broadcast_to(np.stack(inv)[None], (P, BC, NX)), np.float32)


def kernel(**inputs):
    import numpy as np
    import concourse.bacc as bacc
    from concourse.bass_utils import run_bass_kernel_spmd

    a = {k: np.asarray(v) for k, v in inputs.items()}

    def cols(v):
        v = v.reshape(-1, v.shape[-1] // P, P)
        return v.transpose(2, 0, 1).reshape(P, -1)

    def fill(v):
        return np.broadcast_to(v.reshape(1, -1), (P, v.size))

    cond = np.stack([a["c"][0], a["c_ctx"]])
    head = lambda v: np.tile(v[0], 2).reshape(P, 1)
    rt_w = np.concatenate([a["rt_grp_w"], a["rt_exp_w"]], axis=2)
    small = {
        "cond": cond.reshape(2, KC, P).transpose(2, 1, 0).reshape(P, -1),
        "mod_b": cols(a["mod_b"]), "ln1_g": cols(a["ln1_g"]), "ln2_g": cols(a["ln2_g"]),
        "qn_a": head(a["q_norm_a"]), "kn_a": head(a["k_norm_a"]), "qn_c": head(a["q_norm_c"]), "kn_c": head(a["k_norm_c"]),
        "conv_w": a["conv_w"][0].reshape(TAPS, BC, P).transpose(2, 1, 0).reshape(P, -1),
        "conv_b": cols(a["conv_b"]), "cln_g": cols(a["conv_ln_g"]), "cln_b": cols(a["conv_ln_b"]),
        "sink": fill(a["sink_c"]), "pool_scale": cols(a["pool_scale"]),
        "rt_w": rt_w.reshape(2, KC, P, RL).transpose(2, 0, 1, 3).reshape(P, -1),
        "rt_b": fill(np.concatenate([a["rt_grp_b"], a["rt_exp_b"]], axis=1)),
    }
    params = np.concatenate([small[n].reshape(P, w) for n, w in PARAMS], axis=1)
    layer = {
        "norm_g": a["norm_g_2"].reshape(2, 4 * KC, P).transpose(0, 2, 1),
        "pe": a["cmp_pe_2"].reshape(2, 2, CB // 2, P).transpose(0, 3, 1, 2).reshape(2, P, -1),
        "w2": a["cmp_w2_2"].reshape(2, 2, 2, P, DH).transpose(0, 3, 1, 2, 4).reshape(2, P, -1),
    }
    lparams = np.concatenate([layer[n] for n, _ in LPARAMS], axis=2)
    x_in = np.stack([a["x"][0], a["ctx"][0]]).reshape(TG, NX, KC, P).transpose(3, 0, 2, 1)
    arrays = {
        "x_in": x_in, "params": params, "consts": constants(), "invcnt": window_lengths(), "lparams": lparams,
        "pos": np.broadcast_to(a["positions_2"].astype(np.int32), (P, NX)), "mod_w": a["mod_w"],
        "w_in_ab": a["w_in_ab"][0], "w_out_ab": a["w_out_ab"][0], "w_in_cd": a["w_in_cd"][0], "w_out_cd": a["w_out_cd"][0],
        "pool_w": a["pool_w"][0], "ex_gate": a["ex_gate"], "ex_up": a["ex_up"], "ex_down": a["ex_down"], "w_in_2": a["w_in_2"],
        "cmp_w1": a["cmp_w1_2"], "w_nsa_o": a["w_nsa_o_2"], "w_sb_o": a["w_sb_o_2"], "w_out_2": a["w_out_2"],
        "w_ff1": a["w_ff1_2"], "w_ff2": a["w_ff2_2"],
    }
    arrays = {f"in_{n}": np.ascontiguousarray(v) for n, v in arrays.items()}
    nc = bacc.Bacc("TRN2", target_bir_lowering=False, num_devices=1, dynamic_dma_scratch_size=8192)
    args = [nc.dram_tensor(n, v.shape, mybir.dt.from_np(v.dtype), kind="ExternalInput").ap() for n, v in arrays.items()]
    out = nc.dram_tensor("out_T", (P, KC, NX), F32, kind="ExternalOutput").ap()
    y_rows = nc.dram_tensor("y_rows", (MAXB * SLOTS + PAIR, D), F32, kind="Internal").ap()
    hybrid_program(nc, *args, out, y_rows)
    got = run_bass_kernel_spmd(nc, [arrays], core_ids=[0]).results[0]["out_T"]
    return np.asarray(got).transpose(2, 1, 0).reshape(1, NX, D)
```
